# Optimizing a Trainium2 kernel written in Bass

```python
import math
import jax
import jax.numpy as jnp
from jax import lax
import numpy as np
import jax, jax.numpy as jnp

D_MODEL = 1024
BATCH = 1
SEQ = 512
DEPTH = 2

GRID_W = 64
CTX_LEN = 256
RMS_EPS = 1e-6
N_MOD = 6
SHORT_W = 3

HY_WIDTH = 512
HY_EMB = 33
HY_FF = 64
HY_FAST = 0.3
HY_SLOW = 1.5
HY_TARGET = 1e-2
HY_SHIFT = 0.05

ML_HEADS = 4
ML_HEAD_DIM = 128
ML_WIDTH = ML_HEADS * ML_HEAD_DIM
ML_CHUNK = 64
IN0_COLS = 3 * HY_WIDTH + 4 * ML_WIDTH + 4 * ML_HEADS

MLA_HEADS = 8
MLA_NOPE = 128
MLA_ROPE = 64
MLA_V = 128
MLA_Q_RANK = 384
MLA_KV_RANK = 256
MLA_SCALE = (MLA_NOPE + MLA_ROPE) ** -0.5
ROPE_AXIS = MLA_ROPE // 2
ROPE_BASE = 10000.0
Q_BLOCK = 128

D_FF = 2816


F32 = jnp.float32

def rmsnorm(x, g):
    xf = x.astype(F32)
    y = xf * lax.rsqrt(jnp.mean(xf * xf, axis=-1, keepdims=True) + RMS_EPS)
    return (y * g.astype(F32)).astype(x.dtype)

def ada_mod(cv, w, b):
    m = jax.nn.silu(cv) @ w + b
    return jnp.split(m, N_MOD, axis=-1)

def dwconv(x, w):
    k = w.shape[0]
    return lax.conv_general_dilated(x, w[:, None, :].astype(x.dtype), (1,), [(k // 2, k // 2)],
                                    dimension_numbers=('NWC', 'WIO', 'NWC'),
                                    feature_group_count=x.shape[-1])

def hyena_filters(L, fw1, fb1, fw2, fb2, fw3, freq):
    pos = jnp.arange(L, dtype=F32)
    t = (pos / (L - 1))[:, None]
    bands = (HY_EMB - 1) // 2
    f = jnp.linspace(1e-4, bands - 1, bands, dtype=F32)
    ang = (2.0 * math.pi / L) * pos[:, None] * f[None, :]
    z = jnp.concatenate([t, jnp.cos(ang), -jnp.sin(ang)], axis=-1)
    fq = freq.astype(F32)
    h = jnp.sin(fq * (z @ fw1.astype(F32) + fb1.astype(F32)))
    h = jnp.sin(fq * (h @ fw2.astype(F32) + fb2.astype(F32)))
    h = h @ fw3.astype(F32)
    deltas = jnp.linspace(math.log(HY_TARGET) / HY_FAST, math.log(HY_TARGET) / HY_SLOW, HY_WIDTH, dtype=F32)
    decay = jnp.exp(-t * jnp.abs(jnp.tile(deltas, 2))[None, :])
    return h * (decay + HY_SHIFT)

def hyena_mix(u, conv_w, conv_b, filt, bias):
    u = dwconv(u, conv_w) + conv_b
    x0, x1, v = jnp.split(u, 3, axis=-1)
    L = u.shape[1]
    g = (v * x1).astype(F32)
    h = hyena_filters(L, *filt)
    hf, hb = h[:, :HY_WIDTH], h[:, HY_WIDTH:]
    k2 = jnp.concatenate([hf, jnp.zeros((1, HY_WIDTH), F32), hb[:0:-1]], axis=0)
    n = 2 * L
    y = jnp.fft.irfft(jnp.fft.rfft(g, n=n, axis=1) * jnp.fft.rfft(k2, axis=0)[None], n=n, axis=1)[:, :L]
    y = y + g * bias.astype(F32)
    return y.astype(u.dtype) * x0

def mlstm_chunkwise(q, k, v, ig, lf, state):
    B, H, T, d = q.shape
    nc = T // ML_CHUNK

    def chunks(a):
        return jnp.moveaxis(a.reshape((B, H, nc, ML_CHUNK) + a.shape[3:]), 2, 0)

    causal = jnp.tril(jnp.ones((ML_CHUNK, ML_CHUNK), dtype=bool))

    def step(carry, inp):
        C, nv, m = carry
        qc, kc, vc, ic, fc = inp
        b = jnp.cumsum(fc, axis=-1)
        dlog = jnp.where(causal, b[..., :, None] - b[..., None, :] + ic[..., None, :], -jnp.inf)
        inter = b + m[..., None]
        m_t = jnp.maximum(inter, jnp.max(dlog, axis=-1))
        w_in = jnp.exp(dlog - m_t[..., None])
        w_st = jnp.exp(inter - m_t)
        s = jnp.einsum('bhtd,bhsd->bhts', qc, kc) * w_in
        num = jnp.einsum('bhts,bhsd->bhtd', s, vc) + w_st[..., None] * jnp.einsum('bhve,bhte->bhtv', C, qc)
        den = jnp.sum(s, axis=-1) + w_st * jnp.einsum('bhe,bhte->bht', nv, qc)
        h = num / jnp.maximum(jnp.abs(den), jnp.exp(-m_t))[..., None]
        bl = b[..., -1]
        gs = bl[..., None] - b + ic
        m_new = jnp.maximum(bl + m, jnp.max(gs, axis=-1))
        a = jnp.exp(bl + m - m_new)
        ws = jnp.exp(gs - m_new[..., None])
        C_new = a[..., None, None] * C + jnp.einsum('bhs,bhsv,bhse->bhve', ws, vc, kc)
        n_new = a[..., None] * nv + jnp.einsum('bhs,bhse->bhe', ws, kc)
        return (C_new, n_new, m_new), h

    state, hs = lax.scan(step, state, (chunks(q), chunks(k), chunks(v), chunks(ig), chunks(lf)))
    return jnp.moveaxis(hs, 0, 2).reshape(B, H, T, d), state

def mlstm_direction(q, k, v, ig, f_pre, state, reverse):
    lf = jax.nn.log_sigmoid(f_pre)
    if reverse:
        q, k, v = jnp.flip(q, 2), jnp.flip(k, 2), jnp.flip(v, 2)
        ig, lf = jnp.flip(ig, -1), jnp.flip(lf, -1)
    h, state = mlstm_chunkwise(q, k, v, ig, lf, state)
    if reverse:
        h = jnp.flip(h, 2)
    return h, state

def mlstm_inputs(u, conv_w, gate_b):
    B, L, _ = u.shape
    off = 3 * HY_WIDTH
    qk = jax.nn.silu(dwconv(u[..., off:off + 2 * ML_WIDTH], conv_w))
    q, k = jnp.split(qk, 2, axis=-1)
    v = u[..., off + 2 * ML_WIDTH:off + 3 * ML_WIDTH]
    og = u[..., off + 3 * ML_WIDTH:off + 4 * ML_WIDTH]
    gates = u[..., off + 4 * ML_WIDTH:].astype(F32) + gate_b.astype(F32)
    gates = jnp.transpose(gates.reshape(B, L, 4, ML_HEADS), (2, 0, 3, 1))

    def heads(a):
        return jnp.transpose(a.reshape(B, L, ML_HEADS, ML_HEAD_DIM), (0, 2, 1, 3)).astype(F32)

    return heads(q) * ML_HEAD_DIM ** -0.5, heads(k), heads(v), og, gates

def mlstm_out(h, og, norm_g):
    B, H, L, d = h.shape
    t = jnp.swapaxes(h, 1, 2)
    t = t * lax.rsqrt(jnp.mean(t * t, axis=-1, keepdims=True) + RMS_EPS)
    t = t.reshape(B, L, H * d) * norm_g.astype(F32)
    return (t * jax.nn.sigmoid(og.astype(F32))).astype(og.dtype)

def mlstm_mix(u_ctx, u_lat, conv_w, gate_b, norm_g):
    qc, kc, vc, oc, gc = mlstm_inputs(u_ctx, conv_w, gate_b)
    ql, kl, vl, ol, gl = mlstm_inputs(u_lat, conv_w, gate_b)
    B = u_ctx.shape[0]
    zero = (jnp.zeros((B, ML_HEADS, ML_HEAD_DIM, ML_HEAD_DIM), F32),
            jnp.zeros((B, ML_HEADS, ML_HEAD_DIM), F32),
            jnp.zeros((B, ML_HEADS), F32))
    hc_f, st_f = mlstm_direction(qc, kc, vc, gc[0], gc[1], zero, False)
    hl_f, _ = mlstm_direction(ql, kl, vl, gl[0], gl[1], st_f, False)
    hc_b, st_b = mlstm_direction(qc, kc, vc, gc[2], gc[3], zero, True)
    hl_b, _ = mlstm_direction(ql, kl, vl, gl[2], gl[3], st_b, True)
    return mlstm_out(hc_f + hc_b, oc, norm_g), mlstm_out(hl_f + hl_b, ol, norm_g)

def hyena_mlstm_mixer(h_ctx, h_lat, w_in, hy_conv_w, hy_conv_b, hy_filter, hy_bias,
                      ml_conv_w, ml_gate_b, ml_norm_g, w_out):
    u_ctx = h_ctx @ w_in
    u_lat = h_lat @ w_in
    hy_c = hyena_mix(u_ctx[..., :3 * HY_WIDTH], hy_conv_w, hy_conv_b, hy_filter, hy_bias)
    hy_l = hyena_mix(u_lat[..., :3 * HY_WIDTH], hy_conv_w, hy_conv_b, hy_filter, hy_bias)
    ml_c, ml_l = mlstm_mix(u_ctx, u_lat, ml_conv_w, ml_gate_b, ml_norm_g)
    y_ctx = jnp.concatenate([hy_c, ml_c], axis=-1) @ w_out
    y_lat = jnp.concatenate([hy_l, ml_l], axis=-1) @ w_out
    return y_ctx, y_lat

def rope_tables(T):
    n_rows = T // GRID_W
    row = jnp.repeat(jnp.arange(n_rows, dtype=F32), GRID_W)
    col = jnp.tile(jnp.arange(GRID_W, dtype=F32), n_rows)
    inv = ROPE_BASE ** (-jnp.arange(0, ROPE_AXIS, 2, dtype=F32) / ROPE_AXIS)
    ang = jnp.stack([row[:, None] * inv, col[:, None] * inv], axis=1)
    return jnp.cos(ang), jnp.sin(ang)

def apply_rope2d(x, cos, sin):
    xa = x.reshape(x.shape[:-1] + (2, ROPE_AXIS))
    x1, x2 = jnp.split(xa, 2, axis=-1)
    c = cos[None, :, None].astype(x.dtype)
    s = sin[None, :, None].astype(x.dtype)
    return jnp.concatenate([x1 * c - x2 * s, x2 * c + x1 * s], axis=-1).reshape(x.shape)

def mla_down(h, w_down):
    return jnp.split(h @ w_down, [MLA_Q_RANK, MLA_Q_RANK + MLA_KV_RANK], axis=-1)

def mla_q(q_a, q_norm, w_uq, rope):
    B, L, _ = q_a.shape
    q = (rmsnorm(q_a, q_norm) @ w_uq).reshape(B, L, MLA_HEADS, MLA_NOPE + MLA_ROPE)
    if rope is None:
        return q
    q_n, q_r = jnp.split(q, [MLA_NOPE], axis=-1)
    return jnp.concatenate([q_n, apply_rope2d(q_r, *rope)], axis=-1)

def mla_kv(kv_a, k_r, kv_norm, w_ukv, rope):
    B, L, _ = kv_a.shape
    kv = (rmsnorm(kv_a, kv_norm) @ w_ukv).reshape(B, L, MLA_HEADS, MLA_NOPE + MLA_V)
    k_n, v = jnp.split(kv, [MLA_NOPE], axis=-1)
    k_r = k_r[:, :, None, :]
    if rope is not None:
        k_r = apply_rope2d(k_r, *rope)
    k = jnp.concatenate([k_n, jnp.broadcast_to(k_r, (B, L, MLA_HEADS, MLA_ROPE))], axis=-1)
    return k, v

def attend(q, k, v):
    s = jnp.einsum('bqhd,bkhd->bhqk', q, k).astype(F32) * MLA_SCALE
    p = jax.nn.softmax(s, axis=-1).astype(v.dtype)
    return jnp.einsum('bhqk,bkhd->bqhd', p, v)

def mla_mixer(h_ctx, h_lat, ctx_queries, w_down, q_norm, kv_norm, w_uq, w_ukv, w_o):
    B, S, _ = h_lat.shape
    rope = rope_tables(S)
    qa_c, kva_c, kr_c = mla_down(h_ctx, w_down)
    qa_l, kva_l, kr_l = mla_down(h_lat, w_down)
    k_c, v_c = mla_kv(kva_c, kr_c, kv_norm, w_ukv, None)
    k_l, v_l = mla_kv(kva_l, kr_l, kv_norm, w_ukv, rope)
    q_l = mla_q(qa_l, q_norm, w_uq, rope)
    k_all = jnp.concatenate([k_c, k_l], axis=1)
    v_all = jnp.concatenate([v_c, v_l], axis=1)
    nb = S // Q_BLOCK
    qb = jnp.moveaxis(q_l.reshape(B, nb, Q_BLOCK, MLA_HEADS, MLA_NOPE + MLA_ROPE), 1, 0)
    o_l = lax.map(lambda blk: attend(blk, k_all, v_all), qb)
    y_lat = jnp.moveaxis(o_l, 0, 1).reshape(B, S, MLA_HEADS * MLA_V) @ w_o
    y_ctx = None
    if ctx_queries:
        q_c = mla_q(qa_c, q_norm, w_uq, None)
        y_ctx = attend(q_c, k_c, v_c).reshape(B, h_ctx.shape[1], MLA_HEADS * MLA_V) @ w_o
    return y_ctx, y_lat

def conv_ffn(h, w_up, conv_w, conv_b, w_down):
    g, u = jnp.split(h @ w_up, 2, axis=-1)
    g = dwconv(g, conv_w) + conv_b
    return (jax.nn.silu(g) * u) @ w_down

def first_inputs(seed: int = 0) -> dict:
    key = jax.random.key(seed)
    keys = iter(jax.random.split(key, 64))

    def nrm(shape, scale):
        return jax.random.normal(next(keys), shape, F32) * scale

    def gain(n):
        return 1.0 + nrm((n,), 0.02)

    def ffn():
        return (nrm((D_MODEL, 2 * D_FF), D_MODEL ** -0.5), nrm((SHORT_W, D_FF), SHORT_W ** -0.5),
                nrm((D_FF,), 0.02), nrm((D_FF, D_MODEL), D_FF ** -0.5))

    x = nrm((BATCH, SEQ, D_MODEL), 1.0)
    c = nrm((BATCH, D_MODEL), 1.0)
    ctx = nrm((BATCH, CTX_LEN, D_MODEL), 1.0)
    c_ctx = nrm((D_MODEL,), 1.0)
    forget_b = jnp.linspace(3.0, 6.0, ML_HEADS, dtype=F32)
    ml_gate_b = jnp.concatenate([nrm((ML_HEADS,), 0.1), forget_b + nrm((ML_HEADS,), 0.01),
                                 nrm((ML_HEADS,), 0.1), forget_b + nrm((ML_HEADS,), 0.01)])
    f0 = ffn()
    f1 = ffn()
    mix_w = HY_WIDTH + ML_WIDTH
    return {
        'x': x, 'c': c, 'ctx': ctx, 'c_ctx': c_ctx,
        'ada_w_0': nrm((D_MODEL, N_MOD * D_MODEL), 0.5 * D_MODEL ** -0.5),
        'ada_b_0': nrm((N_MOD * D_MODEL,), 0.02),
        'norm_mix_0': gain(D_MODEL), 'norm_ffn_0': gain(D_MODEL),
        'w_in_0': nrm((D_MODEL, IN0_COLS), D_MODEL ** -0.5),
        'hy_conv_w': nrm((SHORT_W, 3 * HY_WIDTH), SHORT_W ** -0.5),
        'hy_conv_b': nrm((3 * HY_WIDTH,), 0.02),
        'hy_fw1': nrm((HY_EMB, HY_FF), HY_EMB ** -0.5),
        'hy_fb1': nrm((HY_FF,), 0.02),
        'hy_fw2': nrm((HY_FF, HY_FF), HY_FF ** -0.5),
        'hy_fb2': nrm((HY_FF,), 0.02),
        'hy_fw3': nrm((HY_FF, 2 * HY_WIDTH), 0.05 * HY_FF ** -0.5),
        'hy_freq': gain(HY_FF),
        'hy_bias': nrm((HY_WIDTH,), 0.1),
        'ml_conv_w': nrm((SHORT_W, 2 * ML_WIDTH), SHORT_W ** -0.5),
        'ml_gate_b': ml_gate_b,
        'ml_norm_g': gain(ML_WIDTH),
        'w_out_0': nrm((mix_w, D_MODEL), mix_w ** -0.5),
        'ffn_up_0': f0[0], 'ffn_conv_w_0': f0[1], 'ffn_conv_b_0': f0[2], 'ffn_down_0': f0[3],
        'ada_w_1': nrm((D_MODEL, N_MOD * D_MODEL), 0.5 * D_MODEL ** -0.5),
        'ada_b_1': nrm((N_MOD * D_MODEL,), 0.02),
        'norm_mix_1': gain(D_MODEL), 'norm_ffn_1': gain(D_MODEL),
        'mla_w_down': nrm((D_MODEL, MLA_Q_RANK + MLA_KV_RANK + MLA_ROPE), D_MODEL ** -0.5),
        'mla_q_norm': gain(MLA_Q_RANK), 'mla_kv_norm': gain(MLA_KV_RANK),
        'mla_w_uq': nrm((MLA_Q_RANK, MLA_HEADS * (MLA_NOPE + MLA_ROPE)), MLA_Q_RANK ** -0.5),
        'mla_w_ukv': nrm((MLA_KV_RANK, MLA_HEADS * (MLA_NOPE + MLA_V)), MLA_KV_RANK ** -0.5),
        'mla_w_o': nrm((MLA_HEADS * MLA_V, D_MODEL), (MLA_HEADS * MLA_V) ** -0.5),
        'ffn_up_1': f1[0], 'ffn_conv_w_1': f1[1], 'ffn_conv_b_1': f1[2], 'ffn_down_1': f1[3],
        'final_norm': gain(D_MODEL),
    }

def first_block(x, c, ctx, c_ctx, ada_w_0, ada_b_0, norm_mix_0, norm_ffn_0, w_in_0, hy_conv_w, hy_conv_b,
              hy_fw1, hy_fb1, hy_fw2, hy_fb2, hy_fw3, hy_freq, hy_bias, ml_conv_w, ml_gate_b, ml_norm_g,
              w_out_0, ffn_up_0, ffn_conv_w_0, ffn_conv_b_0, ffn_down_0, ada_w_1, ada_b_1, norm_mix_1,
              norm_ffn_1, mla_w_down, mla_q_norm, mla_kv_norm, mla_w_uq, mla_w_ukv, mla_w_o, ffn_up_1,
              ffn_conv_w_1, ffn_conv_b_1, ffn_down_1, final_norm):
    ada_w = (ada_w_0, ada_w_1)
    ada_b = (ada_b_0, ada_b_1)
    norm_mix = (norm_mix_0, norm_mix_1)
    norm_ffn = (norm_ffn_0, norm_ffn_1)
    ffn_p = ((ffn_up_0, ffn_conv_w_0, ffn_conv_b_0, ffn_down_0),
             (ffn_up_1, ffn_conv_w_1, ffn_conv_b_1, ffn_down_1))
    hy_filter = (hy_fw1, hy_fb1, hy_fw2, hy_fb2, hy_fw3, hy_freq)
    x_lat, x_ctx = x, ctx
    for layer in range(DEPTH):
        last = layer == DEPTH - 1
        sh1, sc1, g1, sh2, sc2, g2 = ada_mod(c[:, None, :], ada_w[layer], ada_b[layer])
        csh1, csc1, cg1, csh2, csc2, cg2 = ada_mod(c_ctx, ada_w[layer], ada_b[layer])
        h_lat = rmsnorm(x_lat, norm_mix[layer]) * (1 + sc1) + sh1
        h_ctx = rmsnorm(x_ctx, norm_mix[layer]) * (1 + csc1) + csh1
        if layer % 2 == 0:
            y_ctx, y_lat = hyena_mlstm_mixer(h_ctx, h_lat, w_in_0, hy_conv_w, hy_conv_b, hy_filter, hy_bias,
                                             ml_conv_w, ml_gate_b, ml_norm_g, w_out_0)
        else:
            y_ctx, y_lat = mla_mixer(h_ctx, h_lat, not last, mla_w_down, mla_q_norm, mla_kv_norm,
                                     mla_w_uq, mla_w_ukv, mla_w_o)
        x_lat = x_lat + g1 * y_lat
        x_lat = x_lat + g2 * conv_ffn(rmsnorm(x_lat, norm_ffn[layer]) * (1 + sc2) + sh2, *ffn_p[layer])
        if not last:
            x_ctx = x_ctx + cg1 * y_ctx
            x_ctx = x_ctx + cg2 * conv_ffn(rmsnorm(x_ctx, norm_ffn[layer]) * (1 + csc2) + csh2, *ffn_p[layer])
    return rmsnorm(x_lat, final_norm)


DEPTH_2 = 1

HEAD_DIM = 64
N_Q_HEADS = 8
N_KV_HEADS = 2
GQA_GROUP = N_Q_HEADS // N_KV_HEADS
ATTN_W = N_Q_HEADS * HEAD_DIM
KV_W = N_KV_HEADS * HEAD_DIM
ROPE_THETA = 10000.0
SSD_HEAD_DIM = 64
SSD_HEADS = 8
SSD_W = SSD_HEADS * SSD_HEAD_DIM
SSD_GROUPS = 2
HEADS_PER_GROUP = SSD_HEADS // SSD_GROUPS
D_STATE = 64
D_CONV = 7
CONV_CH = SSD_W + 2 * SSD_GROUPS * D_STATE
CHUNK = 128
SPLIT_SIZES = (ATTN_W, KV_W, KV_W, SSD_W, CONV_CH, 2 * SSD_HEADS, 2 * D_MODEL)
IN_PROJ = sum(SPLIT_SIZES)
N_EXPERT_GROUPS = 4
EXPERTS_PER_GROUP = 4
N_EXPERTS = N_EXPERT_GROUPS * EXPERTS_PER_GROUP
TOP_K_IN_GROUP = 2
D_EXPERT = 512
EPS = 1e-6


def rmsnorm_2(x, w):
    xf = x.astype(jnp.float32)
    xf = xf * lax.rsqrt(jnp.mean(xf * xf, axis=-1, keepdims=True) + EPS)
    return xf.astype(x.dtype) * w

def rotate_half(u):
    u1, u2 = jnp.split(u, 2, axis=-1)
    return jnp.concatenate([-u2, u1], axis=-1)

def axial_rope_tables(seq_len, dtype):
    rows = seq_len // GRID_W
    row = jnp.repeat(jnp.arange(rows, dtype=jnp.int32), GRID_W)
    col = jnp.tile(jnp.arange(GRID_W, dtype=jnp.int32), rows)
    half = HEAD_DIM // 2
    inv_freq = ROPE_THETA ** (-jnp.arange(0, half, 2, dtype=jnp.float32) / half)
    ang_r = row.astype(jnp.float32)[:, None] * inv_freq[None, :]
    ang_c = col.astype(jnp.float32)[:, None] * inv_freq[None, :]
    cos = jnp.concatenate([jnp.cos(ang_r), jnp.cos(ang_r), jnp.cos(ang_c), jnp.cos(ang_c)], axis=-1)
    sin = jnp.concatenate([jnp.sin(ang_r), jnp.sin(ang_r), jnp.sin(ang_c), jnp.sin(ang_c)], axis=-1)
    return cos.astype(dtype), sin.astype(dtype)

def apply_axial_rope(x, cos, sin):
    xr, xc = jnp.split(x, 2, axis=-1)
    rot = jnp.concatenate([rotate_half(xr), rotate_half(xc)], axis=-1)
    return x * cos[None, :, None, :] + rot * sin[None, :, None, :]

def gqa_attention(q, k, v, q_norm_w, k_norm_w, cos, sin):
    b, s = q.shape[0], q.shape[1]
    q = apply_axial_rope(rmsnorm_2(q, q_norm_w), cos, sin)
    k = apply_axial_rope(rmsnorm_2(k, k_norm_w), cos, sin)
    scale = 1.0 / math.sqrt(HEAD_DIM)
    nb = s // Q_BLOCK
    qb = jnp.moveaxis(q.reshape(b, nb, Q_BLOCK, N_KV_HEADS, GQA_GROUP, HEAD_DIM), 1, 0)

    def one_block(qblk):
        scores = jnp.einsum('bqkgd,bskd->bkgqs', qblk, k).astype(jnp.float32) * scale
        p = jax.nn.softmax(scores, axis=-1).astype(v.dtype)
        return jnp.einsum('bkgqs,bskd->bqkgd', p, v)

    o = lax.map(one_block, qb)
    return jnp.moveaxis(o, 0, 1).reshape(b, s, ATTN_W)

def depthwise_centred_conv(u, w, bias):
    pad = (D_CONV - 1) // 2
    y = lax.conv_general_dilated(u, w[:, None, :], window_strides=(1,), padding=[(pad, pad)],
                                 dimension_numbers=('NWC', 'WIO', 'NWC'),
                                 feature_group_count=u.shape[-1])
    return y + bias

def ssd_chunked(x, dt, a, bm, cm):
    b, L, h, p = x.shape
    n = bm.shape[-1]
    c = L // CHUNK
    xc = x.reshape(b, c, CHUNK, h, p)
    dtc = dt.reshape(b, c, CHUNK, h)
    bc = bm.reshape(b, c, CHUNK, h, n)
    cc = cm.reshape(b, c, CHUNK, h, n)
    a_cum = jnp.cumsum(dtc * a, axis=2)
    seg = a_cum[:, :, :, None, :] - a_cum[:, :, None, :, :]
    tril = jnp.tril(jnp.ones((CHUNK, CHUNK), dtype=bool))[None, None, :, :, None]
    decay = jnp.exp(jnp.where(tril, seg, -jnp.inf))
    xdt = xc * dtc[..., None]
    cb = jnp.einsum('bcihn,bcjhn->bcijh', cc, bc)
    y_diag = jnp.einsum('bcijh,bcjhp->bcihp', cb * decay, xdt)
    decay_to_end = jnp.exp(a_cum[:, :, -1:, :] - a_cum)
    states = jnp.einsum('bcjhn,bcjhp->bchpn', bc * decay_to_end[..., None], xdt)
    chunk_decay = jnp.exp(a_cum[:, :, -1, :])

    def step(carry, inp):
        s_c, d_c = inp
        return carry * d_c[:, :, None, None] + s_c, carry

    h0 = jnp.zeros((b, h, p, n), dtype=x.dtype)
    _, states_in = lax.scan(step, h0, (jnp.moveaxis(states, 1, 0), jnp.moveaxis(chunk_decay, 1, 0)))
    states_in = jnp.moveaxis(states_in, 0, 1)
    y_off = jnp.einsum('bcihn,bchpn->bcihp', cc, states_in) * jnp.exp(a_cum)[..., None]
    return (y_diag + y_off).reshape(b, L, h, p)

def bidirectional_ssd(z, xbc, dt_raw, conv_w, conv_b, dt_bias, a_log, d_skip, norm_w):
    b, s = xbc.shape[0], xbc.shape[1]
    xbc = jax.nn.silu(depthwise_centred_conv(xbc, conv_w, conv_b))
    xs, bm, cm = jnp.split(xbc, [SSD_W, SSD_W + SSD_GROUPS * D_STATE], axis=-1)
    f32 = jnp.float32
    xs = xs.reshape(b, s, SSD_HEADS, SSD_HEAD_DIM).astype(f32)
    bm = jnp.repeat(bm.reshape(b, s, SSD_GROUPS, D_STATE), HEADS_PER_GROUP, axis=2).astype(f32)
    cm = jnp.repeat(cm.reshape(b, s, SSD_GROUPS, D_STATE), HEADS_PER_GROUP, axis=2).astype(f32)
    dt = jax.nn.softplus(dt_raw.reshape(b, s, 2, SSD_HEADS).astype(f32) + dt_bias.astype(f32))
    a = -jnp.exp(a_log.astype(f32))
    y_fwd = ssd_chunked(xs, dt[:, :, 0], a[0], bm, cm)
    flip = lambda u: jnp.flip(u, axis=1)
    y_bwd = flip(ssd_chunked(flip(xs), flip(dt[:, :, 1]), a[1], flip(bm), flip(cm)))
    y = y_fwd + y_bwd + d_skip.astype(f32)[None, None, :, None] * xs
    y = y.reshape(b, s, SSD_W).astype(z.dtype)
    return rmsnorm_2(y * jax.nn.silu(z), norm_w)

def hierarchical_moe(h, w_rg, b_rg, w_re, b_re, w1, w3, w2):
    b, s, d = h.shape
    t = h.reshape(b * s, d)
    p_group = jax.nn.softmax((t @ w_rg + b_rg).astype(jnp.float32), axis=-1)
    g_val, g_idx = lax.top_k(p_group, 1)
    fine = (t @ w_re + b_re).astype(jnp.float32).reshape(-1, N_EXPERT_GROUPS, EXPERTS_PER_GROUP)
    fine_sel = jnp.take_along_axis(fine, g_idx[:, :, None], axis=1)[:, 0]
    e_val, e_idx = lax.top_k(jax.nn.softmax(fine_sel, axis=-1), TOP_K_IN_GROUP)
    e_val = e_val / jnp.sum(e_val, axis=-1, keepdims=True)
    within = jnp.sum(jax.nn.one_hot(e_idx, EXPERTS_PER_GROUP, dtype=jnp.float32) * e_val[..., None], axis=1)
    combine = (jax.nn.one_hot(g_idx[:, 0], N_EXPERT_GROUPS, dtype=jnp.float32)[:, :, None]
               * within[:, None, :] * g_val[:, :, None]).reshape(-1, N_EXPERTS).astype(t.dtype)
    out = jnp.zeros_like(t)
    for e in range(N_EXPERTS):
        y_e = (jax.nn.silu(t @ w1[e]) * (t @ w3[e])) @ w2[e]
        out = out + combine[:, e:e + 1] * y_e
    return out.reshape(b, s, d)

def second_inputs(seed: int = 0) -> dict:
    key = jax.random.key(seed)
    ks = jax.random.split(key, 24)
    f32 = jnp.float32
    L = DEPTH_2

    def nrm(k, shape, fan_in):
        return jax.random.normal(k, shape, f32) * (fan_in ** -0.5)

    def gain(k, shape):
        return 1.0 + 0.02 * jax.random.normal(k, shape, f32)

    dt0 = jnp.exp(jax.random.uniform(ks[9], (L, 2, SSD_HEADS), f32, math.log(1e-3), math.log(1e-1)))
    dt_bias = dt0 + jnp.log(-jnp.expm1(-dt0))
    return {
        "x": jax.random.normal(ks[0], (BATCH, SEQ, D_MODEL), f32),
        "norm_mix_w": gain(ks[1], (L, D_MODEL)),
        "w_in": nrm(ks[2], (L, D_MODEL, IN_PROJ), D_MODEL),
        "b_gate": 0.02 * jax.random.normal(ks[3], (L, 2 * D_MODEL), f32),
        "q_norm_w": gain(ks[4], (L, HEAD_DIM)),
        "k_norm_w": gain(ks[5], (L, HEAD_DIM)),
        "w_attn_o": nrm(ks[6], (L, ATTN_W, D_MODEL), ATTN_W),
        "conv_w": nrm(ks[7], (L, D_CONV, CONV_CH), D_CONV),
        "conv_b": 0.02 * jax.random.normal(ks[8], (L, CONV_CH), f32),
        "dt_bias": dt_bias,
        "a_log": jnp.log(jax.random.uniform(ks[10], (L, 2, SSD_HEADS), f32, 1.0, 16.0)),
        "d_skip": 1.0 + 0.1 * jax.random.normal(ks[11], (L, SSD_HEADS), f32),
        "ssd_norm_w": gain(ks[12], (L, SSD_W)),
        "w_ssd_o": nrm(ks[13], (L, SSD_W, D_MODEL), SSD_W),
        "w_out": nrm(ks[14], (L, D_MODEL, D_MODEL), D_MODEL),
        "norm_ffn_w": gain(ks[15], (L, D_MODEL)),
        "w_router_group": nrm(ks[16], (L, D_MODEL, N_EXPERT_GROUPS), D_MODEL),
        "b_router_group": 0.01 * jax.random.normal(ks[17], (L, N_EXPERT_GROUPS), f32),
        "w_router_expert": nrm(ks[18], (L, D_MODEL, N_EXPERTS), D_MODEL),
        "b_router_expert": 0.01 * jax.random.normal(ks[19], (L, N_EXPERTS), f32),
        "w1": nrm(ks[20], (L, N_EXPERTS, D_MODEL, D_EXPERT), D_MODEL),
        "w3": nrm(ks[21], (L, N_EXPERTS, D_MODEL, D_EXPERT), D_MODEL),
        "w2": nrm(ks[22], (L, N_EXPERTS, D_EXPERT, D_MODEL), D_EXPERT),
    }

def second_block(x, norm_mix_w, w_in, b_gate, q_norm_w, k_norm_w, w_attn_o, conv_w, conv_b,
              dt_bias, a_log, d_skip, ssd_norm_w, w_ssd_o, w_out, norm_ffn_w,
              w_router_group, b_router_group, w_router_expert, b_router_expert, w1, w3, w2):
    b, s, _ = x.shape
    cos, sin = axial_rope_tables(s, x.dtype)
    split_at = [int(v) for v in np.cumsum(SPLIT_SIZES)[:-1]]
    for l in range(DEPTH_2):
        h = rmsnorm_2(x, norm_mix_w[l])
        proj = h @ w_in[l]
        q, k, v, z, xbc, dt_raw, gates = jnp.split(proj, split_at, axis=-1)
        q = q.reshape(b, s, N_Q_HEADS, HEAD_DIM)
        k = k.reshape(b, s, N_KV_HEADS, HEAD_DIM)
        v = v.reshape(b, s, N_KV_HEADS, HEAD_DIM)
        attn = gqa_attention(q, k, v, q_norm_w[l], k_norm_w[l], cos, sin)
        ssd = bidirectional_ssd(z, xbc, dt_raw, conv_w[l], conv_b[l], dt_bias[l],
                                a_log[l], d_skip[l], ssd_norm_w[l])
        g_attn, g_ssd = jnp.split(jax.nn.sigmoid(gates + b_gate[l]), 2, axis=-1)
        merged = g_attn * (attn @ w_attn_o[l]) + g_ssd * (ssd @ w_ssd_o[l])
        x = x + merged @ w_out[l]
        h2 = rmsnorm_2(x, norm_ffn_w[l])
        x = x + hierarchical_moe(h2, w_router_group[l], b_router_group[l], w_router_expert[l],
                                 b_router_expert[l], w1[l], w3[l], w2[l])
    return x


def setup_inputs(seed=0):
    out = dict(first_inputs(seed))
    for name, value in second_inputs(seed + 1).items():
        if name != "x":
            out[name + "_2"] = value
    return out


def reference(
    x, c, ctx, c_ctx, ada_w_0, ada_b_0, norm_mix_0, norm_ffn_0, w_in_0, hy_conv_w, hy_conv_b,
    hy_fw1, hy_fb1, hy_fw2, hy_fb2, hy_fw3, hy_freq, hy_bias, ml_conv_w, ml_gate_b, ml_norm_g,
    w_out_0, ffn_up_0, ffn_conv_w_0, ffn_conv_b_0, ffn_down_0, ada_w_1, ada_b_1, norm_mix_1,
    norm_ffn_1, mla_w_down, mla_q_norm, mla_kv_norm, mla_w_uq, mla_w_ukv, mla_w_o, ffn_up_1,
    ffn_conv_w_1, ffn_conv_b_1, ffn_down_1, final_norm, norm_mix_w_2, w_in_2, b_gate_2,
    q_norm_w_2, k_norm_w_2, w_attn_o_2, conv_w_2, conv_b_2, dt_bias_2, a_log_2, d_skip_2,
    ssd_norm_w_2, w_ssd_o_2, w_out_2, norm_ffn_w_2, w_router_group_2, b_router_group_2,
    w_router_expert_2, b_router_expert_2, w1_2, w3_2, w2_2,
):
    x = first_block(
        x, c, ctx, c_ctx, ada_w_0, ada_b_0, norm_mix_0, norm_ffn_0, w_in_0, hy_conv_w,
        hy_conv_b, hy_fw1, hy_fb1, hy_fw2, hy_fb2, hy_fw3, hy_freq, hy_bias, ml_conv_w,
        ml_gate_b, ml_norm_g, w_out_0, ffn_up_0, ffn_conv_w_0, ffn_conv_b_0, ffn_down_0,
        ada_w_1, ada_b_1, norm_mix_1, norm_ffn_1, mla_w_down, mla_q_norm, mla_kv_norm, mla_w_uq,
        mla_w_ukv, mla_w_o, ffn_up_1, ffn_conv_w_1, ffn_conv_b_1, ffn_down_1, final_norm,
    )
    return second_block(
        x, norm_mix_w_2, w_in_2, b_gate_2, q_norm_w_2, k_norm_w_2, w_attn_o_2, conv_w_2,
        conv_b_2, dt_bias_2, a_log_2, d_skip_2, ssd_norm_w_2, w_ssd_o_2, w_out_2, norm_ffn_w_2,
        w_router_group_2, b_router_group_2, w_router_expert_2, b_router_expert_2, w1_2, w3_2,
        w2_2,
    )


_drawn_inputs = setup_inputs


def setup_inputs(seed=0):
    import zlib

    import numpy as np

    out = dict(_drawn_inputs(seed))
    spreads = {}
    factors = {'norm_mix_0': 4.984,
     'norm_ffn_0': 2.771,
     'hy_conv_b': 5.659,
     'hy_fb1': 8.0,
     'hy_fb2': 5.563,
     'hy_freq': 8.0,
     'ml_norm_g': 28.648,
     'ffn_conv_b_0': 4.866,
     'norm_mix_1': 8.0,
     'norm_ffn_1': 3.035,
     'mla_q_norm': 8.0,
     'mla_kv_norm': 4.447,
     'ffn_conv_b_1': 4.506,
     'b_gate_2': 3.68,
     'q_norm_w_2': 8.0,
     'k_norm_w_2': 8.0,
     'ssd_norm_w_2': 2.727,
     'b_router_group_2': 11.186,
     'b_router_expert_2': 23.15,
     'norm_ffn_w_2': 4.046}
    for name, (base, spread) in spreads.items():
        noise = np.random.default_rng([zlib.crc32(name.encode()), seed]).standard_normal(out[name].shape)
        drawn = base * np.exp(spread * noise) if base else spread * noise
        out[name] = jnp.asarray(drawn.astype(out[name].dtype))
    for name, factor in factors.items():
        out[name] = (out[name] * factor).astype(out[name].dtype)
    return out
```

```python
from contextlib import ExitStack, contextmanager
import math

import numpy as np

import concourse.bass as bass
from concourse import mybir

F32 = mybir.dt.float32
ACT = mybir.ActivationFunctionType
ALU = mybir.AluOpType
AX = mybir.AxisListType

P = 128
D = 1024
DT = D // P
CTX = 256
LAT = 512
T = CTX + LAT
SEGS = ((0, CTX), (CTX, LAT))
SEG_LAT = ((CTX, LAT),)
N_MOD = 6
HY = 512
HYT = HY // P
HY_EMB = 33
HY_FF = 64
ML_HEADS = 4
ML_W = 512
D_FF = 2816
FFT = D_FF // P
MLA_HEADS = 8
Q_RANK = 384
KV_RANK = 256
ROPE = 64
MLA_SCALE = (128 + 64) ** -0.5
GRID_W = 64
EPS = 1e-6
BANK = 512
MAGIC = 1.5 * 2.0 ** 23
TWO_PI_HI = 6.28125
TWO_PI_LO = 2 * math.pi - TWO_PI_HI
PI_BELOW = 3.1415925
SSD_HEADS = 8
N_EXPERTS = 16
D_EXPERT = 512
ROWS = 64
BWD = 32
ATANH_TERMS = (15, 13, 11, 9, 7, 5, 3)


VECTORS = [
    ("c", 8), ("c_ctx", 8), ("ada_b_0", 48), ("ada_b_1", 48), ("norm_mix_0", 8), ("norm_ffn_0", 8),
    ("norm_mix_1", 8), ("norm_ffn_1", 8), ("final_norm", 8), ("norm_mix_w_2", 8), ("norm_ffn_w_2", 8),
    ("hy_conv_w", 36), ("hy_conv_b", 12), ("hy_bias", 4), ("ml_conv_w", 24), ("ml_norm_g", 4),
    ("ffn_conv_w_0", 66), ("ffn_conv_b_0", 22), ("ffn_conv_w_1", 66), ("ffn_conv_b_1", 22),
    ("mla_q_norm", 3), ("mla_kv_norm", 2), ("b_gate_2", 16), ("conv_w_2", 42), ("conv_b_2", 6),
    ("ssd_norm_w_2", 4), ("qk_norm_2", 2), ("hy_small", 3), ("ml_gate_b", 1), ("ssd_rows", 2),
    ("d_skip", 4), ("b_router", 20),
]
COL = {}
_at = 0
for _name, _n in VECTORS:
    COL[_name] = _at
    _at += _n
N_COLS = _at

CONSTS = [("ident", 128), ("ones", 128), ("ones64", 128), ("onecol", 127), ("s_le_t", 128), ("s_ge_t", 128),
          ("rot_gqa", 128), ("eps", 1), ("first", 4)]
CAT = {}
_at = 0
for _name, _n in CONSTS:
    CAT[_name] = _at
    _at += _n
N_CONST = _at


class Kernel:

    def __init__(self, nc, ctx, dram):
        self.nc, self.ctx, self.dram = nc, ctx, dram

        def sb(name, cols):
            return ctx.enter_context(nc.sbuf_tensor(name, [P, cols], F32))

        self.x = sb("x_res", DT * T)[:, :].rearrange("p (k t) -> p k t", t=T)
        self.h = sb("h_norm", DT * T)[:, :].rearrange("p (k t) -> p k t", t=T)
        self.arena = sb("arena", 24576)
        self.ring = sb("ring", 12288)
        self.vec = sb("vec", N_COLS)
        self.cst = sb("cst", N_CONST)
        self.mod = sb("mod", N_MOD * DT * 2)[:, :].rearrange("p (n c) -> p n c", c=2)
        self.mod_next = sb("mod_next", N_MOD * DT * 2)[:, :].rearrange("p (n c) -> p n c", c=2)
        self.gain = sb("gain", 2 * DT * 2)[:, :].rearrange("p (a k c) -> p a k c", a=2, c=2)
        self.silu_c = sb("silu_c", DT * 2)[:, :].rearrange("p (k c) -> p k c", c=2)
        self.row = sb("row", T)
        self.ps = ctx.enter_context(nc.psum_tensor("ps", [P, 8 * BANK], F32))
        self.n_stage, self.used = 0, 0
        self.sems = [[ctx.enter_context(nc.semaphore(f"{n}_{s}")) for s in range(32)] for n in ("even", "odd")]

    def stage(self):
        self.n_stage += 1
        self.spent, self.used = self.used, 0

    def sem(self, name):
        self.used += 1
        return self.sems[self.n_stage % 2][self.used - 1]

    @contextmanager
    def block(self):
        with self.nc.Block() as block:
            @block.gpsimd
            def _(pool):
                for s in self.sems[(self.n_stage + 1) % 2][:self.spent]:
                    pool.sem_clear(s)
            yield block

    def col(self, name, n=0):
        return self.vec[:, bass.ds(n + COL[name], 1)]

    def const(self, name, width=None, at=0):
        n = dict(CONSTS)[name] if width is None else width
        return self.cst[:, CAT[name] + at:CAT[name] + at + n]

    def bank(self, b, n=BANK, at=0):
        return self.ps[:, b * BANK + at:b * BANK + at + n]

    def pair(self, p):
        return self.ps[:, 2 * p * BANK + BANK - CTX:(2 * p + 2) * BANK]

    def area(self, at, tiles, width):
        return self.arena[:, at:at + tiles * width].rearrange("p (k t) -> p k t", t=width)


class Chain:

    def __init__(self, engine, sem):
        self.engine, self.sem, self.n, self.base = engine, sem, 0, 0

    def link(self, instruction):
        self.n += 1
        instruction.then_inc(self.sem, 1)
        self.engine.wait_ge(self.sem, self.base + self.n)

    def turn(self, i, per_turn):
        self.n, self.base = 0, i * per_turn


def free_all(engine, sems):
    for s in sems:
        engine.sem_inc(s, 1)


class Stream:

    def __init__(self, k, name, slots):
        self.src, self.slots = k.dram[name], slots
        self.tiles = self.src.shape[0]
        self.n = len(slots)
        self.landed = [k.sem(f"landed{s}") for s in range(self.n)]
        assert self.tiles % self.n == 0

    def load(self, sp, used):
        for s in range(self.n):
            sp.dma_start(self.slots[s], self.src[s]).then_inc(self.landed[s], 16)
        if self.tiles > self.n:
            with sp.Fori(1, self.tiles // self.n) as i:
                for s in range(self.n):
                    sp.wait_ge(used[s], i)
                    sp.dma_start(self.slots[s], self.src[i * self.n + s]).then_inc(self.landed[s], 16)


def ring_slots(k, n, width, at=0):
    return [k.ring[:, at + s * width:at + (s + 1) * width] for s in range(n)]


def project(k, pe, slot, kt, x_of, psum_of, segs, m=P, col=0, width=P):
    for s, (t0, n) in enumerate(segs):
        for kk in range(kt):
            last = k.nc.tensor.matmul(psum_of(s), slot[:, kk * width + col:kk * width + col + m],
                                      x_of(kk)[:, t0:t0 + n], start=kk == 0, stop=kk == kt - 1)
    return last


def seg_out(k, p):
    pair = k.pair(p)
    return lambda s: pair[:, SEGS[s][0]:SEGS[s][0] + SEGS[s][1]]


def load_inputs(k):
    nc = k.nc
    k.stage()
    tok = k.area(0, 6, D)
    consts, tokens = k.sem("consts"), k.sem("tokens")
    turned = [k.sem("turned_wide"), k.sem("turned_narrow")]
    kept = [k.sem("kept_wide"), k.sem("kept_narrow")]
    halves = ((0, 4), (4, 2))
    with k.block() as block:
        @block.sync
        def _(sp):
            sp.dma_start(k.cst[:, :], k.dram["consts"]).then_inc(consts, 16)
            sp.dma_start(tok[:, 0:2, :], k.dram["ctx"].rearrange("(a p) d -> p a d", p=P)).then_inc(tokens, 16)
            sp.dma_start(tok[:, 2:6, :], k.dram["x"].rearrange("(a p) d -> p a d", p=P)).then_inc(tokens, 16)
            sp.dma_start(k.vec[:, :], k.dram["vectors"]).then_inc(consts, 16)
            sp.wait_ge(consts, 32)

        @block.tensor
        def _(pe):
            pe.wait_ge(consts, 32)
            pe.wait_ge(tokens, 32)
            for d in range(DT):
                for g, (a0, n) in enumerate(halves):
                    if d >= 4:
                        pe.wait_ge(kept[g], d - 3)
                    for a in range(n):
                        last = nc.tensor.transpose(k.bank(2 * (d % 4) + g, P, a * P),
                                                   tok[:, a0 + a, d * P:(d + 1) * P], k.const("ident"))
                    last.then_inc(turned[g], 1)

        @block.vector
        def _(dve):
            for d in range(DT):
                dve.wait_ge(turned[0], d + 1)
                nc.vector.tensor_copy(k.x[:, d, 0:4 * P], k.bank(2 * (d % 4))).then_inc(kept[0], 1)

        @block.scalar
        def _(act):
            for d in range(DT):
                act.wait_ge(turned[1], d + 1)
                nc.scalar.copy(k.x[:, d, 4 * P:T], k.bank(2 * (d % 4) + 1, 2 * P)).then_inc(kept[1], 1)
            act.wait_ge(consts, 32)
            nc.scalar.activation(k.silu_c[:, :, 0], k.vec[:, COL["c"]:COL["c"] + DT], ACT.Silu)
            nc.scalar.activation(k.silu_c[:, :, 1], k.vec[:, COL["c_ctx"]:COL["c_ctx"] + DT], ACT.Silu)


def mixer_gains(k, layer, mod):
    for a, norm in enumerate(("norm_mix", "norm_ffn")):
        w = COL[f"{norm}_{layer}"]
        for c in range(2):
            k.nc.vector.scalar_tensor_tensor(
                out=k.gain[:, a, :, c], in0=mod[:, (3 * a + 1) * DT:(3 * a + 2) * DT, c], scalar=1.0,
                in1=k.vec[:, w:w + DT], op0=ALU.add, op1=ALU.mult)


def modulations(k, layer):
    nc = k.nc
    k.stage()
    n = 8
    stream = Stream(k, f"ada_w_{layer}", ring_slots(k, n, D))
    done = [k.sem(f"product{s}") for s in range(n)]
    kept = [k.sem(f"kept{s}") for s in range(n)]
    all_kept = k.sem("all_kept")
    turns = stream.tiles // n
    with k.block() as block:
        @block.sync
        def _(sp):
            stream.load(sp, done)

        @block.tensor
        def _(pe):
            with pe.Fori(0, turns) as i:
                for s in range(n):
                    pe.wait_ge(stream.landed[s], 16 * i + 16)
                    pe.wait_ge(kept[s], i + 1)
                    for kk in range(DT):
                        last = nc.tensor.matmul(k.bank(s, 2), stream.slots[s][:, kk * P:(kk + 1) * P],
                                                k.silu_c[:, kk, :], start=kk == 0, stop=kk == DT - 1)
                    last.then_inc(done[s], 1)

        @block.vector
        def _(dve):
            free_all(dve, kept)
            with dve.Fori(0, turns) as i:
                for s in range(n):
                    dve.wait_ge(done[s], i + 1)
                    nc.vector.tensor_scalar(k.mod[:, i * n + s, :], k.bank(s, 2), k.col(f"ada_b_{layer}", i * n + s),
                                            None, ALU.add).then_inc(kept[s], 1)
            for s in range(n):
                dve.wait_ge(kept[s], turns + 1)
            mixer_gains(k, layer, k.mod)


def normalise(k, gain_of, shift_of, segs, dst=None, x=None, kt=DT, root_of=D):
    nc = k.nc
    k.stage()
    dst, x = k.h if dst is None else dst, k.x if x is None else x
    sq = k.h
    t0, t1 = segs[0][0], T
    squares, sums, root, scaled, inverse, ends = (k.sem(s) for s in ("squares", "sums", "root", "scaled", "inverse", "ends"))
    with k.block() as block:
        @block.scalar
        def _(act):
            for kk in range(kt):
                nc.scalar.activation(sq[:, kk, t0:t1], x[:, kk, t0:t1], ACT.Square).then_inc(squares, 1)
            act.wait_ge(sums, 1)
            nc.scalar.activation(k.row[:, t0:t1], k.pair(0)[:, t0:t1], ACT.Sqrt, bias=k.const("eps"),
                                 scale=1.0 / root_of).then_inc(root, 1)
            for kk in range(kt):
                act.wait_ge(scaled, kk + 1)
                for s, (a, n) in enumerate(segs):
                    c = 0 if a else 1
                    shift = 0.0 if shift_of is None else shift_of(kk, c)
                    nc.scalar.activation(dst[:, kk, a:a + n], dst[:, kk, a:a + n], ACT.Identity,
                                         scale=gain_of(kk, c), bias=shift)

        @block.tensor
        def _(pe):
            for kk in range(kt):
                pe.wait_ge(squares, kk + 1)
                for a, n in segs:
                    last = nc.tensor.matmul(k.pair(0)[:, a:a + n], k.const("ones"), sq[:, kk, a:a + n],
                                            start=kk == 0, stop=kk == kt - 1)
            last.then_inc(sums, 1)

        @block.vector
        def _(dve):
            dve.wait_ge(root, 1)
            nc.vector.reciprocal(k.row[:, t0:t1], k.row[:, t0:t1]).then_inc(inverse, 1)
            dve.wait_ge(inverse, 1)
            for kk in range(kt):
                nc.vector.tensor_tensor(dst[:, kk, t0:t1], x[:, kk, t0:t1], k.row[:, t0:t1],
                                        ALU.mult).then_inc(scaled, 1)


def project_conv(k, weights, dst, conv_w, conv_b, silu, taps=3, segs=SEGS):
    nc = k.nc
    k.stage()
    stream = Stream(k, weights, ring_slots(k, 2, D))
    tiles, turns = stream.tiles, stream.tiles // 2
    t0 = segs[0][0]
    product, taken = [k.sem("product0"), k.sem("product1")], [k.sem("taken0"), k.sem("taken1")]
    middle, summed = k.sem("middle"), k.sem("summed")
    offsets = [o - taps // 2 for o in range(taps) if o != taps // 2]
    per_tile = len(offsets) * len(segs)

    def sums(n, p):
        return k.ring[:, 2 * D + p * T:2 * D + (p + 1) * T][:, t0:T] if silu else dst[:, n, :]

    with k.block() as block:
        @block.sync
        def _(sp):
            stream.load(sp, product)

        @block.tensor
        def _(pe):
            with pe.Fori(0, turns) as i:
                for p in range(2):
                    pe.wait_ge(stream.landed[p], 16 * i + 16)
                    pe.wait_ge(taken[p], i + 1)
                    project(k, pe, stream.slots[p], DT, lambda kk: k.h[:, kk, :],
                            lambda s: k.pair(p)[:, segs[s][0]:segs[s][0] + segs[s][1]], segs).then_inc(product[p], 1)

        @block.scalar
        def _(act):
            with act.Fori(0, turns) as i:
                for p in range(2):
                    n = 2 * i + p
                    act.wait_ge(product[p], i + 1)
                    bias = k.col(conv_b, n) if conv_b else 0.0
                    nc.scalar.activation(sums(n, p), k.pair(p)[:, t0:T], ACT.Identity,
                                         scale=k.col(conv_w, n + tiles * (taps // 2)), bias=bias).then_inc(middle, 1)
                    if silu:
                        act.wait_ge(summed, per_tile * (n + 1))
                        nc.scalar.activation(dst[:, n, :], sums(n, p), ACT.Silu)

        @block.vector
        def _(dve):
            free_all(dve, taken)
            with dve.Fori(0, turns) as i:
                for p in range(2):
                    n = 2 * i + p
                    dve.wait_ge(middle, n + 1)
                    for m, o in enumerate(offsets):
                        for a, w in segs:
                            lo, hi = max(a, a - o), min(a + w, a + w - o)
                            out = sums(n, p)[:, lo - t0:hi - t0]
                            nc.vector.scalar_tensor_tensor(out=out, in0=k.pair(p)[:, lo + o:hi + o],
                                                           scalar=k.col(conv_w, n + tiles * (o + taps // 2)), in1=out,
                                                           op0=ALU.mult, op1=ALU.add).then_inc(summed, 1)
                        dve.wait_ge(summed, per_tile * n + len(segs) * (m + 1))
                    nc.vector.sem_inc(taken[p], 1)


def ffn_up(k, layer, hidden, scratch, segs, ada=False):
    nc = k.nc
    k.stage()
    stream = Stream(k, f"ffn_up_{layer}", ring_slots(k, 2, 2 * D))
    turns, ns = stream.tiles // 2, len(segs)
    t0, t1 = segs[0][0], T
    conv_w, conv_b = f"ffn_conv_w_{layer}", f"ffn_conv_b_{layer}"
    product, taken = [k.sem("product0"), k.sem("product1")], [k.sem("taken0"), k.sem("taken1")]
    middle, left, right, gated, scratch_free = (k.sem(s) for s in ("middle", "left", "right", "gated", "scratch_free"))
    ada_w = k.dram[f"ada_w_{layer + 1}"] if ada else None
    ada_slot = [k.ring[:, (4 + s) * D:(5 + s) * D] for s in range(8)]
    ada_landed = [k.sem(f"ada_landed{s}") for s in range(8)]
    ada_done, ada_kept = k.sem("ada_done"), k.sem("ada_kept")
    in_loop = 4 * turns

    def modulate(pe, slot, out):
        for kk in range(DT):
            last = nc.tensor.matmul(out, slot[:, kk * P:(kk + 1) * P], k.silu_c[:, kk, :], start=kk == 0,
                                    stop=kk == DT - 1)
        return last

    def modulated(n, product):
        return nc.vector.tensor_scalar(k.mod_next[:, n, :], product, k.col(f"ada_b_{layer + 1}", n), None, ALU.add)

    with k.block() as block:
        @block.sync
        def _(sp):
            if not ada:
                stream.load(sp, product)
                return
            for p in range(2):
                sp.dma_start(stream.slots[p], stream.src[p]).then_inc(stream.landed[p], 16)
            for s in range(8):
                tile = s if s < 4 else in_loop + s - 4
                sp.dma_start(ada_slot[s], ada_w[tile]).then_inc(ada_landed[s], 16)
            with sp.Fori(1, turns) as i:
                for p in range(2):
                    sp.wait_ge(product[p], i)
                    sp.dma_start(stream.slots[p], stream.src[2 * i + p]).then_inc(stream.landed[p], 16)
                    for s in (2 * p, 2 * p + 1):
                        sp.dma_start(ada_slot[s], ada_w[4 * i + s]).then_inc(ada_landed[s], 16)

        @block.tensor
        def _(pe):
            with pe.Fori(0, turns) as i:
                for p in range(2):
                    pe.wait_ge(stream.landed[p], 16 * i + 16)
                    pe.wait_ge(taken[p], i + 1)
                    if ada:
                        for s in (2 * p, 2 * p + 1):
                            pe.wait_ge(ada_landed[s], 16 * i + 16)
                            modulate(pe, ada_slot[s], k.bank(4 * p, 2, 2 * (s % 2)))
                    for half in range(2):
                        last = project(k, pe, stream.slots[p], DT, lambda kk: k.h[:, kk, :],
                                       lambda s: k.pair(2 * p + half)[:, segs[s][0]:segs[s][0] + segs[s][1]],
                                       segs, col=half * P, width=2 * P)
                    last.then_inc(product[p], 1)
            if ada:
                pe.wait_ge(taken[0], turns + 1)
                for s in range(4, 8):
                    pe.wait_ge(ada_landed[s], 16)
                    last = modulate(pe, ada_slot[s], k.bank(0, 2, 2 * (s - 4)))
                last.then_inc(ada_done, 1)

        @block.scalar
        def _(act):
            with act.Fori(0, turns) as i:
                for p in range(2):
                    n = 2 * i + p
                    act.wait_ge(product[p], i + 1)
                    act.wait_ge(taken[p], i + 1)
                    nc.scalar.activation(scratch[:, p, t0:t1], k.pair(2 * p)[:, t0:t1], ACT.Identity,
                                         scale=k.col(conv_w, n + FFT), bias=k.col(conv_b, n)).then_inc(middle, 1)
                    act.wait_ge(right, ns * (n + 1))
                    nc.scalar.activation(scratch[:, p, t0:t1], scratch[:, p, t0:t1], ACT.Silu).then_inc(gated, 1)

        @block.vector
        def _(dve):
            free_all(dve, taken)
            with dve.Fori(0, turns) as i:
                for p in range(2):
                    n = 2 * i + p
                    dve.wait_ge(middle, n + 1)
                    if ada:
                        for s in (2 * p, 2 * p + 1):
                            modulated(4 * i + s, k.bank(4 * p, 2, 2 * (s % 2))).then_inc(ada_kept, 1)
                    for a, w in segs:
                        out = scratch[:, p, a + 1:a + w]
                        nc.vector.scalar_tensor_tensor(out=out, in0=k.pair(2 * p)[:, a:a + w - 1],
                                                       scalar=k.col(conv_w, n), in1=out, op0=ALU.mult,
                                                       op1=ALU.add).then_inc(left, 1)
                    dve.wait_ge(left, ns * (n + 1))
                    for a, w in segs:
                        out = scratch[:, p, a:a + w - 1]
                        nc.vector.scalar_tensor_tensor(out=out, in0=k.pair(2 * p)[:, a + 1:a + w],
                                                       scalar=k.col(conv_w, n + 2 * FFT), in1=out,
                                                       op0=ALU.mult, op1=ALU.add).then_inc(right, 1)
                    dve.wait_ge(gated, n + 1)
                    nc.vector.tensor_tensor(hidden[:, n, t0:t1], scratch[:, p, t0:t1],
                                            k.pair(2 * p + 1)[:, t0:t1], ALU.mult).then_inc(taken[p], 1)
            if ada:
                dve.wait_ge(ada_done, 1)
                for s in range(4):
                    modulated(in_loop + s, k.bank(0, 2, 2 * s)).then_inc(ada_kept, 1)
                dve.wait_ge(ada_kept, in_loop + 4)
                mixer_gains(k, layer + 1, k.mod_next)


def project_residual(k, weights, kt, x_of, mod_index, segs, mod=None):
    nc = k.nc
    mod = k.mod if mod is None else mod
    k.stage()
    stream = Stream(k, weights, ring_slots(k, 2, kt * P))
    turns = stream.tiles // 2
    product, taken = [k.sem("product0"), k.sem("product1")], [k.sem("taken0"), k.sem("taken1")]
    with k.block() as block:
        @block.sync
        def _(sp):
            stream.load(sp, product)

        @block.tensor
        def _(pe):
            with pe.Fori(0, turns) as i:
                for p in range(2):
                    pe.wait_ge(stream.landed[p], 16 * i + 16)
                    pe.wait_ge(taken[p], i + 1)
                    project(k, pe, stream.slots[p], kt, x_of,
                            lambda s: k.pair(p)[:, segs[s][0]:segs[s][0] + segs[s][1]], segs).then_inc(product[p], 1)

        @block.vector
        def _(dve):
            free_all(dve, taken)
            with dve.Fori(0, turns) as i:
                for p in range(2):
                    n = 2 * i + p
                    dve.wait_ge(product[p], i + 1)
                    for a, w in segs:
                        x = k.x[:, n, a:a + w]
                        gate = 1.0 if mod_index is None else mod[:, bass.ds(n + mod_index * DT, 1), 0 if a else 1]
                        last = nc.vector.scalar_tensor_tensor(out=x, in0=k.pair(p)[:, a:a + w], scalar=gate, in1=x,
                                                              op0=ALU.mult, op1=ALU.add)
                    last.then_inc(taken[p], 1)


def hyena(k, u):
    nc = k.nc
    k.stage()
    A = 9216
    gain_at = 8 * T
    fw = k.arena[:, 22016:23168]
    fw1, fw2, fw3 = fw[0:HY_EMB, 0:64], fw[0:HY_FF, 64:128], fw[0:HY_FF, 128:1152]
    ml_rows = k.area(18432, 4, 512)
    tmp = k.area(17408, 2, 512)
    loads, kept, done, sine, drawn = (k.sem(s) for s in ("loads", "kept", "done", "sine", "drawn"))
    sizes = []
    for L, off, ring_at, dec, z, g_at in ((LAT, CTX, 0, k.ring[:, 10240:12288], k.arena[:, 20480:20992], gain_at),
                                          (CTX, 0, 8192, k.arena[:, 20992:22016], k.arena[:, 23168:23424], gain_at + 2048)):
        n = L // P
        tab = [k.ring[:, ring_at + j * n * L:ring_at + (j + 1) * n * L].rearrange("p (a t) -> p a t", t=L) for j in range(4)]
        sizes.append((L, off, n, tab, dec.rearrange("p (a c) -> p a c", c=HY), z[0:HY_EMB, :], k.area(g_at, n, HY)))
    spec = k.area(13312, 8, HY)
    hsum, hdif = k.area(A, 4, HY), k.area(A + 2048, 4, HY)
    yspec = k.area(A, 8, HY)
    with k.block() as block:
        @block.sync
        def _(sp):
            sp.dma_start(fw1, k.dram["hy_fw1"]).then_inc(loads, 16)
            sp.dma_start(fw2, k.dram["hy_fw2"]).then_inc(loads, 16)
            sp.dma_start(fw3, k.dram["hy_fw3"]).then_inc(loads, 16)
            for size, name in zip(sizes, ("lat", "ctx")):
                L, off, n, tab, dec, z, gT = size
                sp.dma_start(z, k.dram[f"hy_pos_{name}"]).then_inc(loads, 16)
                sp.dma_start(dec, k.dram[f"hy_decay_{name}"]).then_inc(loads, 16)
                for j in range(4):
                    sp.dma_start(tab[j], k.dram[f"hy_dft_{name}"][j]).then_inc(loads, 16)

        @block.tensor
        def _(pe):
            pe.wait_ge(loads, 16 * 15)
            group = 0

            def begin(need=0):
                need = max(need, group - 3)
                if need > 0:
                    pe.wait_ge(kept, need)
                return 2 * (group % 4)
            for turn, (L, off, n, tab, dec, z, gT) in enumerate(sizes):
                base = group
                b = begin()
                nc.tensor.matmul(k.bank(b, L)[0:HY_FF, :], fw1, z, start=True, stop=True).then_inc(done, 1)
                group += 1
                if turn == 0:
                    pe.wait_ge(drawn, 1)
                for a in range(n):
                    b = begin()
                    for c in range(HYT):
                        last = nc.tensor.transpose(k.bank(b, P, c * P), u[:, 4 + c, off + a * P:off + (a + 1) * P],
                                                   k.const("ident"))
                    last.then_inc(done, 1)
                    group += 1
                b = begin()
                pe.wait_ge(sine, 2 * turn + 1)
                nc.tensor.matmul(k.bank(b, L)[0:HY_FF, :], fw2, ml_rows[0:HY_FF, 2, 0:L], start=True,
                                 stop=True).then_inc(done, 1)
                group += 1
                pe.wait_ge(sine, 2 * turn + 2)
                for a in range(n):
                    b = begin()
                    for half in range(2):
                        last = nc.tensor.matmul(k.bank(b + half), ml_rows[0:HY_FF, 3, a * P:(a + 1) * P],
                                                fw3[:, half * HY:(half + 1) * HY], start=True, stop=True)
                    last.then_inc(done, 1)
                    group += 1
                filters = group
                for f in range(n):
                    b = begin(filters)
                    for part, src in ((0, hsum), (1, hdif)):
                        for a in range(n):
                            last = nc.tensor.matmul(k.bank(b + part), tab[part][:, a, f * P:(f + 1) * P], src[:, a, :],
                                                    start=a == 0, stop=a == n - 1)
                    last.then_inc(done, 1)
                    group += 1
                spectra = group
                for f in range(n):
                    b = begin(spectra)
                    for part in range(2):
                        for a in range(n):
                            last = nc.tensor.matmul(k.bank(b + part), tab[part][:, a, f * P:(f + 1) * P], gT[:, a, :],
                                                    start=a == 0, stop=a == n - 1)
                    last.then_inc(done, 1)
                    group += 1
                products = group
                for c in range(HYT):
                    b = begin(products)
                    for part in range(2):
                        for f in range(n):
                            last = nc.tensor.matmul(k.bank(b, L), yspec[:, 4 * part + f, c * P:(c + 1) * P],
                                                    tab[2 + part][:, f, :], start=part == 0 and f == 0,
                                                    stop=part == 1 and f == n - 1)
                    last.then_inc(done, 1)
                    group += 1

        @block.scalar
        def _(act):
            for turn, size in enumerate(sizes):
                for layer in range(2):
                    act.wait_ge(drawn, 2 * turn + layer + 2)
                    nc.scalar.activation(ml_rows[0:HY_FF, 2 + layer, 0:size[0]], ml_rows[0:HY_FF, layer, 0:size[0]],
                                         ACT.Sin).then_inc(sine, 1)

        @block.vector
        def _(dve):
            chain = Chain(dve, k.sem("chain"))
            group = 0
            nc.vector.tensor_tensor(u[:, 4:8, :], u[:, 4:8, :], u[:, 8:12, :], ALU.mult).then_inc(drawn, 1)
            dve.wait_ge(drawn, 1)

            def sine_argument(b, L, layer, bias):
                arg, turns = ml_rows[0:HY_FF, layer, 0:L], tmp[0:HY_FF, 0, 0:L]
                chain.link(nc.vector.tensor_scalar(arg, k.bank(b, L)[0:HY_FF, :],
                                                   k.vec[0:HY_FF, COL["hy_small"] + bias:COL["hy_small"] + bias + 1],
                                                   k.vec[0:HY_FF, COL["hy_small"] + 2:COL["hy_small"] + 3],
                                                   ALU.add, ALU.mult))
                chain.link(nc.vector.tensor_scalar(turns, arg, 1 / (2 * math.pi), MAGIC, ALU.mult, ALU.add))
                chain.link(nc.vector.tensor_scalar(turns, turns, MAGIC, None, ALU.subtract))
                for part in (TWO_PI_HI, TWO_PI_LO):
                    chain.link(nc.vector.scalar_tensor_tensor(out=arg, in0=turns, scalar=-part, in1=arg,
                                                              op0=ALU.mult, op1=ALU.add))
                nc.vector.tensor_scalar(arg, arg, PI_BELOW, -PI_BELOW, ALU.min, ALU.max).then_inc(drawn, 1)

            def take(ins):
                ins.then_inc(kept, 1)

            for turn, (L, off, n, tab, dec, z, gT) in enumerate(sizes):
                dve.wait_ge(done, group + 1)
                sine_argument(2 * (group % 4), L, 0, 0)
                dve.wait_ge(drawn, 2 * turn + 2)
                nc.vector.sem_inc(kept, 1)
                group += 1
                for a in range(n):
                    dve.wait_ge(done, group + 1)
                    take(nc.vector.tensor_copy(gT[:, a, :], k.bank(2 * (group % 4))))
                    group += 1
                dve.wait_ge(done, group + 1)
                sine_argument(2 * (group % 4), L, 1, 1)
                dve.wait_ge(drawn, 2 * turn + 3)
                nc.vector.sem_inc(kept, 1)
                group += 1
                for a in range(n):
                    dve.wait_ge(done, group + 1)
                    b = 2 * (group % 4)
                    for half in range(2):
                        chain.link(nc.vector.tensor_tensor(tmp[:, half, :], k.bank(b + half), dec[:, a, :], ALU.mult))
                    if a == 0:
                        chain.link(nc.vector.memset(tmp[0:1, 1, :], 0.0))
                    chain.link(nc.vector.tensor_tensor(hsum[:, a, :], tmp[:, 0, :], tmp[:, 1, :], ALU.add))
                    take(nc.vector.tensor_tensor(hdif[:, a, :], tmp[:, 0, :], tmp[:, 1, :], ALU.subtract))
                    dve.wait_ge(kept, group + 1)
                    group += 1
                for f in range(n):
                    dve.wait_ge(done, group + 1)
                    b = 2 * (group % 4)
                    chain.link(nc.vector.tensor_copy(spec[:, f, :], k.bank(b)))
                    take(nc.vector.tensor_copy(spec[:, 4 + f, :], k.bank(b + 1)))
                    group += 1
                dve.wait_ge(kept, group)
                for f in range(n):
                    dve.wait_ge(done, group + 1)
                    b = 2 * (group % 4)
                    re, im = spec[:, f, :], spec[:, 4 + f, :]
                    chain.link(nc.vector.tensor_tensor(tmp[:, 0, :], k.bank(b), re, ALU.mult))
                    chain.link(nc.vector.tensor_tensor(tmp[:, 1, :], k.bank(b + 1), im, ALU.mult))
                    chain.link(nc.vector.tensor_tensor(yspec[:, f, :], tmp[:, 0, :], tmp[:, 1, :], ALU.subtract))
                    chain.link(nc.vector.tensor_tensor(tmp[:, 0, :], k.bank(b), im, ALU.mult))
                    chain.link(nc.vector.tensor_tensor(tmp[:, 1, :], k.bank(b + 1), re, ALU.mult))
                    take(nc.vector.tensor_tensor(yspec[:, 4 + f, :], tmp[:, 0, :], tmp[:, 1, :], ALU.add))
                    dve.wait_ge(kept, group + 1)
                    group += 1
                for c in range(HYT):
                    dve.wait_ge(done, group + 1)
                    g, x0 = u[:, 4 + c, off:off + L], u[:, c, off:off + L]
                    chain.link(nc.vector.scalar_tensor_tensor(out=g, in0=g, scalar=k.col("hy_bias", c),
                                                              in1=k.bank(2 * (group % 4), L), op0=ALU.mult, op1=ALU.add))
                    take(nc.vector.tensor_tensor(x0, g, x0, ALU.mult))
                    group += 1



def project_act(k, weights, dst, func, bias, segs, kt=DT, x=None, par=2):
    nc = k.nc
    k.stage()
    x = k.h if x is None else x
    stream = Stream(k, weights, ring_slots(k, par, kt * P))
    turns = stream.tiles // par
    t0 = segs[0][0]
    product, taken = ([k.sem(f"{s}{p}") for p in range(par)] for s in ("product", "taken"))
    with k.block() as block:
        @block.sync
        def _(sp):
            stream.load(sp, product)

        @block.tensor
        def _(pe):
            with pe.Fori(0, turns) as i:
                for p in range(par):
                    pe.wait_ge(stream.landed[p], 16 * i + 16)
                    pe.wait_ge(taken[p], i + 1)
                    project(k, pe, stream.slots[p], kt, lambda kk: x[:, kk, :],
                            lambda s: k.pair(p)[:, segs[s][0]:segs[s][0] + segs[s][1]], segs).then_inc(product[p], 1)

        @block.scalar
        def _(act):
            free_all(act, taken)
            with act.Fori(0, turns) as i:
                for p in range(par):
                    n = i * par + p
                    act.wait_ge(product[p], i + 1)
                    nc.scalar.activation(dst[:, n, :], k.pair(p)[:, t0:T], func,
                                         bias=k.col(bias, n) if bias else 0.0).then_inc(taken[p], 1)


def project_tokens(k, weights, dst, kt, x_of, token_tiles, width, at=0):
    nc = k.nc
    k.stage()
    slot = k.ring[:, at:at + kt * width]
    landed, product, taken = k.sem("landed"), k.sem("product"), k.sem("taken")
    with k.block() as block:
        @block.sync
        def _(sp):
            sp.dma_start(slot, k.dram[weights]).then_inc(landed, 16)

        @block.tensor
        def _(pe):
            pe.wait_ge(landed, 16)
            for j, a in enumerate(token_tiles):
                if j >= 4:
                    pe.wait_ge(taken, j - 3)
                for kk in range(kt):
                    last = nc.tensor.matmul(k.bank(j % 4, width), x_of(kk)[:, a * P:(a + 1) * P],
                                            slot[:, kk * width:(kk + 1) * width], start=kk == 0, stop=kk == kt - 1)
                last.then_inc(product, 1)

        @block.vector
        def _(dve):
            for j in range(len(token_tiles)):
                dve.wait_ge(product, j + 1)
                nc.vector.tensor_copy(dst[:, j, :], k.bank(j % 4, width)).then_inc(taken, 1)


def log1p_series(k, chain, e, inv, sq, acc):
    nc = k.nc
    chain.link(nc.vector.tensor_scalar(inv, e, 2.0, None, ALU.add))
    chain.link(nc.vector.reciprocal(inv, inv))
    chain.link(nc.vector.tensor_tensor(e, e, inv, ALU.mult))
    chain.link(nc.vector.tensor_tensor(sq, e, e, ALU.mult))
    chain.link(nc.vector.tensor_scalar(acc, sq, 1.0 / ATANH_TERMS[0], None, ALU.mult))
    for n in ATANH_TERMS[1:]:
        chain.link(nc.vector.scalar_tensor_tensor(out=acc, in0=acc, scalar=1.0 / n, in1=sq, op0=ALU.add, op1=ALU.mult))
    chain.link(nc.vector.scalar_tensor_tensor(out=acc, in0=acc, scalar=1.0, in1=e, op0=ALU.add, op1=ALU.mult))


def mlstm_gates(k, c_rows, neg_m, floor):
    nc = k.nc
    k.stage()
    raw, e, inv, sq, acc, gate_in, logf, cum = (k.arena[:, 18432 + j * T:18432 + (j + 1) * T] for j in range(8))
    w = k.ring[:, 0:DT * 16]
    landed, product, raw_ready, exp_ready, logs, cleared, moved, summed, absolute = (
        k.sem(s) for s in ("landed", "product", "raw", "exp", "logs", "cleared", "moved", "summed", "absolute"))
    one = k.const("ones", 1)
    with k.block() as block:
        @block.sync
        def _(sp):
            sp.dma_start(w, k.dram["w_in_gates"]).then_inc(landed, 16)
            sp.wait_ge(cleared, 1)
            sp.wait_ge(logs, 1)
            for d, row in ((0, 0), (1, BWD)):
                sp.dma_start(gate_in[row:row + ML_HEADS, :], raw[8 * d:8 * d + ML_HEADS, :]).then_inc(moved, 16)
                sp.dma_start(logf[row:row + ML_HEADS, :], acc[8 * d + 4:8 * d + 4 + ML_HEADS, :]).then_inc(moved, 16)

        @block.tensor
        def _(pe):
            pe.wait_ge(landed, 16)
            project(k, pe, w, DT, lambda kk: k.h[:, kk, :], lambda s: seg_out(k, 0)(s)[0:16, :], SEGS, m=16,
                    width=16).then_inc(product, 1)

        @block.scalar
        def _(act):
            act.wait_ge(raw_ready, 1)
            nc.scalar.activation(e[0:16, :], raw[0:16, :], ACT.Abs).then_inc(absolute, 1)
            act.wait_ge(absolute, 1)
            nc.scalar.activation(e[0:16, :], e[0:16, :], ACT.Exp, scale=-1.0).then_inc(exp_ready, 1)
            act.wait_ge(summed, 1)
            nc.scalar.activation(floor, sq[0:ROWS, :], ACT.Exp, scale=-1.0)

        @block.vector
        def _(dve):
            chain = Chain(dve, k.sem("chain"))
            nc.vector.memset(gate_in[0:ROWS, :], 0.0)
            nc.vector.memset(cum[0:ROWS, :], 0.0)
            nc.vector.memset(logf[0:ROWS, :], 0.0).then_inc(cleared, 1)
            dve.wait_ge(product, 1)
            nc.vector.tensor_scalar(raw[0:16, :], k.pair(0)[0:16, :], k.vec[0:16, COL["ml_gate_b"]:COL["ml_gate_b"] + 1],
                                    None, ALU.add).then_inc(raw_ready, 1)
            dve.wait_ge(exp_ready, 1)
            log1p_series(k, chain, e[0:16, :], inv[0:16, :], sq[0:16, :], acc[0:16, :])
            chain.link(nc.vector.tensor_scalar(inv[0:16, :], raw[0:16, :], 0.0, None, ALU.min))
            nc.vector.scalar_tensor_tensor(out=acc[0:16, :], in0=acc[0:16, :], scalar=-2.0, in1=inv[0:16, :],
                                           op0=ALU.mult, op1=ALU.add).then_inc(logs, 1)
            dve.wait_ge(moved, 64)
            fwd, bwd = slice(0, ML_HEADS), slice(BWD, BWD + ML_HEADS)
            runs = ((fwd, slice(0, T), None), (bwd, slice(CTX - 1, None, -1), None), (bwd, slice(T - 1, CTX - 1, -1), 0))

            def scan(out, data, op):
                for rows, span, start in runs:
                    n = CTX if span.start == CTX - 1 else (LAT if start is not None else T)
                    chain.link(nc.vector.tensor_tensor_scan(
                        out[rows, span], k.cst[rows, CAT["ones"]:CAT["ones"] + 1].to_broadcast([ML_HEADS, n]), data[rows, span],
                        0.0 if start is None else out[rows, start:start + 1], ALU.mult, op))

            scan(cum, logf, ALU.add)
            chain.link(nc.vector.tensor_tensor(c_rows, gate_in[0:ROWS, :], cum[0:ROWS, :], ALU.subtract))
            chain.link(nc.vector.memset(e[0:ROWS, :], 0.0))
            scan(e, c_rows, ALU.max)
            chain.link(nc.vector.tensor_tensor(sq[0:ROWS, :], e[0:ROWS, :], cum[0:ROWS, :], ALU.add))
            nc.vector.tensor_scalar(neg_m, e[0:ROWS, :], -1.0, None, ALU.mult).then_inc(summed, 1)


def mlstm(k):
    q, kk_, v, og = k.area(8 * T, 4, T), k.area(12 * T, 4, T), k.area(16 * T, 6, ML_W), k.area(20 * T, 4, T)
    slots = [k.arena[:, 18432 + j * T:18432 + (j + 1) * T] for j in range(8)]
    c_rows, neg_m, floor = slots[1 + 4][0:ROWS, :], slots[2][0:ROWS, :], k.row[0:ROWS, :]
    c_rows = k.ring[0:ROWS, 12288 - T:12288]
    mlstm_gates(k, c_rows, neg_m, floor)
    project_conv(k, "w_in_qk", k.area(8 * T, 8, T), "ml_conv_w", None, True)
    project_act(k, "w_in_og", og, ACT.Sigmoid, None, SEGS)
    project_tokens(k, "w_in_v", v, DT, lambda n: k.h[:, n, :], range(6), ML_W)
    mlstm_core(k, q, kk_, v, og, c_rows, neg_m, floor, slots)


def mlstm_core(k, q, key, v, og, c_rows, neg_m, floor, slots):
    nc = k.nc
    k.stage()
    flat = k.h.rearrange("p k t -> p (k t)")
    c_col = flat[:, 0:6 * ROWS].rearrange("p (a r) -> p a r", r=ROWS)
    scores = flat[:, T:T + 6 * T].rearrange("p (j t) -> p j t", t=T)
    weights, probs = (slots[3], slots[4]), (slots[5], slots[6])
    bcast = k.ring[:, 0:8 * T].rearrange("p (r t) -> p r t", t=T)
    num = k.ring[:, 8 * T:16 * T].rearrange("p (r t) -> p r t", t=T)
    recip, sq_rows = slots[7][0:ROWS, :], slots[2][0:ROWS, :]
    squares = (slots[3], slots[4])
    scale = float(P) ** -0.5

    def select(row):
        return k.cst[0:ROWS, CAT["ident"] + row:CAT["ident"] + row + 1].to_broadcast([ROWS, P])

    def one_row(row):
        return k.const("onecol", ROWS, ROWS - 1 - row)

    rows = [(d, h, d * BWD + h) for d in range(2) for h in range(ML_HEADS)]
    units = []
    for h in range(ML_HEADS):
        for j in range(6):
            units.append((h, 0, j, ((j * P, T),), ((j + 1) * P, T)))
        for j in (1, 0, 5, 4, 3, 2):
            if j < 2:
                spans = ((0, (j + 1) * P), (CTX, T)) if j == 0 else ((0, T),)
                units.append((h, 1, j, spans, (0, j * P), (CTX, T)))
            else:
                units.append((h, 1, j, ((CTX, (j + 1) * P),), (CTX, j * P)))

    names = ("c_turned", "c_kept", "row_out", "row_kept", "s_done", "s_kept", "diag", "weighed", "prob", "pv",
             "num_kept", "recip_ready", "norm_out", "norm_taken", "squared", "sum_done", "root", "inverse")
    (c_turned, c_kept, row_out, row_kept, s_done, s_kept, diag, weighed, prob, pv, num_kept, recip_ready, norm_out,
     norm_taken, squared, sum_done, root, inverse) = (k.sem(s) for s in names)

    def pieces(spans):
        out = []
        for a, b in spans:
            for s0, n in SEGS:
                lo, hi = max(a, s0), min(b, s0 + n)
                if lo < hi:
                    out.append((lo, hi))
        return out

    with k.block() as block:
        @block.tensor
        def _(pe):
            for a in range(6):
                last = nc.tensor.transpose(k.bank(0, ROWS, a * ROWS), c_rows[:, a * P:(a + 1) * P],
                                           k.cst[0:ROWS, CAT["ident"]:CAT["ident"] + ROWS])
            last.then_inc(c_turned, 1)
            for n, (d, h, row) in enumerate(rows):
                if n >= 3:
                    pe.wait_ge(row_kept, n - 2)
                for a, w in SEGS:
                    last = nc.tensor.matmul(k.pair(1 + n % 3)[:, a:a + w], select(row), neg_m[:, a:a + w],
                                            start=True, stop=True)
                last.then_inc(row_out, 1)
            pe.wait_ge(row_kept, len(rows))
            pe.wait_ge(c_kept, 1)
            for u, (h, d, j, spans, *off) in enumerate(units):
                if u % 12 == 0:
                    for jj in range(6):
                        m = 6 * h + jj
                        if m >= 2:
                            pe.wait_ge(s_kept, m - 1)
                        for a, b in pieces(((0, T),) if jj < 2 else ((CTX, T),)):
                            last = nc.tensor.matmul(k.pair(m % 2)[:, a:b], key[:, h, jj * P:(jj + 1) * P], q[:, h, a:b],
                                                    start=True, stop=True)
                        last.then_inc(s_done, 1)
                first = u % 6 == 0
                if first and u:
                    pe.wait_ge(num_kept, u // 6)
                pe.wait_ge(prob, u + 1)
                for a, b in pieces(spans):
                    nc.tensor.matmul(k.pair(2)[:, a:b], v[:, j, h * P:(h + 1) * P], probs[u % 2][:, a:b],
                                     start=first, stop=u % 6 == 5, skip_group_check=True)
                    last = nc.tensor.matmul(k.pair(3)[0:ROWS, a:b], one_row(d * BWD + h), probs[u % 2][:, a:b],
                                            start=u == 0, stop=u == len(units) - 1, skip_group_check=True)
                last.then_inc(pv, 1)
            pe.wait_ge(recip_ready, 1)
            for n in range(8):
                h, d = n // 2, n % 2
                if n >= 2:
                    pe.wait_ge(norm_taken, n - 1)
                for a, w in SEGS:
                    last = nc.tensor.matmul(k.pair(n % 2)[:, a:a + w], select(d * BWD + h), recip[:, a:a + w],
                                            start=True, stop=True)
                last.then_inc(norm_out, 1)
            for h in range(ML_HEADS):
                pe.wait_ge(squared, h + 1)
                for a, w in SEGS:
                    last = nc.tensor.matmul(k.pair(2)[0:ROWS, a:a + w], one_row(h), squares[h % 2][:, a:a + w],
                                            start=h == 0, stop=h == ML_HEADS - 1)
                last.then_inc(sum_done, 1)
            pe.wait_ge(inverse, 1)
            for h in range(ML_HEADS):
                n = 8 + h
                pe.wait_ge(norm_taken, n - 1)
                for a, w in SEGS:
                    last = nc.tensor.matmul(k.pair(n % 2)[:, a:a + w], select(h), sq_rows[:, a:a + w],
                                            start=True, stop=True)
                last.then_inc(norm_out, 1)

        @block.scalar
        def _(act):
            for n in range(len(rows)):
                act.wait_ge(row_out, n + 1)
                nc.scalar.copy(bcast[:, n, :], k.pair(1 + n % 3)).then_inc(row_kept, 1)
            act.wait_ge(row_kept, len(rows))
            for u, (h, d, j, spans, *off) in enumerate(units):
                if u % 12 == 0:
                    if u:
                        act.wait_ge(prob, u)
                    for jj in range(6):
                        m = 6 * h + jj
                        act.wait_ge(s_done, m + 1)
                        a = 0 if jj < 2 else CTX
                        nc.scalar.mul(scores[:, jj, a:T], k.pair(m % 2)[:, a:T], scale).then_inc(s_kept, 1)
                act.wait_ge(diag, u + 1)
                w = weights[u % 2]
                last = nc.scalar.activation(w[:, j * P:(j + 1) * P], w[:, j * P:(j + 1) * P], ACT.Exp)
                for a, b in off:
                    if a < b:
                        last = nc.scalar.activation(w[:, a:b], bcast[:, 4 * d + h, a:b], ACT.Exp,
                                                    bias=c_col[:, j, d * BWD + h:d * BWD + h + 1])
                last.then_inc(weighed, 1)
            for h in range(ML_HEADS):
                act.wait_ge(norm_taken, 2 * h + 2)
                if h >= 2:
                    act.wait_ge(sum_done, h - 1)
                nc.scalar.activation(squares[h % 2], num[:, h, :], ACT.Square).then_inc(squared, 1)
            act.wait_ge(sum_done, ML_HEADS)
            nc.scalar.activation(sq_rows, k.pair(2)[0:ROWS, :], ACT.Sqrt, scale=1.0 / P,
                                 bias=k.cst[0:ROWS, CAT["eps"]:CAT["eps"] + 1]).then_inc(root, 1)

        @block.vector
        def _(dve):
            chain = Chain(dve, k.sem("chain"))
            dve.wait_ge(c_turned, 1)
            nc.vector.tensor_copy(c_col, k.bank(0, 6 * ROWS).rearrange("p (a r) -> p a r", r=ROWS)).then_inc(c_kept, 1)
            dve.wait_ge(c_kept, 1)
            dve.wait_ge(row_kept, len(rows))

            def diagonal(u):
                h, d, j = units[u][:3]
                span = slice(j * P, (j + 1) * P)
                nc.vector.tensor_scalar(weights[u % 2][:, span], bcast[:, 4 * d + h, span],
                                        c_col[:, j, d * BWD + h:d * BWD + h + 1], 0.0, ALU.add, ALU.min).then_inc(diag, 1)

            diagonal(0)
            for u, (h, d, j, spans, *off) in enumerate(units):
                if u + 1 < len(units):
                    diagonal(u + 1)
                dve.wait_ge(weighed, u + 1)
                dve.wait_ge(s_kept, 6 * h + 6)
                if u >= 2:
                    dve.wait_ge(pv, u - 1)
                for a, b in spans:
                    chain.link(nc.vector.tensor_tensor(probs[u % 2][:, a:b], scores[:, j, a:b], weights[u % 2][:, a:b],
                                                       ALU.mult))
                span = slice(j * P, (j + 1) * P)
                nc.vector.tensor_tensor(probs[u % 2][:, span], probs[u % 2][:, span],
                                        k.const("s_ge_t" if d else "s_le_t"), ALU.mult).then_inc(prob, 1)
                if u % 6 == 5:
                    dve.wait_ge(pv, u + 1)
                    nc.vector.tensor_copy(num[:, 4 * d + h, :], k.pair(2)).then_inc(num_kept, 1)
            chain.link(nc.vector.tensor_copy(recip, k.pair(3)[0:ROWS, :]))
            chain.link(nc.vector.scalar_tensor_tensor(out=recip, in0=recip, scalar=-1.0, in1=recip, op0=ALU.mult,
                                                      op1=ALU.max))
            chain.link(nc.vector.tensor_tensor(recip, recip, floor, ALU.max))
            nc.vector.reciprocal(recip, recip).then_inc(recip_ready, 1)
            dve.wait_ge(num_kept, 8)
            for n in range(8):
                h, d = n // 2, n % 2
                dve.wait_ge(norm_out, n + 1)
                part = num[:, 4 * d + h, :]
                if d == 0:
                    nc.vector.tensor_tensor(part, part, k.pair(n % 2), ALU.mult).then_inc(norm_taken, 1)
                else:
                    chain.link(nc.vector.tensor_tensor(part, part, k.pair(n % 2), ALU.mult))
                    dve.wait_ge(norm_taken, n)
                    nc.vector.tensor_tensor(num[:, h, :], num[:, h, :], part, ALU.add).then_inc(norm_taken, 1)
            dve.wait_ge(root, 1)
            nc.vector.reciprocal(sq_rows, sq_rows).then_inc(inverse, 1)
            for h in range(ML_HEADS):
                n = 8 + h
                dve.wait_ge(norm_out, n + 1)
                chain.link(nc.vector.scalar_tensor_tensor(out=num[:, h, :], in0=num[:, h, :], scalar=k.col("ml_norm_g", h),
                                                          in1=k.pair(n % 2), op0=ALU.mult, op1=ALU.mult))
                nc.vector.tensor_tensor(k.arena[:, (4 + h) * T:(5 + h) * T], num[:, h, :], og[:, h, :],
                                        ALU.mult).then_inc(norm_taken, 1)



def rotate(k, parts, cos, sin, scratch):
    nc = k.nc
    k.stage()
    partner, summed = k.sem("partner"), k.sem("summed")
    with k.block() as block:
        @block.tensor
        def _(pe):
            for n, x in enumerate(parts):
                if n >= 4:
                    pe.wait_ge(summed, n - 3)
                nc.tensor.matmul(k.bank(n % 4), k.const("rot_gqa"), x, start=True, stop=True).then_inc(partner, 1)

        @block.vector
        def _(dve):
            chain = Chain(dve, k.sem("chain"))
            for n, x in enumerate(parts):
                dve.wait_ge(partner, n + 1)
                chain.link(nc.vector.tensor_tensor(scratch, k.bank(n % 4), sin, ALU.mult))
                chain.link(nc.vector.tensor_tensor(x, x, cos, ALU.mult))
                nc.vector.tensor_tensor(x, x, scratch, ALU.add).then_inc(summed, 1)
                dve.wait_ge(summed, n + 1)


def attention(k, heads, key_segs, scores_of, value_of, out_rows, dst_of, scale):
    nc = k.nc
    k.stage()
    lo = key_segs[0][0]
    width = T - lo
    tiles = width // P
    probs = [k.ring[:, b * T:b * T + width] for b in range(2)]
    turned = [k.ring[:, 2 * T + b * tiles * LAT:2 * T + (b + 1) * tiles * LAT].rearrange("p (a t) -> p a t", t=LAT)
              for b in range(2)]
    stats = k.row[:, 0:32].rearrange("p (b c) -> p b c", c=4)
    units = [(h, a) for h in range(heads) for a in range(4)]
    names = ("scored", "peak", "raised", "normed", "t_done", "t_kept", "o_done", "o_kept")
    scored, peak, raised, normed, t_done, t_kept, o_done, o_kept = (k.sem(s) for s in names)
    with k.block() as block:
        @block.tensor
        def _(pe):
            def score(u):
                if u >= 2:
                    pe.wait_ge(raised, u - 1)
                terms = scores_of(*units[u])
                for t0, n in key_segs:
                    for m, (queries, keys) in enumerate(terms):
                        last = nc.tensor.matmul(k.pair(u % 2)[:, t0:t0 + n], queries, keys[:, t0:t0 + n], start=m == 0,
                                                stop=m == len(terms) - 1)
                last.then_inc(scored, 1)

            score(0)
            for u, (h, a) in enumerate(units):
                if u + 1 < len(units):
                    score(u + 1)
                pe.wait_ge(normed, u + 1)
                if u:
                    pe.wait_ge(t_kept, u)
                for b in range(tiles):
                    last = nc.tensor.transpose(k.pair(2)[:, lo + b * P:lo + (b + 1) * P], probs[u % 2][:, b * P:(b + 1) * P],
                                               k.const("ident"))
                last.then_inc(t_done, 1)
                if a == 3:
                    pe.wait_ge(t_kept, u + 1)
                    if h >= 2:
                        pe.wait_ge(o_kept, h - 1)
                    for b in range(tiles):
                        last = nc.tensor.matmul(k.bank(6 + h % 2)[out_rows(h), :], value_of(h, b), turned[h % 2][:, b, :],
                                                start=b == 0, stop=b == tiles - 1)
                    last.then_inc(o_done, 1)

        @block.vector
        def _(dve):
            chain = Chain(dve, k.sem("chain"))

            def find_peak(u):
                dve.wait_ge(scored, u + 1)
                b = u % 8
                chain.link(nc.vector.tensor_reduce(stats[:, b, 0:1], k.pair(u % 2)[:, lo:T], AX.X, ALU.max))
                nc.vector.tensor_scalar(stats[:, b, 1:2], stats[:, b, 0:1], -scale, None, ALU.mult).then_inc(peak, 1)

            find_peak(0)
            for u in range(len(units)):
                if u + 1 < len(units):
                    find_peak(u + 1)
                dve.wait_ge(raised, u + 1)
                b = u % 8
                chain.link(nc.vector.reciprocal(stats[:, b, 3:4], stats[:, b, 2:3]))
                nc.vector.tensor_scalar(probs[u % 2], probs[u % 2], stats[:, b, 3:4], None, ALU.mult).then_inc(normed, 1)

        @block.scalar
        def _(act):
            def raise_(u):
                act.wait_ge(peak, u + 1)
                if u >= 2:
                    act.wait_ge(t_done, u - 1)
                nc.scalar.activation(probs[u % 2], k.pair(u % 2)[:, lo:T], ACT.Exp, scale=scale,
                                     bias=stats[:, u % 8, 1:2], accum_out=stats[:, u % 8, 2:3]).then_inc(raised, 1)

            raise_(0)
            for u, (h, a) in enumerate(units):
                if u + 1 < len(units):
                    raise_(u + 1)
                act.wait_ge(t_done, u + 1)
                if h >= 2:
                    act.wait_ge(o_done, h - 1)
                nc.scalar.copy(turned[h % 2][:, :, a * P:(a + 1) * P],
                               k.pair(2)[:, lo:T].rearrange("p (b q) -> p b q", q=P)).then_inc(t_kept, 1)
                if a == 3:
                    act.wait_ge(o_done, h + 1)
                    nc.scalar.copy(dst_of(h), k.bank(6 + h % 2)[out_rows(h), :]).then_inc(o_kept, 1)


def load(k, pairs):
    nc = k.nc
    k.stage()
    landed = k.sem("landed")
    with k.block() as block:
        @block.sync
        def _(sp):
            for dst, name in pairs:
                sp.dma_start(dst, k.dram[name]).then_inc(landed, 16)
            sp.wait_ge(landed, 16 * len(pairs))


def mla(k):
    qa, kva = k.area(0, 3, T), k.area(3 * T, 3, T)
    qn, kn = k.area(6 * T, 8, LAT), k.area(6 * T + 4096, 8, T)
    v = k.area(6 * T + 4096 + 8 * T, 6, D)
    at = 6 * T + 4096 + 14 * T + 6 * (D - T)
    qr = k.area(at, 4, LAT)
    cos, sin, scratch = (k.arena[:, at + 2048 + j * LAT:at + 2048 + (j + 1) * LAT] for j in range(3))
    load(k, ((cos, "rope_cos"), (sin, "rope_sin")))
    project_act(k, "mla_w_qa", qa[:, :, CTX:T], ACT.Identity, None, SEG_LAT, par=3)
    project_act(k, "mla_w_kva", kva, ACT.Identity, None, SEGS, par=3)
    normalise(k, lambda n, c: k.col("mla_q_norm", n), None, SEG_LAT, qa, qa, kt=3, root_of=Q_RANK)
    normalise(k, lambda n, c: k.col("mla_kv_norm", n), None, SEGS, kva, kva, kt=2, root_of=KV_RANK)
    project_act(k, "mla_w_qn", qn, ACT.Identity, None, SEG_LAT, kt=3, x=qa)
    project_act(k, "mla_w_qr", qr, ACT.Identity, None, SEG_LAT, kt=3, x=qa)
    project_act(k, "mla_w_kn", kn, ACT.Identity, None, SEGS, kt=2, x=kva)
    for half in range(2):
        project_tokens(k, f"mla_w_v{half}", v[:, :, half * 512:(half + 1) * 512], 2, lambda n: kva[:, n, :], range(6), 512)
    rotate(k, [qr[:, n, :] for n in range(4)] + [kva[:, 2, CTX:T]], cos, sin, scratch)

    def scores_of(h, a):
        half = slice(64 * (h % 2), 64 * (h % 2) + 64)
        return ((qn[:, h, a * P:(a + 1) * P], kn[:, h, :]), (qr[half, h // 2, a * P:(a + 1) * P], kva[half, 2, :]))

    attention(k, MLA_HEADS, SEGS, scores_of, lambda h, b: v[:, b, h * P:(h + 1) * P], lambda h: slice(0, P),
              lambda h: k.h[:, h, CTX:T], MLA_SCALE)
    project_residual(k, "mla_w_o", DT, lambda n: k.h[:, n, :], 2, SEG_LAT, k.mod_next)



def normalise_heads(k, x, gain_col, squares, roots):
    nc = k.nc
    k.stage()
    n_tiles = x.shape[1]
    squared, summed, root, inverse, normed = (k.sem(s) for s in ("squared", "summed", "root", "inverse", "normed"))
    with k.block() as block:
        @block.tensor
        def _(pe):
            for n in range(n_tiles):
                pe.wait_ge(squared, n + 1)
                nc.tensor.matmul(k.bank(n), k.const("ones64"), squares[n % 2], start=True, stop=True).then_inc(summed, 1)

        @block.scalar
        def _(act):
            for n in range(n_tiles):
                if n >= 2:
                    act.wait_ge(summed, n - 1)
                nc.scalar.activation(squares[n % 2], x[:, n, :], ACT.Square).then_inc(squared, 1)
            for n in range(n_tiles):
                act.wait_ge(summed, n + 1)
                if n >= 2:
                    act.wait_ge(normed, n - 1)
                nc.scalar.activation(roots[n % 2], k.bank(n), ACT.Sqrt, scale=1.0 / 64, bias=k.const("eps")).then_inc(root, 1)

        @block.vector
        def _(dve):
            for n in range(n_tiles):
                dve.wait_ge(root, n + 1)
                nc.vector.reciprocal(roots[n % 2], roots[n % 2]).then_inc(inverse, 1)
                dve.wait_ge(inverse, n + 1)
                nc.vector.scalar_tensor_tensor(out=x[:, n, :], in0=x[:, n, :], scalar=gain_col(n), in1=roots[n % 2],
                                               op0=ALU.mult, op1=ALU.mult).then_inc(normed, 1)


def ssd_rows(k, sums, step, decay):
    nc = k.nc
    k.stage()
    raw, e, inv, sq, acc = (k.ring[:, 2048 + j * LAT:2048 + (j + 1) * LAT] for j in range(5))
    w = k.ring[:, 0:DT * 16]
    r16 = slice(0, 16)
    cols = k.vec[r16, COL["ssd_rows"]:COL["ssd_rows"] + 2]
    names = ("landed", "product", "raw_ready", "absolute", "exp_ready", "rates", "steps", "cleared", "moved", "negated")
    landed, product, raw_ready, absolute, exp_ready, rates, steps, cleared, moved, negated = (k.sem(s) for s in names)
    with k.block() as block:
        @block.sync
        def _(sp):
            sp.dma_start(w, k.dram["w_in_dt"]).then_inc(landed, 16)
            sp.wait_ge(cleared, 1)
            sp.wait_ge(steps, 2)
            for d, row in ((0, 0), (1, BWD)):
                sp.dma_start(step[row:row + SSD_HEADS, :], acc[8 * d:8 * d + 8, :]).then_inc(moved, 16)
                sp.dma_start(decay[row:row + SSD_HEADS, :], sq[8 * d:8 * d + 8, :]).then_inc(moved, 16)

        @block.tensor
        def _(pe):
            pe.wait_ge(landed, 16)
            project(k, pe, w, DT, lambda n: k.h[:, n, :], lambda s: k.bank(0)[r16, :], SEG_LAT, m=16,
                    width=16).then_inc(product, 1)

        @block.scalar
        def _(act):
            act.wait_ge(raw_ready, 1)
            nc.scalar.activation(e[r16, :], raw[r16, :], ACT.Abs).then_inc(absolute, 1)
            act.wait_ge(absolute, 1)
            nc.scalar.activation(e[r16, :], e[r16, :], ACT.Exp, scale=-1.0).then_inc(exp_ready, 1)
            nc.scalar.activation(k.row[r16, 0:1], cols[:, 1:2], ACT.Exp).then_inc(rates, 1)

        @block.vector
        def _(dve):
            chain = Chain(dve, k.sem("chain"))
            for j in range(4):
                chain.link(nc.vector.memset(sums[j], 0.0))
            chain.link(nc.vector.memset(step, 0.0))
            nc.vector.memset(decay, 0.0).then_inc(cleared, 1)
            dve.wait_ge(product, 1)
            nc.vector.tensor_scalar(raw[r16, :], k.bank(0)[r16, :], cols[:, 0:1], None, ALU.add).then_inc(raw_ready, 1)
            dve.wait_ge(exp_ready, 1)
            log1p_series(k, chain, e[r16, :], inv[r16, :], sq[r16, :], acc[r16, :])
            chain.link(nc.vector.tensor_scalar(inv[r16, :], raw[r16, :], 0.0, None, ALU.max))
            nc.vector.scalar_tensor_tensor(out=acc[r16, :], in0=acc[r16, :], scalar=2.0, in1=inv[r16, :], op0=ALU.mult,
                                           op1=ALU.add).then_inc(steps, 1)
            dve.wait_ge(steps, 1)
            dve.wait_ge(rates, 1)
            nc.vector.tensor_scalar(sq[r16, :], acc[r16, :], k.row[r16, 0:1], -1.0, ALU.mult, ALU.mult).then_inc(steps, 1)
            dve.wait_ge(moved, 64)
            for j in range(4):
                for row, span, n in ((0, slice(j * P, LAT), LAT - j * P),
                                     (BWD, slice((j + 1) * P - 1, None, -1), (j + 1) * P)):
                    rows = slice(row, row + SSD_HEADS)
                    chain.link(nc.vector.tensor_tensor_scan(
                        sums[j][rows, span], k.cst[rows, CAT["ones"]:CAT["ones"] + 1].to_broadcast([SSD_HEADS, n]),
                        decay[rows, span], 0.0, ALU.mult, ALU.add))


def ssd_core(k, xbc, xs, sums, step, work, y):
    nc = k.nc
    k.stage()
    cb = k.ring[:, 0:8 * LAT].rearrange("p (u t) -> p u t", t=LAT)
    weights = [k.ring[:, (8 + b) * LAT:(9 + b) * LAT] for b in range(2)]
    probs = [k.ring[:, (10 + b) * LAT:(11 + b) * LAT] for b in range(2)]
    back = [k.ring[:, 12 * LAT + b * P:12 * LAT + (b + 1) * P] for b in range(2)]
    neg = k.ring[:, 12 * LAT + 256:12 * LAT + 512].rearrange("p (j r) -> p j r", r=ROWS)
    dt = k.ring[:, 12 * LAT + 512:12 * LAT + 768].rearrange("p (j r) -> p j r", r=ROWS)

    def select(row):
        return k.cst[0:ROWS, CAT["ident"] + row:CAT["ident"] + row + 1].to_broadcast([ROWS, P])

    units = [(h, j) for h in range(SSD_HEADS) for j in range(4)]
    names = ("prep", "prep_kept", "spread", "diag", "weighed", "prob", "pv", "y_kept")
    prep, prep_kept, spread, diag, weighed, prob, pv, y_kept = (k.sem(s) for s in names)
    n_prep = 4 + 2 + 8
    with k.block() as block:
        @block.tensor
        def _(pe):
            g = 0

            def begin():
                if g >= 4:
                    pe.wait_ge(prep_kept, g - 3)
                return k.bank(g % 4)
            for a in range(4):
                b = begin()
                for c in range(4):
                    last = nc.tensor.transpose(b[:, c * P:(c + 1) * P], xbc[:, c, a * P:(a + 1) * P], k.const("ident"))
                last.then_inc(prep, 1)
                g += 1
            ident64 = k.cst[0:ROWS, CAT["ident"]:CAT["ident"] + ROWS]
            for src in (lambda j: sums[j], lambda j: step):
                b = begin()
                for j in range(4):
                    last = nc.tensor.transpose(b[:, j * ROWS:(j + 1) * ROWS], src(j)[:, j * P:(j + 1) * P], ident64)
                last.then_inc(prep, 1)
                g += 1
            for grp in range(2):
                rows = slice(64 * grp, 64 * grp + 64)
                for j in range(4):
                    b = begin()
                    nc.tensor.matmul(b, xbc[rows, 4, j * P:(j + 1) * P], xbc[rows, 5, :], start=True,
                                     stop=True).then_inc(prep, 1)
                    g += 1
            pe.wait_ge(prep_kept, n_prep)

            def spread_rows(u):
                h, j = units[u]
                if u >= 2:
                    pe.wait_ge(weighed, u - 1)
                a, b = k.bank(2 * (u % 2)), k.bank(2 * (u % 2) + 1)
                if j:
                    nc.tensor.matmul(a[:, 0:j * P], select(BWD + h), sums[j][:, 0:j * P], start=True, stop=True)
                nc.tensor.matmul(a[:, j * P:LAT], select(h), sums[j][:, j * P:LAT], start=True, stop=True)
                nc.tensor.matmul(b[:, 0:P], select(BWD + h), sums[j][:, j * P:(j + 1) * P], start=True,
                                 stop=True).then_inc(spread, 1)

            spread_rows(0)
            for u, (h, j) in enumerate(units):
                if u + 1 < len(units):
                    spread_rows(u + 1)
                pe.wait_ge(prob, u + 1)
                if j == 0 and h >= 4:
                    pe.wait_ge(y_kept, h - 3)
                rows = slice(64 * (h % 2), 64 * (h % 2) + 64)
                nc.tensor.matmul(k.bank(4 + h % 4)[rows, :], xs[:, j, h * 64:(h + 1) * 64], probs[u % 2], start=j == 0,
                                 stop=j == 3).then_inc(pv, 1)

        @block.scalar
        def _(act):
            act.wait_ge(prep_kept, n_prep)
            for u, (h, j) in enumerate(units):
                act.wait_ge(diag, u + 1)
                w, a = weights[u % 2], k.bank(2 * (u % 2))
                nc.scalar.activation(back[u % 2], back[u % 2], ACT.Exp)
                last = nc.scalar.activation(w[:, j * P:(j + 1) * P], w[:, j * P:(j + 1) * P], ACT.Exp)
                if j:
                    last = nc.scalar.activation(w[:, 0:j * P], a[:, 0:j * P], ACT.Exp,
                                                bias=neg[:, j, BWD + h:BWD + h + 1])
                if j < 3:
                    last = nc.scalar.activation(w[:, (j + 1) * P:LAT], a[:, (j + 1) * P:LAT], ACT.Exp,
                                                bias=neg[:, j, h:h + 1])
                last.then_inc(weighed, 1)

        @block.vector
        def _(dve):
            chain = Chain(dve, k.sem("chain"))
            g = 0
            for a in range(4):
                dve.wait_ge(prep, g + 1)
                nc.vector.tensor_copy(xs[:, a, :], k.bank(g % 4)).then_inc(prep_kept, 1)
                g += 1
            dve.wait_ge(prep, g + 1)
            nc.vector.tensor_scalar(neg, k.bank(g % 4, 4 * ROWS).rearrange("p (j r) -> p j r", r=ROWS), -1.0, None,
                                    ALU.mult).then_inc(prep_kept, 1)
            g += 1
            dve.wait_ge(prep, g + 1)
            nc.vector.tensor_copy(dt, k.bank(g % 4, 4 * ROWS).rearrange("p (j r) -> p j r", r=ROWS)).then_inc(prep_kept, 1)
            g += 1
            for n in range(8):
                dve.wait_ge(prep, g + 1)
                nc.vector.tensor_copy(cb[:, n, :], k.bank(g % 4)).then_inc(prep_kept, 1)
                g += 1
            dve.wait_ge(prep_kept, n_prep)

            def diagonal(u):
                h, j = units[u]
                dve.wait_ge(spread, u + 1)
                span = slice(j * P, (j + 1) * P)
                nc.vector.tensor_scalar(weights[u % 2][:, span], k.bank(2 * (u % 2))[:, span], neg[:, j, h:h + 1], 0.0,
                                        ALU.add, ALU.min)
                nc.vector.tensor_scalar(back[u % 2], k.bank(2 * (u % 2) + 1)[:, 0:P], neg[:, j, BWD + h:BWD + h + 1], 0.0,
                                        ALU.add, ALU.min).then_inc(diag, 1)

            diagonal(0)
            for u, (h, j) in enumerate(units):
                if u + 1 < len(units):
                    diagonal(u + 1)
                dve.wait_ge(weighed, u + 1)
                if u >= 2:
                    dve.wait_ge(pv, u - 1)
                w, p, c = weights[u % 2], probs[u % 2], cb[:, 4 * (h // 4) + j, :]
                f, b = dt[:, j, h:h + 1], dt[:, j, BWD + h:BWD + h + 1]
                span = slice(j * P, (j + 1) * P)
                if j:
                    nc.vector.scalar_tensor_tensor(out=p[:, 0:j * P], in0=w[:, 0:j * P], scalar=b, in1=c[:, 0:j * P],
                                                   op0=ALU.mult, op1=ALU.mult)
                if j < 3:
                    nc.vector.scalar_tensor_tensor(out=p[:, (j + 1) * P:LAT], in0=w[:, (j + 1) * P:LAT], scalar=f,
                                                   in1=c[:, (j + 1) * P:LAT], op0=ALU.mult, op1=ALU.mult)
                chain.link(nc.vector.scalar_tensor_tensor(out=w[:, span], in0=w[:, span], scalar=f, in1=k.const("s_le_t"),
                                                          op0=ALU.mult, op1=ALU.mult))
                chain.link(nc.vector.scalar_tensor_tensor(out=back[u % 2], in0=back[u % 2], scalar=b,
                                                          in1=k.const("s_ge_t"), op0=ALU.mult, op1=ALU.mult))
                chain.link(nc.vector.tensor_tensor(w[:, span], w[:, span], back[u % 2], ALU.add))
                nc.vector.tensor_tensor(p[:, span], w[:, span], c[:, span], ALU.mult).then_inc(prob, 1)
                if j == 3:
                    dve.wait_ge(pv, u + 1)
                    rows = slice(64 * (h % 2), 64 * (h % 2) + 64)
                    nc.vector.scalar_tensor_tensor(out=y[rows, h // 2, :], in0=xbc[rows, h // 2, :],
                                                   scalar=k.vec[rows, COL["d_skip"] + h // 2:COL["d_skip"] + h // 2 + 1],
                                                   in1=k.bank(4 + h % 4)[rows, :], op0=ALU.mult,
                                                   op1=ALU.add).then_inc(y_kept, 1)


def multiply(k, pairs):
    nc = k.nc
    k.stage()
    with k.block() as block:
        @block.vector
        def _(dve):
            for x, y in pairs:
                nc.vector.tensor_tensor(x, x, y, ALU.mult)


def merge(k, attn, ssd, gates, dst):
    nc = k.nc
    k.stage()
    stream = Stream(k, "w_merge", ring_slots(k, 2, D))
    scratch = [k.ring[:, 2048 + b * LAT:2048 + (b + 1) * LAT] for b in range(2)]
    product, taken = [k.sem("product0"), k.sem("product1")], [k.sem("taken0"), k.sem("taken1")]
    with k.block() as block:
        @block.sync
        def _(sp):
            stream.load(sp, product)

        @block.tensor
        def _(pe):
            with pe.Fori(0, stream.tiles // 2) as i:
                for p in range(2):
                    pe.wait_ge(stream.landed[p], 16 * i + 16)
                    pe.wait_ge(taken[p], i + 1)
                    for half, x in enumerate((attn, ssd)):
                        last = project(k, pe, stream.slots[p][:, half * 512:(half + 1) * 512], 4, lambda n: x[:, n, :],
                                       lambda s: k.bank(2 * p + half), ((0, LAT),))
                    last.then_inc(product[p], 1)

        @block.vector
        def _(dve):
            free_all(dve, taken)
            chain = Chain(dve, k.sem("chain"))
            with dve.Fori(0, stream.tiles // 2) as i:
                chain.turn(i, 4)
                for p in range(2):
                    n = 2 * i + p
                    dve.wait_ge(product[p], i + 1)
                    chain.link(nc.vector.tensor_tensor(scratch[0], k.bank(2 * p), gates[:, n, :], ALU.mult))
                    chain.link(nc.vector.tensor_tensor(scratch[1], k.bank(2 * p + 1), gates[:, n + DT, :], ALU.mult))
                    nc.vector.tensor_tensor(dst[:, n, CTX:T], scratch[0], scratch[1], ALU.add).then_inc(taken[p], 1)
                    dve.wait_ge(taken[p], i + 2)


def second_mixer(k):
    qk, z, xbc = k.area(0, 6, LAT), k.area(3072, 4, LAT), k.area(5120, 6, LAT)
    gates, v, xs = k.area(8192, 16, LAT), k.area(16384, 4, P), k.area(16896, 4, 512)
    attn, y = k.area(18944, 4, LAT), k.area(20992, 4, LAT)
    cos, sin, scratch = (k.arena[:, 23040 + j * LAT:23040 + (j + 1) * LAT] for j in range(3))
    sums = [k.arena[0:ROWS, j * LAT:(j + 1) * LAT] for j in range(4)]
    step, decay = k.arena[0:ROWS, 2048:2560], k.arena[0:ROWS, 2560:3072]
    load(k, ((cos, "rope_cos"), (sin, "rope_sin")))
    project_act(k, "w_qk_2", qk, ACT.Identity, None, SEG_LAT)
    project_act(k, "w_z_2", z, ACT.Silu, None, SEG_LAT)
    project_act(k, "w_gates_2", gates, ACT.Sigmoid, "b_gate_2", SEG_LAT)
    project_conv(k, "w_xbc_2", xbc, "conv_w_2", "conv_b_2", True, 7, SEG_LAT)
    project_tokens(k, "w_v_2", v, DT, lambda n: k.h[:, n, :], range(2, 6), P)
    ring = [k.ring[:, j * LAT:(j + 1) * LAT] for j in range(4)]
    normalise_heads(k, qk, lambda n: k.col("qk_norm_2", 0 if n < 4 else 1), ring[0:2], ring[2:4])
    rotate(k, [qk[:, n, :] for n in range(6)], cos, sin, scratch)

    def half(h):
        return slice(64 * (h % 2), 64 * (h % 2) + 64)

    def shifted(n, rows):
        at = n * LAT - CTX
        return _Tokens(k.arena, rows, at)

    attention(k, SSD_HEADS, SEG_LAT,
              lambda h, a: ((qk[half(h), h // 2, a * P:(a + 1) * P], shifted(4 + h // 4, half(h))),),
              lambda h, b: v[:, b, (h // 4) * 64:(h // 4) * 64 + 64], half, lambda h: attn[half(h), h // 2, :], 0.125)
    ssd_rows(k, sums, step, decay)
    ssd_core(k, xbc, xs, sums, step, None, y)
    multiply(k, [(y[:, n, :], z[:, n, :]) for n in range(4)])
    y_all = _Tiles(y)
    normalise(k, lambda n, c: k.col("ssd_norm_w_2", n), None, SEG_LAT, y_all, y_all, kt=4, root_of=512)
    merge(k, attn, y, gates, k.h)
    project_residual(k, "w_out_2", DT, lambda n: k.h[:, n, :], None, SEG_LAT)


class _Tokens:

    def __init__(self, mem, rows, at):
        self.mem, self.rows, self.at = mem, rows, at

    def __getitem__(self, key):
        _, t = key
        return self.mem[self.rows, self.at + t.start:self.at + t.stop]


class _Tiles:

    def __init__(self, x):
        self.x = x

    def __getitem__(self, key):
        rows, n, t = key
        return self.x[rows, n, t.start - CTX:t.stop - CTX]


def route(k, spread_to):
    nc = k.nc
    k.stage()
    w = k.ring[:, 0:DT * 20]
    at = [20 * DT]

    def room(*shape):
        n = int(np.prod(shape))
        a = k.ring[:, at[0]:at[0] + n]
        at[0] += n
        if len(shape) == 2:
            return a.rearrange("p (a b) -> p a b", b=shape[1])
        return a.rearrange("p (a g e) -> p a g e", g=shape[1], e=shape[2]) if len(shape) == 3 else a

    logits, g_top, g_exp, g_sum, g_hot = room(4, 20), room(4), room(4, 4), room(4), room(4, 4)
    mixed, fine, top1, hot1, rest, top2, hot2 = room(4, 4, 4), room(4, 4), room(4), room(4, 4), room(4, 4), room(4), room(4, 4)
    gap, p1, p2, rank, best, comb = room(4), room(4), room(4), room(4, 4), room(4), room(4, 4, 4)
    rows = k.row[0:N_EXPERTS, 0:LAT]
    names = ("landed", "logit", "spaced", "raised", "turned", "rows_kept", "spread", "spread_kept")
    landed, logit, spaced, raised, turned, rows_kept, spread, spread_kept = (k.sem(s) for s in names)

    def over(a, shape=(P, 4, 4)):
        return a.unsqueeze(2).to_broadcast(list(shape))

    with k.block() as block:
        @block.sync
        def _(sp):
            sp.dma_start(w, k.dram["w_router"]).then_inc(landed, 16)

        @block.tensor
        def _(pe):
            pe.wait_ge(landed, 16)
            for a in range(4):
                for kk in range(DT):
                    last = nc.tensor.matmul(k.bank(0, 20, 20 * a), k.h[:, kk, CTX + a * P:CTX + (a + 1) * P],
                                            w[:, kk * 20:(kk + 1) * 20], start=kk == 0, stop=kk == DT - 1)
            last.then_inc(logit, 1)
            pe.wait_ge(turned, 1)
            flat = comb.rearrange("p a g e -> p a (g e)")
            for a in range(4):
                last = nc.tensor.transpose(k.bank(1, P, a * P)[0:N_EXPERTS, :], flat[:, a, :], k.const("ident"))
            last.then_inc(spread, 1)
            pe.wait_ge(rows_kept, 1)
            for e in range(N_EXPERTS):
                if e >= 4:
                    pe.wait_ge(spread_kept, e - 3)
                nc.tensor.matmul(k.bank(4 + e % 4), k.cst[0:N_EXPERTS, CAT["ident"] + e:CAT["ident"] + e + 1].to_broadcast(
                    [N_EXPERTS, P]), rows, start=True, stop=True).then_inc(spread, 1)

        @block.scalar
        def _(act):
            act.wait_ge(spaced, 1)
            nc.scalar.activation(g_exp, g_exp, ACT.Exp).then_inc(raised, 1)
            act.wait_ge(spaced, 2)
            nc.scalar.activation(gap, gap, ACT.Exp).then_inc(raised, 1)
            for e in range(N_EXPERTS):
                act.wait_ge(spread, e + 2)
                nc.scalar.copy(spread_to[:, e, :], k.bank(4 + e % 4)).then_inc(spread_kept, 1)

        @block.vector
        def _(dve):
            chain = Chain(dve, k.sem("chain"))
            V, link = nc.vector, chain.link
            first = k.const("first").unsqueeze(1).to_broadcast([P, 4, 4])

            def one_hot(out, values, top):
                link(V.tensor_reduce(top, values, AX.X, ALU.max))
                link(V.tensor_tensor(rank, values, over(top), ALU.is_equal))
                link(V.tensor_tensor(rank, rank, first, ALU.mult))
                link(V.tensor_reduce(best, rank, AX.X, ALU.max))
                link(V.tensor_tensor(out, rank, over(best), ALU.is_equal))

            dve.wait_ge(logit, 1)
            bias = k.vec[:, COL["b_router"]:COL["b_router"] + 20].unsqueeze(1).to_broadcast([P, 4, 20])
            link(V.tensor_tensor(logits, k.bank(0, 80).rearrange("p (a n) -> p a n", n=20), bias, ALU.add))
            groups = logits[:, :, 0:4]
            one_hot(g_hot, groups, g_top)
            V.tensor_tensor(g_exp, groups, over(g_top), ALU.subtract).then_inc(spaced, 1)
            link(V.tensor_tensor(mixed, logits[:, :, 4:20].rearrange("p a (g e) -> p a g e", e=4),
                                 g_hot.unsqueeze(3).to_broadcast([P, 4, 4, 4]), ALU.mult))
            link(V.tensor_reduce(fine, mixed.rearrange("p a g e -> p a e g"), AX.X, ALU.add))
            one_hot(hot1, fine, top1)
            link(V.scalar_tensor_tensor(out=rest, in0=hot1, scalar=-3.0e38, in1=fine, op0=ALU.mult, op1=ALU.add))
            one_hot(hot2, rest, top2)
            V.tensor_tensor(gap, top2, top1, ALU.subtract).then_inc(spaced, 1)
            dve.wait_ge(raised, 1)
            link(V.tensor_reduce(g_sum, g_exp, AX.X, ALU.add))
            dve.wait_ge(raised, 2)
            link(V.tensor_scalar(p1, gap, 1.0, None, ALU.add))
            link(V.tensor_tensor(p1, p1, g_sum, ALU.mult))
            link(V.reciprocal(p1, p1))
            link(V.tensor_tensor(p2, p1, gap, ALU.mult))
            link(V.tensor_tensor(hot1, hot1, over(p1), ALU.mult))
            link(V.tensor_tensor(hot2, hot2, over(p2), ALU.mult))
            link(V.tensor_tensor(hot1, hot1, hot2, ALU.add))
            V.tensor_tensor(comb, g_hot.unsqueeze(3).to_broadcast([P, 4, 4, 4]),
                            hot1.unsqueeze(2).to_broadcast([P, 4, 4, 4]), ALU.mult).then_inc(turned, 1)
            dve.wait_ge(spread, 1)
            V.tensor_copy(rows, k.bank(1)[0:N_EXPERTS, :]).then_inc(rows_kept, 1)


def experts(k):
    share = k.ring[:, 4096:4096 + N_EXPERTS * LAT].rearrange("p (e t) -> p e t", t=LAT)
    route(k, share)
    nc = k.nc
    k.stage()
    w13 = [k.arena[:, b * 12288:b * 12288 + 8192] for b in range(2)]
    w2 = [k.arena[:, b * 12288 + 8192:(b + 1) * 12288] for b in range(2)]
    inner = [k.ring[:, b * 2048:(b + 1) * 2048].rearrange("p (f t) -> p f t", t=LAT) for b in range(2)]
    landed13, landed2 = [k.sem("l13_0"), k.sem("l13_1")], [k.sem("l2_0"), k.sem("l2_1")]
    up, silu, gated = ([k.sem(f"{s}{q}") for q in range(2)] for s in ("up", "silu", "gated"))
    down, added = ([k.sem(f"{s}{q}") for q in range(4)] for s in ("down", "added"))
    turns = N_EXPERTS // 2
    with k.block() as block:
        @block.sync
        def _(sp):
            for b in range(2):
                sp.dma_start(w13[b], k.dram["moe_w13"][b]).then_inc(landed13[b], 16)
                sp.dma_start(w2[b], k.dram["moe_w2"][b]).then_inc(landed2[b], 16)
            with sp.Fori(1, turns) as i:
                for b in range(2):
                    e = 2 * i + b
                    sp.wait_ge(up[1], 2 * e - 2)
                    sp.dma_start(w13[b], k.dram["moe_w13"][e]).then_inc(landed13[b], 16)
                    sp.wait_ge(down[3], 2 * e - 2)
                    sp.dma_start(w2[b], k.dram["moe_w2"][e]).then_inc(landed2[b], 16)

        @block.tensor
        def _(pe):
            def up_products(e, b, loads):
                pe.wait_ge(landed13[b], 16 * loads)
                for f in range(4):
                    q = f % 2
                    pe.wait_ge(gated[q], 2 * e + f // 2 + 1)
                    for half in range(2):
                        last = project(k, pe, w13[b][:, f * 2048:(f + 1) * 2048], DT, lambda n: k.h[:, n, :],
                                       lambda s: k.bank(2 * q + half), SEG_LAT, col=half * P, width=2 * P)
                    last.then_inc(up[q], 1)

            def down_products(e, b, loads):
                pe.wait_ge(landed2[b], 16 * loads)
                for q in range(2):
                    pe.wait_ge(gated[q], 2 * e + 3)
                for n in range(DT):
                    pe.wait_ge(added[n % 4], 2 * e + n // 4 + 1)
                    project(k, pe, w2[b][:, n * 512:(n + 1) * 512], 4, lambda f: inner[b][:, f, :],
                            lambda s: k.bank(4 + n % 4), ((0, LAT),)).then_inc(down[n % 4], 1)

            up_products(0, 0, 1)
            with pe.Fori(0, turns - 1) as i:
                up_products(2 * i + 1, 1, i + 1)
                down_products(2 * i, 0, i + 1)
                up_products(2 * i + 2, 0, i + 2)
                down_products(2 * i + 1, 1, i + 1)
            up_products(N_EXPERTS - 1, 1, turns)
            down_products(N_EXPERTS - 2, 0, turns)
            down_products(N_EXPERTS - 1, 1, turns)

        @block.scalar
        def _(act):
            def gates(e, b, reused):
                if reused:
                    act.wait_ge(down[3], 2 * e - 2)
                for f in range(4):
                    q = f % 2
                    act.wait_ge(up[q], 2 * e + f // 2 + 1)
                    nc.scalar.activation(inner[b][:, f, :], k.bank(2 * q), ACT.Silu).then_inc(silu[q], 1)

            for b in range(2):
                gates(b, b, False)
            with act.Fori(1, turns) as i:
                for b in range(2):
                    gates(2 * i + b, b, True)

        @block.vector
        def _(dve):
            free_all(dve, gated + added)
            chain = Chain(dve, k.sem("chain"))

            def gate(e, b):
                for f in range(4):
                    q = f % 2
                    dve.wait_ge(silu[q], 2 * e + f // 2 + 1)
                    chain.link(nc.vector.tensor_tensor(inner[b][:, f, :], inner[b][:, f, :], k.bank(2 * q + 1), ALU.mult))
                    nc.vector.tensor_tensor(inner[b][:, f, :], inner[b][:, f, :], share[:, e, :],
                                            ALU.mult).then_inc(gated[q], 1)

            def add(e):
                for n in range(DT):
                    dve.wait_ge(down[n % 4], 2 * e + n // 4 + 1)
                    x = k.x[:, n, CTX:T]
                    nc.vector.tensor_tensor(x, x, k.bank(4 + n % 4), ALU.add).then_inc(added[n % 4], 1)

            gate(0, 0)
            with dve.Fori(0, turns - 1) as i:
                chain.n, chain.base = 0, 4 + 8 * i
                gate(2 * i + 1, 1)
                add(2 * i)
                gate(2 * i + 2, 0)
                add(2 * i + 1)
            chain.n, chain.base = 0, 4 + 8 * (turns - 1)
            gate(N_EXPERTS - 1, 1)
            add(N_EXPERTS - 2)
            add(N_EXPERTS - 1)


def finish(k, out):
    nc = k.nc
    k.stage()
    tok = k.area(0, 4, D)
    turned, kept, stored = k.sem("turned"), [k.sem("kept0"), k.sem("kept1")], k.sem("stored")
    with k.block() as block:
        @block.tensor
        def _(pe):
            for a in range(4):
                for half in range(2):
                    for d in range(4):
                        last = nc.tensor.transpose(k.bank(2 * a + half, P, d * P),
                                                   k.x[:, 4 * half + d, CTX + a * P:CTX + (a + 1) * P], k.const("ident"))
                    last.then_inc(turned, 1)

        @block.vector
        def _(dve):
            for a in range(4):
                dve.wait_ge(turned, 2 * a + 1)
                nc.vector.tensor_copy(tok[:, a, 0:512], k.bank(2 * a)).then_inc(kept[0], 1)

        @block.scalar
        def _(act):
            for a in range(4):
                act.wait_ge(turned, 2 * a + 2)
                nc.scalar.copy(tok[:, a, 512:1024], k.bank(2 * a + 1)).then_inc(kept[1], 1)

        @block.sync
        def _(sp):
            for a in range(4):
                sp.wait_ge(kept[0], a + 1)
                sp.wait_ge(kept[1], a + 1)
                sp.dma_start(out[a * P:(a + 1) * P, :], tok[:, a, :]).then_inc(stored, 16)
            sp.wait_ge(stored, 64)


STAGES = []


def build(nc, dram, out, upto=None):
    with ExitStack() as ctx:
        k = Kernel(nc, ctx, dram)

        def gain(a):
            return lambda kk, c: k.gain[:, a, kk, c:c + 1]

        def shift(a, layer=0):
            mod = k.mod_next if layer else k.mod
            return lambda kk, c: mod[:, 3 * a * DT + kk, c:c + 1]

        mix = k.area(0, 8, T)
        hidden, scratch = k.area(0, FFT, T), k.area(FFT * T, 2, T)
        steps = [
            ("load", lambda: load_inputs(k)),
            ("mod0", lambda: modulations(k, 0)),
            ("norm0", lambda: normalise(k, gain(0), shift(0), SEGS)),
            ("hyproj", lambda: project_conv(k, "w_in_hy", k.area(0, 12, T), "hy_conv_w", "hy_conv_b", False)),
            ("hyena", lambda: hyena(k, k.area(0, 12, T))),
            ("mlstm", lambda: mlstm(k)),
            ("out0", lambda: project_residual(k, "w_out_0", DT, lambda kk: mix[:, kk, :], 2, SEGS)),
            ("norm0f", lambda: normalise(k, gain(1), shift(1), SEGS)),
            ("up0", lambda: ffn_up(k, 0, hidden, scratch, SEGS, True)),
            ("down0", lambda: project_residual(k, "ffn_down_0", FFT, lambda kk: hidden[:, kk, :], 5, SEGS)),
            ("norm1", lambda: normalise(k, gain(0), shift(0, 1), SEGS)),
            ("mla", lambda: mla(k)),
            ("norm1f", lambda: normalise(k, gain(1), shift(1, 1), SEG_LAT)),
            ("up1", lambda: ffn_up(k, 1, hidden, scratch, SEG_LAT)),
            ("down1", lambda: project_residual(k, "ffn_down_1", FFT, lambda kk: hidden[:, kk, :], 5, SEG_LAT, k.mod_next)),
            ("final", lambda: normalise(k, lambda kk, c: k.col("final_norm", kk), None, SEG_LAT, k.x)),
            ("norm2", lambda: normalise(k, lambda kk, c: k.col("norm_mix_w_2", kk), None, SEG_LAT)),
            ("block2", lambda: second_mixer(k)),
            ("norm2f", lambda: normalise(k, lambda kk, c: k.col("norm_ffn_w_2", kk), None, SEG_LAT)),
            ("moe", lambda: experts(k)),
            ("finish", lambda: finish(k, out)),
        ]
        for name, step in steps:
            step()
            if name == upto:
                break


def tiles(w, width=P):
    kt, n = w.shape[0] // P, w.shape[1] // width
    return np.ascontiguousarray(w.reshape(kt, P, n, width).transpose(2, 1, 0, 3).reshape(n, P, kt * width))


def columns(v):
    return np.asarray(v).reshape(-1, P).T


def padded(v):
    out = np.zeros((P, 1), np.float32)
    out[:v.shape[0], 0] = v
    return out


def rope_tables():
    t = np.arange(LAT)
    axis = np.stack([t // GRID_W, t % GRID_W]).astype(np.float64)
    inv = 10000.0 ** (-np.arange(0, 32, 2) / 32.0)
    ang = axis[:, None, :] * inv[None, :, None]
    ang = np.concatenate([ang, ang], axis=1).reshape(64, LAT)
    sign = np.where((np.arange(64) % 32) < 16, -1.0, 1.0)[:, None]
    return np.cos(ang).astype(np.float32), (sign * np.sin(ang)).astype(np.float32)


def rotation(n):
    r = np.zeros((n, n), np.float32)
    for i in range(n):
        r[i + 16 if i % 32 < 16 else i - 16, i] = 1.0
    return r


def constants():
    out = np.zeros((P, N_CONST), np.float32)
    i = np.arange(P)
    parts = {
        "ident": np.eye(P), "ones": np.ones((P, P)), "ones64": np.kron(np.eye(2), np.ones((64, 64))),
        "onecol": np.tile((np.arange(127) == 63) * 1.0, (P, 1)), "s_le_t": i[:, None] <= i[None, :],
        "s_ge_t": i[:, None] >= i[None, :], "rot_gqa": rotation(P), "eps": np.full((P, 1), EPS),
        "first": np.tile(np.arange(4.0, 0.0, -1.0), (P, 1)),
    }
    for name, a in parts.items():
        out[:, CAT[name]:CAT[name] + a.shape[1]] = a
    return out


def hyena_tables(L):
    n = L // P
    ang = np.pi * np.outer(np.arange(L), 2 * np.arange(L) + 1) / (2 * L)
    fwd = [np.cos(ang), -np.sin(ang)]
    inv = [a.T / L for a in fwd]
    dft = np.stack([a.reshape(n, P, L).transpose(1, 0, 2) for a in fwd + inv]).astype(np.float32)
    pos = np.arange(L, dtype=np.float32)
    t = pos / np.float32(L - 1)
    f = np.linspace(1e-4, 15, 16).astype(np.float32)
    ang = (np.float32(2 * math.pi / L) * pos[:, None] * f[None, :]).astype(np.float32)
    z = np.concatenate([t[:, None], np.cos(ang), -np.sin(ang)], axis=1).T
    deltas = np.abs(np.linspace(math.log(1e-2) / 0.3, math.log(1e-2) / 1.5, HY))
    decay = (np.exp(-t[:, None] * deltas[None, :]) + 0.05).reshape(n, P, HY).transpose(1, 0, 2)
    return dft, np.ascontiguousarray(z.astype(np.float32)), np.ascontiguousarray(decay.astype(np.float32))


def lay_out(inp):
    a = {n: np.asarray(v) for n, v in inp.items()}
    d = {"x": a["x"][0], "ctx": a["ctx"][0], "consts": constants()}
    for layer in range(2):
        d[f"ada_w_{layer}"] = tiles(a[f"ada_w_{layer}"])
        up = a[f"ffn_up_{layer}"].reshape(D, 2, FFT, P).transpose(0, 2, 1, 3).reshape(D, 2 * D_FF)
        d[f"ffn_up_{layer}"] = tiles(up, 2 * P)
        d[f"ffn_down_{layer}"] = tiles(a[f"ffn_down_{layer}"])
    d["w_in_hy"] = tiles(a["w_in_0"][:, 0:3 * HY])
    for n in ("hy_fw1", "hy_fw2", "hy_fw3"):
        d[n] = a[n]
    for name, L in (("lat", LAT), ("ctx", CTX)):
        d[f"hy_dft_{name}"], d[f"hy_pos_{name}"], d[f"hy_decay_{name}"] = hyena_tables(L)
    d["w_out_0"] = tiles(a["w_out_0"])
    v = {n: a[n] for n, _ in VECTORS if n in a}
    one = {
        "hy_small": np.concatenate([padded(a["hy_fb1"]), padded(a["hy_fb2"]), padded(a["hy_freq"])], axis=1),
        "ml_gate_b": padded(a["ml_gate_b"]),
        "ssd_rows": np.concatenate([padded(a["dt_bias_2"].reshape(-1)), padded(a["a_log_2"].reshape(-1))], axis=1),
        "qk_norm_2": np.stack([np.tile(a["q_norm_w_2"][0], 2), np.tile(a["k_norm_w_2"][0], 2)], axis=1),
        "d_skip": columns(np.repeat(a["d_skip_2"][0], 64)),
        "b_router": np.tile(np.concatenate([a["b_router_group_2"][0], a["b_router_expert_2"][0]]), (P, 1)),
    }
    vec = np.zeros((P, N_COLS), np.float32)
    for n, width in VECTORS:
        if n in one:
            part = one[n]
        elif n in v:
            part = columns(v[n].reshape(-1))
        else:
            continue
        vec[:, COL[n]:COL[n] + width] = part
    d["vectors"] = vec
    extra_layout(a, d, vec)
    return d


def extra_layout(a, d, vec):
    w = a["w_in_0"]
    d["w_in_qk"] = tiles(w[:, 1536:2560])
    d["w_in_v"] = tiles(w[:, 2560:3072], ML_W)[0]
    d["w_in_og"] = tiles(w[:, 3072:3584])
    cos, sin = rope_tables()
    d["rope_cos"], d["rope_sin"] = np.tile(cos, (2, 1)), np.tile(sin, (2, 1))
    down = a["mla_w_down"]
    kr = down[:, Q_RANK + KV_RANK:]
    d["mla_w_qa"] = tiles(down[:, 0:Q_RANK])
    d["mla_w_kva"] = tiles(np.concatenate([down[:, Q_RANK:Q_RANK + KV_RANK], kr, kr], axis=1))
    uq = a["mla_w_uq"].reshape(Q_RANK, MLA_HEADS, 192)
    d["mla_w_qn"], d["mla_w_qr"] = tiles(uq[:, :, 0:128].reshape(Q_RANK, -1)), tiles(uq[:, :, 128:].reshape(Q_RANK, -1))
    ukv = a["mla_w_ukv"].reshape(KV_RANK, MLA_HEADS, 2, P)
    d["mla_w_kn"] = tiles(ukv[:, :, 0].reshape(KV_RANK, -1))
    d["mla_w_v0"], d["mla_w_v1"] = tiles(ukv[:, :, 1].reshape(KV_RANK, -1), 512)
    d["mla_w_o"] = tiles(a["mla_w_o"])
    w2 = a["w_in_2"][0]
    kd = w2[:, 512:640].reshape(D, 2, 1, 64)
    kd = np.concatenate([kd, kd], axis=2).reshape(D, 256)
    d["w_qk_2"] = tiles(np.concatenate([w2[:, 0:512], kd], axis=1))
    d["w_v_2"] = tiles(w2[:, 640:768])[0]
    d["w_z_2"], d["w_xbc_2"] = tiles(w2[:, 768:1280]), tiles(w2[:, 1280:2048])
    d["w_in_dt"] = tiles(w2[:, 2048:2064], 16)[0]
    d["w_gates_2"] = tiles(w2[:, 2064:4112])
    d["w_merge"] = np.concatenate([tiles(a["w_attn_o_2"][0]), tiles(a["w_ssd_o_2"][0])], axis=2)
    d["w_out_2"] = tiles(a["w_out_2"][0])
    d["w_router"] = tiles(np.concatenate([a["w_router_group_2"][0], a["w_router_expert_2"][0]], axis=1), 20)[0]
    up = np.stack([a["w1_2"][0], a["w3_2"][0]], axis=2).reshape(N_EXPERTS, DT, P, 2, 4, P)
    d["moe_w13"] = up.transpose(0, 2, 4, 1, 3, 5).reshape(N_EXPERTS, P, 8192)
    d["moe_w2"] = a["w2_2"][0].reshape(N_EXPERTS, 4, P, DT, P).transpose(0, 2, 3, 1, 4).reshape(N_EXPERTS, P, 4096)
    d["w_in_gates"] = tiles(w[:, 3584:3600], 16)[0]


def kernel(**inputs):
    import concourse.bacc as _bacc
    from concourse.bass_utils import run_bass_kernel_spmd as _run

    nc = _bacc.Bacc("TRN2", target_bir_lowering=False, num_devices=1)
    arrays, dram = {}, {}
    for name, a in lay_out(inputs).items():
        arrays[f"in_{name}"] = np.ascontiguousarray(a)
        dram[name] = nc.dram_tensor(f"in_{name}", a.shape, mybir.dt.from_np(a.dtype), kind="ExternalInput").ap()
    out = nc.dram_tensor("out_x", (LAT, D), F32, kind="ExternalOutput").ap()
    build(nc, dram, out)
    r = _run(nc, [arrays], core_ids=[0])
    return np.asarray(r.results[0]["out_x"]).reshape(1, LAT, D)
```

```python
from contextlib import ExitStack, contextmanager
import math

import numpy as np

import concourse.bass as bass
from concourse import mybir

F32 = mybir.dt.float32
F32R = mybir.dt.float32r
ACT = mybir.ActivationFunctionType
ALU = mybir.AluOpType
AX = mybir.AxisListType

P = 128
D = 1024
DT = D // P
CTX = 256
LAT = 512
T = CTX + LAT
SEGS = ((0, CTX), (CTX, LAT))
SEG_LAT = ((CTX, LAT),)
N_MOD = 6
HY = 512
HYT = HY // P
HY_EMB = 33
HY_FF = 64
ML_HEADS = 4
ML_W = 512
D_FF = 2816
FFT = D_FF // P
MLA_HEADS = 8
Q_RANK = 384
KV_RANK = 256
ROPE = 64
MLA_SCALE = (128 + 64) ** -0.5
GRID_W = 64
EPS = 1e-6
BANK = 512
MAGIC = 1.5 * 2.0 ** 23
TWO_PI_HI = 6.28125
TWO_PI_LO = 2 * math.pi - TWO_PI_HI
PI_BELOW = 3.1415925
SSD_HEADS = 8
N_EXPERTS = 16
D_EXPERT = 512
ROWS = 64
BWD = 32
ATANH_TERMS = (15, 13, 11, 9, 7, 5, 3)


VECTORS = [
    ("c", 8), ("c_ctx", 8), ("ada_b_0", 48), ("ada_b_1", 48), ("norm_mix_0", 8), ("norm_ffn_0", 8),
    ("norm_mix_1", 8), ("norm_ffn_1", 8), ("final_norm", 8), ("norm_mix_w_2", 8), ("norm_ffn_w_2", 8),
    ("hy_conv_w", 36), ("hy_conv_b", 12), ("hy_bias", 4), ("ml_conv_w", 24), ("ml_norm_g", 4),
    ("ffn_conv_w_0", 66), ("ffn_conv_b_0", 22), ("ffn_conv_w_1", 66), ("ffn_conv_b_1", 22),
    ("mla_q_norm", 3), ("mla_kv_norm", 2), ("b_gate_2", 16), ("conv_w_2", 42), ("conv_b_2", 6),
    ("ssd_norm_w_2", 4), ("qk_norm_2", 2), ("hy_small", 3), ("ml_gate_b", 1), ("ssd_rows", 2),
    ("d_skip", 4), ("b_router", 20),
]
COL = {}
_at = 0
for _name, _n in VECTORS:
    COL[_name] = _at
    _at += _n
N_COLS = _at

CONSTS = [("ident", 128), ("ones64", 128), ("onecol", 127), ("s_le_t", 128), ("s_ge_t", 128),
          ("rot_gqa", 128), ("eps", 1), ("first", 4)]
CAT = {}
_at = 0
for _name, _n in CONSTS:
    CAT[_name] = _at
    _at += _n
N_CONST = _at
ONE = CAT["onecol"] + 63


X_AT = 0
H_LOW_AT = DT * T
H_HIGH_AT = 2 * DT * T
WORK_AT = 3 * DT * T
RING_AT = WORK_AT + 24576
MEM = RING_AT + 7680


class Pair:

    def __init__(self, k, high_at, low_at, tiles, width, shift=0):
        self.high, self.low = k.rounded(high_at, tiles, width), k.rounded(low_at, tiles, width)
        self.high_plain, self.low_plain = self.high.bitcast(F32), self.low.bitcast(F32)
        self.whole = k.plain(low_at, tiles, width)
        self.shift = shift

    def tokens(self, n, a, b):
        return [part[:, n, a - self.shift:b - self.shift] for part in (self.high, self.low)]


class Kernel:

    def __init__(self, nc, ctx, dram):
        self.nc, self.ctx, self.dram = nc, ctx, dram

        def sb(name, cols):
            return ctx.enter_context(nc.sbuf_tensor(name, [P, cols], F32))

        self.slabs = [(a, b, sb(name, b - a)) for name, a, b in (
            ("x", X_AT, H_LOW_AT), ("h", H_LOW_AT, WORK_AT), ("work", WORK_AT, MEM))]
        self.slab_at, self.aliases = nc.sbuf_base - 4 * MEM, {}
        self.x, self.h, self.h_top = (self.plain(a, DT, T) for a in (X_AT, H_LOW_AT, H_HIGH_AT))
        self.h_pair = Pair(self, H_HIGH_AT, H_LOW_AT, DT, T)
        self.arena, self.ring = self.words(WORK_AT, MEM), self.words(RING_AT, MEM)
        self.vec = sb("vec", N_COLS)
        self.cst = sb("cst", N_CONST)
        self.mod = sb("mod", N_MOD * DT * 2)[:, :].rearrange("p (n c) -> p n c", c=2)
        self.mod_next = sb("mod_next", N_MOD * DT * 2)[:, :].rearrange("p (n c) -> p n c", c=2)
        self.gain = sb("gain", 2 * DT * 2)[:, :].rearrange("p (a k c) -> p a k c", a=2, c=2)
        self.silu_c = sb("silu_c", DT * 2)[:, :].rearrange("p (k c) -> p k c", c=2)
        self.row = sb("row", T)
        self.ps = ctx.enter_context(nc.psum_tensor("ps", [P, 8 * BANK], F32))
        self.n_stage, self.used = 0, 0
        self.sems = [[ctx.enter_context(nc.semaphore(f"{n}_{s}")) for s in range(32)] for n in ("even", "odd")]

    def stage(self):
        self.n_stage += 1
        self.spent, self.used = self.used, 0

    def sem(self, name):
        self.used += 1
        return self.sems[self.n_stage % 2][self.used - 1]

    @contextmanager
    def block(self):
        with self.nc.Block() as block:
            @block.gpsimd
            def _(pool):
                for s in self.sems[(self.n_stage + 1) % 2][:self.spent]:
                    pool.sem_clear(s)
            yield block

    def col(self, name, n=0):
        return self.vec[:, bass.ds(n + COL[name], 1)]

    def const(self, name, width=None, at=0):
        n = dict(CONSTS)[name] if width is None else width
        return self.cst[:, CAT[name] + at:CAT[name] + at + n]

    def bank(self, b, n=BANK, at=0):
        return self.ps[:, b * BANK + at:b * BANK + at + n]

    def pair(self, p):
        return self.ps[:, 2 * p * BANK + BANK - CTX:(2 * p + 2) * BANK]

    def words(self, a, b):
        (start, tensor), = [(start, tensor) for start, end, tensor in self.slabs if start <= a and b <= end]
        return tensor[:, a - start:b - start]

    def rounded_words(self, a, b):
        if (a, b) not in self.aliases:
            self.aliases[a, b] = self.nc.alloc_sbuf_tensor_at(f"rounded_{a}_{b}", [P, b - a], F32R,
                                                              offset=self.slab_at + 4 * a)
        return self.aliases[a, b][:, :]

    def plain(self, at, tiles, width):
        return self.words(at, at + tiles * width).rearrange("p (k t) -> p k t", t=width)

    def rounded(self, at, tiles, width):
        return self.rounded_words(at, at + tiles * width).rearrange("p (k t) -> p k t", t=width)

    def area(self, at, tiles, width):
        return self.plain(WORK_AT + at, tiles, width)


class Chain:

    def __init__(self, engine, sem):
        self.engine, self.sem, self.n, self.base = engine, sem, 0, 0

    def link(self, instruction):
        self.n += 1
        instruction.then_inc(self.sem, 1)
        self.engine.wait_ge(self.sem, self.base + self.n)

    def turn(self, i, per_turn):
        self.n, self.base = 0, i * per_turn


def free_all(engine, sems):
    for s in sems:
        engine.sem_inc(s, 1)


class Stream:

    def __init__(self, k, name, width, n=2):
        self.k, self.src, self.n = k, k.dram[name], n
        self.tiles = self.src.shape[0]
        at = MEM - 3 * n * width
        self.at = at - WORK_AT
        self.raw = [k.words(at + s * width, at + (s + 1) * width) for s in range(n)]
        spots = [(at + (n + 2 * s) * width, at + (n + 2 * s + 1) * width) for s in range(n)]
        self.parts = [tuple(k.rounded_words(a, a + width) for a in spot) for spot in spots]
        self.high_plain = [high.bitcast(F32) for high, low in self.parts]
        self.landed, self.rounded, self.ready = ([k.sem(f"{w}{s}") for s in range(n)] for w in ("landed", "rounded", "ready"))
        assert self.tiles % n == 0

    def load(self, sp):
        for s in range(self.n):
            sp.dma_start(self.raw[s], self.src[s]).then_inc(self.landed[s], 16)
        if self.tiles > self.n:
            with sp.Fori(1, self.tiles // self.n) as i:
                for s in range(self.n):
                    sp.wait_ge(self.ready[s], i)
                    sp.dma_start(self.raw[s], self.src[i * self.n + s]).then_inc(self.landed[s], 16)

    def high(self, act, s, loads):
        act.wait_ge(self.landed[s], 16 * loads)
        self.k.nc.scalar.copy(self.parts[s][0], self.raw[s]).then_inc(self.rounded[s], 1)

    def low(self, dve, s, loads):
        dve.wait_ge(self.rounded[s], loads)
        self.k.nc.vector.tensor_tensor(self.parts[s][1], self.raw[s], self.high_plain[s],
                                       ALU.subtract).then_inc(self.ready[s], 1)


def in_turns(engine, turns, turn):
    if turns > 1:
        with engine.Fori(0, turns - 1) as i:
            turn(i, False)
    turn(turns - 1, True)


def three_passes(k, out, stationary, moving, start, stop):
    (sh, sl), (mh, ml) = stationary, moving
    k.nc.tensor.matmul(out, sh, mh, start=start, stop=False)
    k.nc.tensor.matmul(out, sh, ml, start=False, stop=False)
    return k.nc.tensor.matmul(out, sl, mh, start=False, stop=stop)


def project(k, parts, kt, x, psum_of, segs, col=0, width=P):
    for s, (t0, n) in enumerate(segs):
        for kk in range(kt):
            at = kk * width + col
            last = three_passes(k, psum_of(s), [w[:, at:at + P] for w in parts], x.tokens(kk, t0, t0 + n),
                                kk == 0, kk == kt - 1)
    return last


def project_few(k, w, psum_of, segs, m):
    for s, (t0, n) in enumerate(segs):
        for kk in range(DT):
            for part, x in enumerate((k.h_pair.high_plain, k.h_pair.low_plain)):
                last = k.nc.tensor.matmul(psum_of(s), w[:, kk * m:(kk + 1) * m], x[:, kk, t0:t0 + n],
                                          start=kk == 0 and part == 0, stop=kk == DT - 1 and part == 1)
    return last


def seg_out(k, p):
    pair = k.pair(p)
    return lambda s: pair[:, SEGS[s][0]:SEGS[s][0] + SEGS[s][1]]


def load_inputs(k):
    nc = k.nc
    k.stage()
    tok = k.area(0, 6, D)
    consts, tokens = k.sem("consts"), k.sem("tokens")
    turned = [k.sem("turned_wide"), k.sem("turned_narrow")]
    kept = [k.sem("kept_wide"), k.sem("kept_narrow")]
    halves = ((0, 4), (4, 2))
    with k.block() as block:
        @block.sync
        def _(sp):
            sp.dma_start(k.cst[:, :], k.dram["consts"]).then_inc(consts, 16)
            sp.dma_start(tok[:, 0:2, :], k.dram["ctx"].rearrange("(a p) d -> p a d", p=P)).then_inc(tokens, 16)
            sp.dma_start(tok[:, 2:6, :], k.dram["x"].rearrange("(a p) d -> p a d", p=P)).then_inc(tokens, 16)
            sp.dma_start(k.vec[:, :], k.dram["vectors"]).then_inc(consts, 16)
            sp.wait_ge(consts, 32)

        @block.tensor
        def _(pe):
            pe.wait_ge(consts, 32)
            pe.wait_ge(tokens, 32)
            for d in range(DT):
                for g, (a0, n) in enumerate(halves):
                    if d >= 4:
                        pe.wait_ge(kept[g], d - 3)
                    for a in range(n):
                        last = nc.tensor.transpose(k.bank(2 * (d % 4) + g, P, a * P),
                                                   tok[:, a0 + a, d * P:(d + 1) * P], k.const("ident"))
                    last.then_inc(turned[g], 1)

        @block.vector
        def _(dve):
            for d in range(DT):
                dve.wait_ge(turned[0], d + 1)
                nc.vector.tensor_copy(k.x[:, d, 0:4 * P], k.bank(2 * (d % 4))).then_inc(kept[0], 1)

        @block.scalar
        def _(act):
            for d in range(DT):
                act.wait_ge(turned[1], d + 1)
                nc.scalar.copy(k.x[:, d, 4 * P:T], k.bank(2 * (d % 4) + 1, 2 * P)).then_inc(kept[1], 1)
            act.wait_ge(consts, 32)
            nc.scalar.activation(k.silu_c[:, :, 0], k.vec[:, COL["c"]:COL["c"] + DT], ACT.Silu)
            nc.scalar.activation(k.silu_c[:, :, 1], k.vec[:, COL["c_ctx"]:COL["c_ctx"] + DT], ACT.Silu)


def mixer_gains(k, layer, mod):
    for a, norm in enumerate(("norm_mix", "norm_ffn")):
        w = COL[f"{norm}_{layer}"]
        for c in range(2):
            k.nc.vector.scalar_tensor_tensor(
                out=k.gain[:, a, :, c], in0=mod[:, (3 * a + 1) * DT:(3 * a + 2) * DT, c], scalar=1.0,
                in1=k.vec[:, w:w + DT], op0=ALU.add, op1=ALU.mult)


def modulations(k, layer, mod):
    nc = k.nc
    k.stage()
    n, group = 3, 4 * DT * P
    src = k.dram[f"ada_w_{layer}"]
    turns = src.shape[0] // n
    slots = [k.words(MEM - (s + 1) * group, MEM - s * group) for s in range(n)]
    rows = [k.arena[0:2, s * 512:(s + 1) * 512] for s in range(n)]
    landed, done, held, turned, kept = ([k.sem(f"{w}{s}") for s in range(n)] for w in ("landed", "done", "held", "turned", "kept"))
    with k.block() as block:
        @block.sync
        def _(sp):
            for s in range(n):
                sp.dma_start(slots[s], src[s]).then_inc(landed[s], 16)
            with sp.Fori(1, turns) as i:
                for s in range(n):
                    sp.wait_ge(done[s], i)
                    sp.dma_start(slots[s], src[i * n + s]).then_inc(landed[s], 16)

        @block.tensor
        def _(pe):
            with pe.Fori(0, turns) as i:
                for s in range(n):
                    pe.wait_ge(landed[s], 16 * i + 16)
                    pe.wait_ge(kept[s], i + 1)
                    for kk in range(DT):
                        last = nc.tensor.matmul(k.bank(s)[0:2, :], k.silu_c[:, kk, :], slots[s][:, kk * 512:(kk + 1) * 512],
                                                start=kk == 0, stop=kk == DT - 1)
                    last.then_inc(done[s], 1)
                    pe.wait_ge(held[s], i + 1)
                    for j in range(4):
                        last = nc.tensor.matmul(k.bank(4 + s, 2, 2 * j), rows[s][:, j * P:(j + 1) * P],
                                                k.cst[0:2, CAT["ident"]:CAT["ident"] + 2], start=True, stop=True)
                    last.then_inc(turned[s], 1)

        @block.vector
        def _(dve):
            free_all(dve, kept)
            with dve.Fori(0, turns) as i:
                for s in range(n):
                    dve.wait_ge(done[s], i + 1)
                    nc.vector.tensor_copy(rows[s], k.bank(s)[0:2, :]).then_inc(held[s], 1)
                    dve.wait_ge(turned[s], i + 1)
                    at = 4 * (i * n + s)
                    bias = k.vec[:, bass.ds(at + COL[f"ada_b_{layer}"], 4)].unsqueeze(2).to_broadcast([P, 4, 2])
                    nc.vector.tensor_tensor(mod[:, bass.ds(at, 4), :],
                                            k.bank(4 + s, 8).rearrange("p (j c) -> p j c", c=2), bias,
                                            ALU.add).then_inc(kept[s], 1)
            for s in range(n):
                dve.wait_ge(kept[s], turns + 1)
            mixer_gains(k, layer, mod)


def normalise(k, gain_of, shift_of, segs, dst=None, x=None, kt=DT, root_of=D, pair=None):
    nc = k.nc
    k.stage()
    dst, x = k.h if dst is None else dst, k.x if x is None else x
    sq = k.h_top
    moved, rounded = k.sem("moved"), k.sem("rounded")
    t0, t1 = segs[0][0], T
    squares, sums, root, scaled, inverse, ends = (k.sem(s) for s in ("squares", "sums", "root", "scaled", "inverse", "ends"))
    with k.block() as block:
        @block.scalar
        def _(act):
            for kk in range(kt):
                nc.scalar.activation(sq[:, kk, t0:t1], x[:, kk, t0:t1], ACT.Square).then_inc(squares, 1)
            act.wait_ge(sums, 1)
            nc.scalar.activation(k.row[:, t0:t1], k.pair(0)[:, t0:t1], ACT.Sqrt, bias=k.const("eps"),
                                 scale=1.0 / root_of).then_inc(root, 1)
            for kk in range(kt):
                act.wait_ge(scaled, kk + 1)
                for s, (a, n) in enumerate(segs):
                    c = 0 if a else 1
                    shift = 0.0 if shift_of is None else shift_of(kk, c)
                    last = nc.scalar.activation(dst[:, kk, a:a + n], dst[:, kk, a:a + n], ACT.Identity,
                                                scale=gain_of(kk, c), bias=shift)
                last.then_inc(moved, 1)
                if pair:
                    act.wait_ge(moved, kk + 1)
                    nc.scalar.copy(pair.high[:, kk, t0:t1], dst[:, kk, t0:t1]).then_inc(rounded, 1)

        @block.tensor
        def _(pe):
            for kk in range(kt):
                pe.wait_ge(squares, kk + 1)
                for a, n in segs:
                    last = nc.tensor.matmul(k.pair(0)[:, a:a + n], k.const("onecol", 1, 63).to_broadcast([P, P]), sq[:, kk, a:a + n],
                                            start=kk == 0, stop=kk == kt - 1)
            last.then_inc(sums, 1)

        @block.vector
        def _(dve):
            dve.wait_ge(root, 1)
            nc.vector.reciprocal(k.row[:, t0:t1], k.row[:, t0:t1]).then_inc(inverse, 1)
            dve.wait_ge(inverse, 1)
            for kk in range(kt):
                nc.vector.tensor_tensor(dst[:, kk, t0:t1], x[:, kk, t0:t1], k.row[:, t0:t1],
                                        ALU.mult).then_inc(scaled, 1)
            if pair:
                for kk in range(kt):
                    dve.wait_ge(rounded, kk + 1)
                    nc.vector.tensor_tensor(pair.low[:, kk, t0:t1], dst[:, kk, t0:t1], pair.high_plain[:, kk, t0:t1],
                                            ALU.subtract)


def split(k, tiles):
    nc = k.nc
    k.stage()
    rounded = k.sem("rounded")
    with k.block() as block:
        @block.scalar
        def _(act):
            for whole, high, high_plain, low in tiles:
                nc.scalar.copy(high, whole).then_inc(rounded, 1)

        @block.vector
        def _(dve):
            for n, (whole, high, high_plain, low) in enumerate(tiles):
                dve.wait_ge(rounded, n + 1)
                nc.vector.tensor_tensor(low, whole, high_plain, ALU.subtract)


def whole_tiles(pair, wholes, segs_from=0):
    return [(w, pair.high[:, n, segs_from:segs_from + w.shape[1]], pair.high_plain[:, n, segs_from:segs_from + w.shape[1]],
             pair.low[:, n, segs_from:segs_from + w.shape[1]]) for n, w in enumerate(wholes)]


def project_conv(k, weights, dst, conv_w, conv_b, silu, taps=3, segs=SEGS):
    nc = k.nc
    k.stage()
    stream = Stream(k, weights, D)
    tiles, turns = stream.tiles, stream.tiles // 2
    t0 = segs[0][0]
    product, taken = [k.sem("product0"), k.sem("product1")], [k.sem("taken0"), k.sem("taken1")]
    middle, summed = k.sem("middle"), k.sem("summed")
    offsets = [o - taps // 2 for o in range(taps) if o != taps // 2]
    per_tile = len(offsets) * len(segs)

    def sums(n, p):
        return k.arena[:, stream.at - (p + 1) * T:stream.at - p * T][:, t0:T] if silu else dst[:, n, :]

    with k.block() as block:
        @block.sync
        def _(sp):
            stream.load(sp)

        @block.tensor
        def _(pe):
            with pe.Fori(0, turns) as i:
                for p in range(2):
                    pe.wait_ge(stream.ready[p], i + 1)
                    pe.wait_ge(taken[p], i + 1)
                    project(k, stream.parts[p], DT, k.h_pair,
                            lambda s: k.pair(p)[:, segs[s][0]:segs[s][0] + segs[s][1]], segs).then_inc(product[p], 1)

        @block.scalar
        def _(act):
            for p in range(2):
                stream.high(act, p, 1)

            def turn(i, last):
                for p in range(2):
                    n = 2 * i + p
                    act.wait_ge(product[p], i + 1)
                    if not last:
                        stream.high(act, p, i + 2)
                    bias = k.col(conv_b, n) if conv_b else 0.0
                    nc.scalar.activation(sums(n, p), k.pair(p)[:, t0:T], ACT.Identity,
                                         scale=k.col(conv_w, n + tiles * (taps // 2)), bias=bias).then_inc(middle, 1)
                    if silu:
                        act.wait_ge(summed, per_tile * (n + 1))
                        nc.scalar.activation(dst[:, n, :], sums(n, p), ACT.Silu)

            in_turns(act, turns, turn)

        @block.vector
        def _(dve):
            free_all(dve, taken)
            for p in range(2):
                stream.low(dve, p, 1)

            def turn(i, last):
                for p in range(2):
                    n = 2 * i + p
                    if not last:
                        stream.low(dve, p, i + 2)
                    dve.wait_ge(middle, n + 1)
                    for m, o in enumerate(offsets):
                        for a, w in segs:
                            lo, hi = max(a, a - o), min(a + w, a + w - o)
                            out = sums(n, p)[:, lo - t0:hi - t0]
                            nc.vector.scalar_tensor_tensor(out=out, in0=k.pair(p)[:, lo + o:hi + o],
                                                           scalar=k.col(conv_w, n + tiles * (o + taps // 2)), in1=out,
                                                           op0=ALU.mult, op1=ALU.add).then_inc(summed, 1)
                        dve.wait_ge(summed, per_tile * n + len(segs) * (m + 1))
                    nc.vector.sem_inc(taken[p], 1)

            in_turns(dve, turns, turn)


def ffn_up(k, layer, hidden, scratch, segs):
    nc = k.nc
    k.stage()
    stream = Stream(k, f"ffn_up_{layer}", 2 * D)
    turns, ns = stream.tiles // 2, len(segs)
    t0, t1 = segs[0][0], T
    conv_w, conv_b = f"ffn_conv_w_{layer}", f"ffn_conv_b_{layer}"
    product, taken = [k.sem("product0"), k.sem("product1")], [k.sem("taken0"), k.sem("taken1")]
    middle, left, right, gated = (k.sem(s) for s in ("middle", "left", "right", "gated"))
    with k.block() as block:
        @block.sync
        def _(sp):
            stream.load(sp)

        @block.tensor
        def _(pe):
            with pe.Fori(0, turns) as i:
                for p in range(2):
                    pe.wait_ge(stream.ready[p], i + 1)
                    pe.wait_ge(taken[p], i + 1)
                    for half in range(2):
                        last = project(k, stream.parts[p], DT, k.h_pair,
                                       lambda s: k.pair(2 * p + half)[:, segs[s][0]:segs[s][0] + segs[s][1]],
                                       segs, col=half * P, width=2 * P)
                    last.then_inc(product[p], 1)

        @block.scalar
        def _(act):
            for p in range(2):
                stream.high(act, p, 1)

            def turn(i, last):
                for p in range(2):
                    n = 2 * i + p
                    act.wait_ge(product[p], i + 1)
                    if not last:
                        stream.high(act, p, i + 2)
                    act.wait_ge(taken[p], i + 1)
                    nc.scalar.activation(scratch[:, p, t0:t1], k.pair(2 * p)[:, t0:t1], ACT.Identity,
                                         scale=k.col(conv_w, n + FFT), bias=k.col(conv_b, n)).then_inc(middle, 1)
                    act.wait_ge(right, ns * (n + 1))
                    nc.scalar.activation(scratch[:, p, t0:t1], scratch[:, p, t0:t1], ACT.Silu).then_inc(gated, 1)

            in_turns(act, turns, turn)

        @block.vector
        def _(dve):
            free_all(dve, taken)
            for p in range(2):
                stream.low(dve, p, 1)

            def turn(i, last):
                for p in range(2):
                    n = 2 * i + p
                    if not last:
                        stream.low(dve, p, i + 2)
                    dve.wait_ge(middle, n + 1)
                    for a, w in segs:
                        out = scratch[:, p, a + 1:a + w]
                        nc.vector.scalar_tensor_tensor(out=out, in0=k.pair(2 * p)[:, a:a + w - 1],
                                                       scalar=k.col(conv_w, n), in1=out, op0=ALU.mult,
                                                       op1=ALU.add).then_inc(left, 1)
                    dve.wait_ge(left, ns * (n + 1))
                    for a, w in segs:
                        out = scratch[:, p, a:a + w - 1]
                        nc.vector.scalar_tensor_tensor(out=out, in0=k.pair(2 * p)[:, a + 1:a + w],
                                                       scalar=k.col(conv_w, n + 2 * FFT), in1=out,
                                                       op0=ALU.mult, op1=ALU.add).then_inc(right, 1)
                    dve.wait_ge(gated, n + 1)
                    nc.vector.tensor_tensor(hidden[:, n, t0:t1], scratch[:, p, t0:t1],
                                            k.pair(2 * p + 1)[:, t0:t1], ALU.mult).then_inc(taken[p], 1)

            in_turns(dve, turns, turn)


def ffn_down(k, weights, hidden, mod, seg):
    nc = k.nc
    k.stage()
    (t0, w), c = seg, 0 if seg[0] else 1
    stream = Stream(k, weights, D)
    turns = stream.tiles // 2
    at = WORK_AT + FFT * T
    inner = Pair(k, at, at + 2 * LAT, 2, LAT)
    product, rounded, cut, summed = [k.sem("product0"), k.sem("product1")], k.sem("rounded"), k.sem("cut"), k.sem("summed")
    with k.block() as block:
        @block.sync
        def _(sp):
            stream.load(sp)

        @block.tensor
        def _(pe):
            def turn(i, first, last):
                for p in range(2):
                    pe.wait_ge(stream.ready[p], i + 1)
                    pe.wait_ge(cut, 2 * i + p + 1)
                    for n in range(DT):
                        done = three_passes(k, k.bank(n, w), [part[:, n * P:(n + 1) * P] for part in stream.parts[p]],
                                            inner.tokens(p, 0, w), first and p == 0, last and p == 1)
                    done.then_inc(product[p], 1)

            turn(0, True, False)
            with pe.Fori(1, turns - 1) as i:
                turn(i, False, False)
            turn(turns - 1, False, True)

        @block.scalar
        def _(act):
            def high(n, p, loads):
                stream.high(act, p, loads)
                nc.scalar.copy(inner.high[:, p, 0:w], hidden[:, n, t0:t0 + w]).then_inc(rounded, 1)

            for p in range(2):
                high(p, p, 1)
            with act.Fori(0, turns - 1) as i:
                for p in range(2):
                    act.wait_ge(product[p], i + 1)
                    high(2 * i + p + 2, p, i + 2)

        @block.vector
        def _(dve):
            def low(n, p, loads):
                stream.low(dve, p, loads)
                dve.wait_ge(rounded, n + 1)
                nc.vector.tensor_tensor(inner.low[:, p, 0:w], hidden[:, n, t0:t0 + w], inner.high_plain[:, p, 0:w],
                                        ALU.subtract).then_inc(cut, 1)

            for p in range(2):
                low(p, p, 1)
            with dve.Fori(0, turns - 1) as i:
                for p in range(2):
                    low(2 * i + p + 2, p, i + 2)
            dve.wait_ge(product[1], turns)
            for n in range(DT):
                x = k.x[:, n, t0:t0 + w]
                nc.vector.scalar_tensor_tensor(out=x, in0=k.bank(n, w), scalar=mod[:, 5 * DT + n, c:c + 1], in1=x,
                                               op0=ALU.mult, op1=ALU.add).then_inc(summed, 1)


def project_residual(k, weights, x_in, mod_index, segs, mod=None):
    nc = k.nc
    mod = k.mod if mod is None else mod
    k.stage()
    stream = Stream(k, weights, D)
    turns = stream.tiles // 2
    product, taken = [k.sem("product0"), k.sem("product1")], [k.sem("taken0"), k.sem("taken1")]
    with k.block() as block:
        @block.sync
        def _(sp):
            stream.load(sp)

        @block.tensor
        def _(pe):
            with pe.Fori(0, turns) as i:
                for p in range(2):
                    pe.wait_ge(stream.ready[p], i + 1)
                    pe.wait_ge(taken[p], i + 1)
                    project(k, stream.parts[p], DT, x_in,
                            lambda s: k.pair(p)[:, segs[s][0]:segs[s][0] + segs[s][1]], segs).then_inc(product[p], 1)

        @block.scalar
        def _(act):
            for p in range(2):
                stream.high(act, p, 1)
            with act.Fori(0, turns - 1) as i:
                for p in range(2):
                    act.wait_ge(product[p], i + 1)
                    stream.high(act, p, i + 2)

        @block.vector
        def _(dve):
            free_all(dve, taken)
            for p in range(2):
                stream.low(dve, p, 1)

            def turn(i, last):
                for p in range(2):
                    n = 2 * i + p
                    dve.wait_ge(product[p], i + 1)
                    if not last:
                        stream.low(dve, p, i + 2)
                    for a, w in segs:
                        x = k.x[:, n, a:a + w]
                        gate = 1.0 if mod_index is None else mod[:, bass.ds(n + mod_index * DT, 1), 0 if a else 1]
                        done = nc.vector.scalar_tensor_tensor(out=x, in0=k.pair(p)[:, a:a + w], scalar=gate, in1=x,
                                                              op0=ALU.mult, op1=ALU.add)
                    done.then_inc(taken[p], 1)

            in_turns(dve, turns, turn)


def hyena(k, u):
    nc = k.nc
    k.stage()
    A = 9216
    gain_at = 8 * T
    fw = k.arena[:, 20480:21632]
    fw1, fw2, fw3 = fw[0:HY_EMB, 0:64], fw[0:HY_FF, 64:128], fw[0:HY_FF, 128:1152]
    sine_rows = k.area(18432, 3, 512)
    tmp = k.area(17408, 2, 512)
    loads, kept, done, sine, drawn = (k.sem(s) for s in ("loads", "kept", "done", "sine", "drawn"))
    sizes = []
    for L, off, dec, z, g_at in ((LAT, CTX, k.arena[:, 29824:31872], k.arena[:, 19968:20480], gain_at),
                                 (CTX, 0, k.arena[:, 29824:30848], k.arena[:, 31872:32128], gain_at + 2048)):
        n = L // P
        tab = [k.area(21632 + j * n * L, n, L) for j in range(4)]
        sizes.append((L, off, n, tab, dec.rearrange("p (a c) -> p a c", c=HY), z[0:HY_EMB, :], k.area(g_at, n, HY)))
    spec = k.area(13312, 8, HY)
    hsum, hdif = k.area(A, 4, HY), k.area(A + 2048, 4, HY)
    yspec = k.area(A, 8, HY)
    with k.block() as block:
        @block.sync
        def _(sp):
            sp.dma_start(fw1, k.dram["hy_fw1"]).then_inc(loads, 16)
            sp.dma_start(fw2, k.dram["hy_fw2"]).then_inc(loads, 16)
            sp.dma_start(fw3, k.dram["hy_fw3"]).then_inc(loads, 16)
            for size, name in zip(sizes, ("lat", "ctx")):
                L, off, n, tab, dec, z, gT = size
                if name == "ctx":
                    sp.wait_ge(done, 2 + 4 * (LAT // P) + HYT)
                sp.dma_start(z, k.dram[f"hy_pos_{name}"]).then_inc(loads, 16)
                sp.dma_start(dec, k.dram[f"hy_decay_{name}"]).then_inc(loads, 16)
                for j in range(4):
                    sp.dma_start(tab[j], k.dram[f"hy_dft_{name}"][j]).then_inc(loads, 16)

        @block.tensor
        def _(pe):
            pe.wait_ge(loads, 16 * 9)
            group = 0

            def begin(need=0):
                need = max(need, group - 3)
                if need > 0:
                    pe.wait_ge(kept, need)
                return 2 * (group % 4)
            for turn, (L, off, n, tab, dec, z, gT) in enumerate(sizes):
                if turn == 1:
                    pe.wait_ge(loads, 16 * 15)
                b = begin()
                nc.tensor.matmul(k.bank(b, L)[0:HY_FF, :], fw1, z, start=True, stop=True).then_inc(done, 1)
                group += 1
                if turn == 0:
                    pe.wait_ge(drawn, 1)
                for a in range(n):
                    b = begin()
                    for c in range(HYT):
                        last = nc.tensor.transpose(k.bank(b, P, c * P), u[:, 4 + c, off + a * P:off + (a + 1) * P],
                                                   k.const("ident"))
                    last.then_inc(done, 1)
                    group += 1
                b = begin()
                pe.wait_ge(sine, 2 * turn + 1)
                nc.tensor.matmul(k.bank(b, L)[0:HY_FF, :], fw2, sine_rows[0:HY_FF, 1, 0:L], start=True,
                                 stop=True).then_inc(done, 1)
                group += 1
                pe.wait_ge(sine, 2 * turn + 2)
                for a in range(n):
                    b = begin()
                    for half in range(2):
                        last = nc.tensor.matmul(k.bank(b + half), sine_rows[0:HY_FF, 2, a * P:(a + 1) * P],
                                                fw3[:, half * HY:(half + 1) * HY], start=True, stop=True)
                    last.then_inc(done, 1)
                    group += 1
                filters = group
                for f in range(n):
                    b = begin(filters)
                    for part, src in ((0, hsum), (1, hdif)):
                        for a in range(n):
                            last = nc.tensor.matmul(k.bank(b + part), tab[part][:, a, f * P:(f + 1) * P], src[:, a, :],
                                                    start=a == 0, stop=a == n - 1)
                    last.then_inc(done, 1)
                    group += 1
                spectra = group
                for f in range(n):
                    b = begin(spectra)
                    for part in range(2):
                        for a in range(n):
                            last = nc.tensor.matmul(k.bank(b + part), tab[part][:, a, f * P:(f + 1) * P], gT[:, a, :],
                                                    start=a == 0, stop=a == n - 1)
                    last.then_inc(done, 1)
                    group += 1
                products = group
                for c in range(HYT):
                    b = begin(products)
                    for part in range(2):
                        for f in range(n):
                            last = nc.tensor.matmul(k.bank(b, L), yspec[:, 4 * part + f, c * P:(c + 1) * P],
                                                    tab[2 + part][:, f, :], start=part == 0 and f == 0,
                                                    stop=part == 1 and f == n - 1)
                    last.then_inc(done, 1)
                    group += 1

        @block.scalar
        def _(act):
            for turn, size in enumerate(sizes):
                for layer in range(2):
                    act.wait_ge(drawn, 2 * turn + layer + 2)
                    nc.scalar.activation(sine_rows[0:HY_FF, 1 + layer, 0:size[0]], sine_rows[0:HY_FF, 0, 0:size[0]],
                                         ACT.Sin).then_inc(sine, 1)

        @block.vector
        def _(dve):
            chain = Chain(dve, k.sem("chain"))
            group = 0
            nc.vector.tensor_tensor(u[:, 4:8, :], u[:, 4:8, :], u[:, 8:12, :], ALU.mult).then_inc(drawn, 1)
            dve.wait_ge(drawn, 1)

            def sine_argument(b, L, bias):
                arg, turns = sine_rows[0:HY_FF, 0, 0:L], tmp[0:HY_FF, 0, 0:L]
                chain.link(nc.vector.tensor_scalar(arg, k.bank(b, L)[0:HY_FF, :],
                                                   k.vec[0:HY_FF, COL["hy_small"] + bias:COL["hy_small"] + bias + 1],
                                                   k.vec[0:HY_FF, COL["hy_small"] + 2:COL["hy_small"] + 3],
                                                   ALU.add, ALU.mult))
                chain.link(nc.vector.tensor_scalar(turns, arg, 1 / (2 * math.pi), MAGIC, ALU.mult, ALU.add))
                chain.link(nc.vector.tensor_scalar(turns, turns, MAGIC, None, ALU.subtract))
                for part in (TWO_PI_HI, TWO_PI_LO):
                    chain.link(nc.vector.scalar_tensor_tensor(out=arg, in0=turns, scalar=-part, in1=arg,
                                                              op0=ALU.mult, op1=ALU.add))
                nc.vector.tensor_scalar(arg, arg, PI_BELOW, -PI_BELOW, ALU.min, ALU.max).then_inc(drawn, 1)

            def take(ins):
                ins.then_inc(kept, 1)

            for turn, (L, off, n, tab, dec, z, gT) in enumerate(sizes):
                dve.wait_ge(done, group + 1)
                sine_argument(2 * (group % 4), L, 0)
                dve.wait_ge(drawn, 2 * turn + 2)
                nc.vector.sem_inc(kept, 1)
                group += 1
                for a in range(n):
                    dve.wait_ge(done, group + 1)
                    take(nc.vector.tensor_copy(gT[:, a, :], k.bank(2 * (group % 4))))
                    group += 1
                dve.wait_ge(done, group + 1)
                sine_argument(2 * (group % 4), L, 1)
                dve.wait_ge(drawn, 2 * turn + 3)
                nc.vector.sem_inc(kept, 1)
                group += 1
                for a in range(n):
                    dve.wait_ge(done, group + 1)
                    b = 2 * (group % 4)
                    for half in range(2):
                        chain.link(nc.vector.tensor_tensor(tmp[:, half, :], k.bank(b + half), dec[:, a, :], ALU.mult))
                    if a == 0:
                        chain.link(nc.vector.memset(tmp[0:1, 1, :], 0.0))
                    chain.link(nc.vector.tensor_tensor(hsum[:, a, :], tmp[:, 0, :], tmp[:, 1, :], ALU.add))
                    take(nc.vector.tensor_tensor(hdif[:, a, :], tmp[:, 0, :], tmp[:, 1, :], ALU.subtract))
                    dve.wait_ge(kept, group + 1)
                    group += 1
                for f in range(n):
                    dve.wait_ge(done, group + 1)
                    b = 2 * (group % 4)
                    chain.link(nc.vector.tensor_copy(spec[:, f, :], k.bank(b)))
                    take(nc.vector.tensor_copy(spec[:, 4 + f, :], k.bank(b + 1)))
                    group += 1
                dve.wait_ge(kept, group)
                for f in range(n):
                    dve.wait_ge(done, group + 1)
                    b = 2 * (group % 4)
                    re, im = spec[:, f, :], spec[:, 4 + f, :]
                    chain.link(nc.vector.tensor_tensor(tmp[:, 0, :], k.bank(b), re, ALU.mult))
                    chain.link(nc.vector.tensor_tensor(tmp[:, 1, :], k.bank(b + 1), im, ALU.mult))
                    chain.link(nc.vector.tensor_tensor(yspec[:, f, :], tmp[:, 0, :], tmp[:, 1, :], ALU.subtract))
                    chain.link(nc.vector.tensor_tensor(tmp[:, 0, :], k.bank(b), im, ALU.mult))
                    chain.link(nc.vector.tensor_tensor(tmp[:, 1, :], k.bank(b + 1), re, ALU.mult))
                    take(nc.vector.tensor_tensor(yspec[:, 4 + f, :], tmp[:, 0, :], tmp[:, 1, :], ALU.add))
                    dve.wait_ge(kept, group + 1)
                    group += 1
                for c in range(HYT):
                    dve.wait_ge(done, group + 1)
                    g, x0 = u[:, 4 + c, off:off + L], u[:, c, off:off + L]
                    chain.link(nc.vector.scalar_tensor_tensor(out=g, in0=g, scalar=k.col("hy_bias", c),
                                                              in1=k.bank(2 * (group % 4), L), op0=ALU.mult, op1=ALU.add))
                    take(nc.vector.tensor_tensor(x0, g, x0, ALU.mult))
                    group += 1



def project_act(k, weights, dst, func, bias, segs, kt=DT, x=None):
    nc = k.nc
    k.stage()
    x = k.h_pair if x is None else x
    stream = Stream(k, weights, kt * P)
    turns = stream.tiles // 2
    t0 = segs[0][0]
    product, taken = [k.sem("product0"), k.sem("product1")], [k.sem("taken0"), k.sem("taken1")]
    with k.block() as block:
        @block.sync
        def _(sp):
            stream.load(sp)

        @block.tensor
        def _(pe):
            with pe.Fori(0, turns) as i:
                for p in range(2):
                    pe.wait_ge(stream.ready[p], i + 1)
                    pe.wait_ge(taken[p], i + 1)
                    project(k, stream.parts[p], kt, x,
                            lambda s: k.pair(p)[:, segs[s][0]:segs[s][0] + segs[s][1]], segs).then_inc(product[p], 1)

        @block.scalar
        def _(act):
            free_all(act, taken)
            for p in range(2):
                stream.high(act, p, 1)

            def turn(i, last):
                for p in range(2):
                    n = 2 * i + p
                    act.wait_ge(product[p], i + 1)
                    if not last:
                        stream.high(act, p, i + 2)
                    nc.scalar.activation(dst[:, n, :], k.pair(p)[:, t0:T], func,
                                         bias=k.col(bias, n) if bias else 0.0).then_inc(taken[p], 1)

            in_turns(act, turns, turn)

        @block.vector
        def _(dve):
            with dve.Fori(0, turns) as i:
                for p in range(2):
                    stream.low(dve, p, i + 1)


def project_tokens(k, weights, dst, kt, x, token_tiles, width):
    nc = k.nc
    k.stage()
    at = MEM - 3 * kt * width
    raw = k.plain(at, kt, width)
    w = Pair(k, at + kt * width, at + 2 * kt * width, kt, width)
    landed, rounded, ready, product, taken = (k.sem(s) for s in ("landed", "rounded", "ready", "product", "taken"))
    with k.block() as block:
        @block.sync
        def _(sp):
            sp.dma_start(raw, k.dram[weights].rearrange("p (k n) -> p k n", n=width)).then_inc(landed, 16)

        @block.tensor
        def _(pe):
            for j, a in enumerate(token_tiles):
                if j >= 4:
                    pe.wait_ge(taken, j - 3)
                for kk in range(kt):
                    if j == 0:
                        pe.wait_ge(ready, kk + 1)
                    last = three_passes(k, k.bank(j % 4, width), x.tokens(kk, a * P, (a + 1) * P),
                                        w.tokens(kk, 0, width), kk == 0, kk == kt - 1)
                last.then_inc(product, 1)

        @block.scalar
        def _(act):
            act.wait_ge(landed, 16)
            for kk in range(kt):
                nc.scalar.copy(w.high[:, kk, :], raw[:, kk, :]).then_inc(rounded, 1)

        @block.vector
        def _(dve):
            for kk in range(kt):
                dve.wait_ge(rounded, kk + 1)
                nc.vector.tensor_tensor(w.low[:, kk, :], raw[:, kk, :], w.high_plain[:, kk, :],
                                        ALU.subtract).then_inc(ready, 1)
            for j in range(len(token_tiles)):
                dve.wait_ge(product, j + 1)
                nc.vector.tensor_copy(dst[:, j, :], k.bank(j % 4, width)).then_inc(taken, 1)


def log1p_series(k, chain, e, inv, sq, acc):
    nc = k.nc
    chain.link(nc.vector.tensor_scalar(inv, e, 2.0, None, ALU.add))
    chain.link(nc.vector.reciprocal(inv, inv))
    chain.link(nc.vector.tensor_tensor(e, e, inv, ALU.mult))
    chain.link(nc.vector.tensor_tensor(sq, e, e, ALU.mult))
    chain.link(nc.vector.tensor_scalar(acc, sq, 1.0 / ATANH_TERMS[0], None, ALU.mult))
    for n in ATANH_TERMS[1:]:
        chain.link(nc.vector.scalar_tensor_tensor(out=acc, in0=acc, scalar=1.0 / n, in1=sq, op0=ALU.add, op1=ALU.mult))
    chain.link(nc.vector.scalar_tensor_tensor(out=acc, in0=acc, scalar=1.0, in1=e, op0=ALU.add, op1=ALU.mult))


def mlstm_gates(k, c_rows, neg_m, floor):
    nc = k.nc
    k.stage()
    raw, e, inv, sq, acc, gate_in, logf, cum = (k.arena[:, (8 + j) * T:(9 + j) * T] for j in range(8))
    w = k.ring[:, 0:DT * 16]
    landed, product, raw_ready, exp_ready, logs, cleared, moved, summed, absolute = (
        k.sem(s) for s in ("landed", "product", "raw", "exp", "logs", "cleared", "moved", "summed", "absolute"))
    one = k.const("onecol", 1, 63)
    with k.block() as block:
        @block.sync
        def _(sp):
            sp.dma_start(w, k.dram["w_in_gates"]).then_inc(landed, 16)
            sp.wait_ge(cleared, 1)
            sp.wait_ge(logs, 1)
            for d, row in ((0, 0), (1, BWD)):
                sp.dma_start(gate_in[row:row + ML_HEADS, :], raw[8 * d:8 * d + ML_HEADS, :]).then_inc(moved, 16)
                sp.dma_start(logf[row:row + ML_HEADS, :], acc[8 * d + 4:8 * d + 4 + ML_HEADS, :]).then_inc(moved, 16)

        @block.tensor
        def _(pe):
            pe.wait_ge(landed, 16)
            project_few(k, w, lambda s: seg_out(k, 0)(s)[0:16, :], SEGS, 16).then_inc(product, 1)

        @block.scalar
        def _(act):
            act.wait_ge(raw_ready, 1)
            nc.scalar.activation(e[0:16, :], raw[0:16, :], ACT.Abs).then_inc(absolute, 1)
            act.wait_ge(absolute, 1)
            nc.scalar.activation(e[0:16, :], e[0:16, :], ACT.Exp, scale=-1.0).then_inc(exp_ready, 1)
            act.wait_ge(summed, 1)
            nc.scalar.activation(floor, sq[0:ROWS, :], ACT.Exp, scale=-1.0)

        @block.vector
        def _(dve):
            chain = Chain(dve, k.sem("chain"))
            nc.vector.memset(gate_in[0:ROWS, :], 0.0)
            nc.vector.memset(cum[0:ROWS, :], 0.0)
            nc.vector.memset(logf[0:ROWS, :], 0.0).then_inc(cleared, 1)
            dve.wait_ge(product, 1)
            nc.vector.tensor_scalar(raw[0:16, :], k.pair(0)[0:16, :], k.vec[0:16, COL["ml_gate_b"]:COL["ml_gate_b"] + 1],
                                    None, ALU.add).then_inc(raw_ready, 1)
            dve.wait_ge(exp_ready, 1)
            log1p_series(k, chain, e[0:16, :], inv[0:16, :], sq[0:16, :], acc[0:16, :])
            chain.link(nc.vector.tensor_scalar(inv[0:16, :], raw[0:16, :], 0.0, None, ALU.min))
            nc.vector.scalar_tensor_tensor(out=acc[0:16, :], in0=acc[0:16, :], scalar=-2.0, in1=inv[0:16, :],
                                           op0=ALU.mult, op1=ALU.add).then_inc(logs, 1)
            dve.wait_ge(moved, 64)
            fwd, bwd = slice(0, ML_HEADS), slice(BWD, BWD + ML_HEADS)
            runs = ((fwd, slice(0, T), None), (bwd, slice(CTX - 1, None, -1), None), (bwd, slice(T - 1, CTX - 1, -1), 0))

            def scan(out, data, op):
                for rows, span, start in runs:
                    n = CTX if span.start == CTX - 1 else (LAT if start is not None else T)
                    chain.link(nc.vector.tensor_tensor_scan(
                        out[rows, span], k.cst[rows, ONE:ONE + 1].to_broadcast([ML_HEADS, n]), data[rows, span],
                        0.0 if start is None else out[rows, start:start + 1], ALU.mult, op))

            scan(cum, logf, ALU.add)
            chain.link(nc.vector.tensor_tensor(c_rows, gate_in[0:ROWS, :], cum[0:ROWS, :], ALU.subtract))
            chain.link(nc.vector.memset(e[0:ROWS, :], 0.0))
            scan(e, c_rows, ALU.max)
            chain.link(nc.vector.tensor_tensor(sq[0:ROWS, :], e[0:ROWS, :], cum[0:ROWS, :], ALU.add))
            nc.vector.tensor_scalar(neg_m, e[0:ROWS, :], -1.0, None, ALU.mult).then_inc(summed, 1)


def mlstm(k):
    q, key, v, og = k.area(8 * T, 4, T), k.area(12 * T, 4, T), k.area(16 * T, 6, ML_W), k.area(20 * T, 4, T)
    slots = [k.arena[:, 24 * T + j * T:24 * T + (j + 1) * T] for j in range(8)]
    c_rows, neg_m, floor = slots[0][0:ROWS, :], slots[1][0:ROWS, :], k.row[0:ROWS, :]
    mlstm_gates(k, c_rows, neg_m, floor)
    project_conv(k, "w_in_qk", k.area(8 * T, 8, T), "ml_conv_w", None, True)
    project_act(k, "w_in_og", og, ACT.Sigmoid, None, SEGS)
    project_tokens(k, "w_in_v", v, DT, k.h_pair, range(6), ML_W)
    mlstm_core(k, q, key, v, og, c_rows, neg_m, floor, slots)


def mlstm_core(k, q, key, v, og, c_rows, neg_m, floor, slots):
    nc = k.nc
    k.stage()
    flat = k.words(H_LOW_AT, WORK_AT)
    c_col = flat[:, 0:6 * ROWS].rearrange("p (a r) -> p a r", r=ROWS)
    scores = flat[:, T:T + 6 * T].rearrange("p (j t) -> p j t", t=T)
    weights, probs = (slots[3], slots[4]), (slots[5], slots[6])
    bcast = flat[:, 7 * T:15 * T].rearrange("p (r t) -> p r t", t=T)
    num = k.plain(MEM - 8 * T, 8, T)
    recip, sq_rows = slots[7][0:ROWS, :], slots[2][0:ROWS, :]
    squares = (slots[3], slots[4])
    scale = float(P) ** -0.5

    def select(row):
        return k.cst[0:ROWS, CAT["ident"] + row:CAT["ident"] + row + 1].to_broadcast([ROWS, P])

    def one_row(row):
        return k.const("onecol", ROWS, ROWS - 1 - row)

    rows = [(d, h, d * BWD + h) for d in range(2) for h in range(ML_HEADS)]
    units = []
    for h in range(ML_HEADS):
        for j in range(6):
            units.append((h, 0, j, ((j * P, T),), ((j + 1) * P, T)))
        for j in (1, 0, 5, 4, 3, 2):
            if j < 2:
                spans = ((0, (j + 1) * P), (CTX, T)) if j == 0 else ((0, T),)
                units.append((h, 1, j, spans, (0, j * P), (CTX, T)))
            else:
                units.append((h, 1, j, ((CTX, (j + 1) * P),), (CTX, j * P)))

    names = ("c_turned", "c_kept", "row_out", "row_kept", "s_done", "s_kept", "diag", "weighed", "prob", "pv",
             "num_kept", "recip_ready", "norm_out", "norm_taken", "squared", "sum_done", "root", "inverse")
    (c_turned, c_kept, row_out, row_kept, s_done, s_kept, diag, weighed, prob, pv, num_kept, recip_ready, norm_out,
     norm_taken, squared, sum_done, root, inverse) = (k.sem(s) for s in names)

    def pieces(spans):
        out = []
        for a, b in spans:
            for s0, n in SEGS:
                lo, hi = max(a, s0), min(b, s0 + n)
                if lo < hi:
                    out.append((lo, hi))
        return out

    with k.block() as block:
        @block.tensor
        def _(pe):
            for a in range(6):
                last = nc.tensor.transpose(k.bank(0, ROWS, a * ROWS), c_rows[:, a * P:(a + 1) * P],
                                           k.cst[0:ROWS, CAT["ident"]:CAT["ident"] + ROWS])
            last.then_inc(c_turned, 1)
            for n, (d, h, row) in enumerate(rows):
                if n >= 3:
                    pe.wait_ge(row_kept, n - 2)
                for a, w in SEGS:
                    last = nc.tensor.matmul(k.pair(1 + n % 3)[:, a:a + w], select(row), neg_m[:, a:a + w],
                                            start=True, stop=True)
                last.then_inc(row_out, 1)
            pe.wait_ge(row_kept, len(rows))
            pe.wait_ge(c_kept, 1)
            for u, (h, d, j, spans, *off) in enumerate(units):
                if u % 12 == 0:
                    for jj in range(6):
                        m = 6 * h + jj
                        if m >= 2:
                            pe.wait_ge(s_kept, m - 1)
                        for a, b in pieces(((0, T),) if jj < 2 else ((CTX, T),)):
                            last = nc.tensor.matmul(k.pair(m % 2)[:, a:b], key[:, h, jj * P:(jj + 1) * P], q[:, h, a:b],
                                                    start=True, stop=True)
                        last.then_inc(s_done, 1)
                first = u % 6 == 0
                if first and u:
                    pe.wait_ge(num_kept, u // 6)
                pe.wait_ge(prob, u + 1)
                for a, b in pieces(spans):
                    nc.tensor.matmul(k.pair(2)[:, a:b], v[:, j, h * P:(h + 1) * P], probs[u % 2][:, a:b],
                                     start=first, stop=u % 6 == 5, skip_group_check=True)
                    last = nc.tensor.matmul(k.pair(3)[0:ROWS, a:b], one_row(d * BWD + h), probs[u % 2][:, a:b],
                                            start=u == 0, stop=u == len(units) - 1, skip_group_check=True)
                last.then_inc(pv, 1)
            pe.wait_ge(recip_ready, 1)
            for n in range(8):
                h, d = n // 2, n % 2
                if n >= 2:
                    pe.wait_ge(norm_taken, n - 1)
                for a, w in SEGS:
                    last = nc.tensor.matmul(k.pair(n % 2)[:, a:a + w], select(d * BWD + h), recip[:, a:a + w],
                                            start=True, stop=True)
                last.then_inc(norm_out, 1)
            for h in range(ML_HEADS):
                pe.wait_ge(squared, h + 1)
                for a, w in SEGS:
                    last = nc.tensor.matmul(k.pair(2)[0:ROWS, a:a + w], one_row(h), squares[h % 2][:, a:a + w],
                                            start=h == 0, stop=h == ML_HEADS - 1)
                last.then_inc(sum_done, 1)
            pe.wait_ge(inverse, 1)
            for h in range(ML_HEADS):
                n = 8 + h
                pe.wait_ge(norm_taken, n - 1)
                for a, w in SEGS:
                    last = nc.tensor.matmul(k.pair(n % 2)[:, a:a + w], select(h), sq_rows[:, a:a + w],
                                            start=True, stop=True)
                last.then_inc(norm_out, 1)

        @block.scalar
        def _(act):
            for n in range(len(rows)):
                act.wait_ge(row_out, n + 1)
                nc.scalar.copy(bcast[:, n, :], k.pair(1 + n % 3)).then_inc(row_kept, 1)
            act.wait_ge(row_kept, len(rows))
            for u, (h, d, j, spans, *off) in enumerate(units):
                if u % 12 == 0:
                    if u:
                        act.wait_ge(prob, u)
                    for jj in range(6):
                        m = 6 * h + jj
                        act.wait_ge(s_done, m + 1)
                        a = 0 if jj < 2 else CTX
                        nc.scalar.mul(scores[:, jj, a:T], k.pair(m % 2)[:, a:T], scale).then_inc(s_kept, 1)
                act.wait_ge(diag, u + 1)
                w = weights[u % 2]
                last = nc.scalar.activation(w[:, j * P:(j + 1) * P], w[:, j * P:(j + 1) * P], ACT.Exp)
                for a, b in off:
                    if a < b:
                        last = nc.scalar.activation(w[:, a:b], bcast[:, 4 * d + h, a:b], ACT.Exp,
                                                    bias=c_col[:, j, d * BWD + h:d * BWD + h + 1])
                last.then_inc(weighed, 1)
            for h in range(ML_HEADS):
                act.wait_ge(norm_taken, 2 * h + 2)
                if h >= 2:
                    act.wait_ge(sum_done, h - 1)
                nc.scalar.activation(squares[h % 2], num[:, h, :], ACT.Square).then_inc(squared, 1)
            act.wait_ge(sum_done, ML_HEADS)
            nc.scalar.activation(sq_rows, k.pair(2)[0:ROWS, :], ACT.Sqrt, scale=1.0 / P,
                                 bias=k.cst[0:ROWS, CAT["eps"]:CAT["eps"] + 1]).then_inc(root, 1)

        @block.vector
        def _(dve):
            chain = Chain(dve, k.sem("chain"))
            dve.wait_ge(c_turned, 1)
            nc.vector.tensor_copy(c_col, k.bank(0, 6 * ROWS).rearrange("p (a r) -> p a r", r=ROWS)).then_inc(c_kept, 1)
            dve.wait_ge(c_kept, 1)
            dve.wait_ge(row_kept, len(rows))

            def diagonal(u):
                h, d, j = units[u][:3]
                span = slice(j * P, (j + 1) * P)
                nc.vector.tensor_scalar(weights[u % 2][:, span], bcast[:, 4 * d + h, span],
                                        c_col[:, j, d * BWD + h:d * BWD + h + 1], 0.0, ALU.add, ALU.min).then_inc(diag, 1)

            diagonal(0)
            for u, (h, d, j, spans, *off) in enumerate(units):
                if u + 1 < len(units):
                    diagonal(u + 1)
                dve.wait_ge(weighed, u + 1)
                dve.wait_ge(s_kept, 6 * h + 6)
                if u >= 2:
                    dve.wait_ge(pv, u - 1)
                for a, b in spans:
                    chain.link(nc.vector.tensor_tensor(probs[u % 2][:, a:b], scores[:, j, a:b], weights[u % 2][:, a:b],
                                                       ALU.mult))
                span = slice(j * P, (j + 1) * P)
                nc.vector.tensor_tensor(probs[u % 2][:, span], probs[u % 2][:, span],
                                        k.const("s_ge_t" if d else "s_le_t"), ALU.mult).then_inc(prob, 1)
                if u % 6 == 5:
                    dve.wait_ge(pv, u + 1)
                    nc.vector.tensor_copy(num[:, 4 * d + h, :], k.pair(2)).then_inc(num_kept, 1)
            chain.link(nc.vector.tensor_copy(recip, k.pair(3)[0:ROWS, :]))
            chain.link(nc.vector.scalar_tensor_tensor(out=recip, in0=recip, scalar=-1.0, in1=recip, op0=ALU.mult,
                                                      op1=ALU.max))
            chain.link(nc.vector.tensor_tensor(recip, recip, floor, ALU.max))
            nc.vector.reciprocal(recip, recip).then_inc(recip_ready, 1)
            dve.wait_ge(num_kept, 8)
            for n in range(8):
                h, d = n // 2, n % 2
                dve.wait_ge(norm_out, n + 1)
                part = num[:, 4 * d + h, :]
                if d == 0:
                    nc.vector.tensor_tensor(part, part, k.pair(n % 2), ALU.mult).then_inc(norm_taken, 1)
                else:
                    chain.link(nc.vector.tensor_tensor(part, part, k.pair(n % 2), ALU.mult))
                    dve.wait_ge(norm_taken, n)
                    nc.vector.tensor_tensor(num[:, h, :], num[:, h, :], part, ALU.add).then_inc(norm_taken, 1)
            dve.wait_ge(root, 1)
            nc.vector.reciprocal(sq_rows, sq_rows).then_inc(inverse, 1)
            for h in range(ML_HEADS):
                n = 8 + h
                dve.wait_ge(norm_out, n + 1)
                chain.link(nc.vector.scalar_tensor_tensor(out=num[:, h, :], in0=num[:, h, :], scalar=k.col("ml_norm_g", h),
                                                          in1=k.pair(n % 2), op0=ALU.mult, op1=ALU.mult))
                nc.vector.tensor_tensor(k.arena[:, (4 + h) * T:(5 + h) * T], num[:, h, :], og[:, h, :],
                                        ALU.mult).then_inc(norm_taken, 1)



def rotate(k, parts, cos, sin, scratch):
    nc = k.nc
    k.stage()
    partner, summed = k.sem("partner"), k.sem("summed")
    with k.block() as block:
        @block.tensor
        def _(pe):
            for n, x in enumerate(parts):
                if n >= 4:
                    pe.wait_ge(summed, n - 3)
                nc.tensor.matmul(k.bank(n % 4), k.const("rot_gqa"), x, start=True, stop=True).then_inc(partner, 1)

        @block.vector
        def _(dve):
            chain = Chain(dve, k.sem("chain"))
            for n, x in enumerate(parts):
                dve.wait_ge(partner, n + 1)
                chain.link(nc.vector.tensor_tensor(scratch, k.bank(n % 4), sin, ALU.mult))
                chain.link(nc.vector.tensor_tensor(x, x, cos, ALU.mult))
                nc.vector.tensor_tensor(x, x, scratch, ALU.add).then_inc(summed, 1)
                dve.wait_ge(summed, n + 1)


def attention(k, heads, key_segs, scores_of, value_of, out_rows, dst_of, scale):
    nc = k.nc
    k.stage()
    lo = key_segs[0][0]
    width = T - lo
    tiles = width // P
    probs = [k.ring[:, b * T:b * T + width] for b in range(2)]
    turned = [k.ring[:, 2 * T + b * tiles * LAT:2 * T + (b + 1) * tiles * LAT].rearrange("p (a t) -> p a t", t=LAT)
              for b in range(2)]
    stats = k.row[:, 0:32].rearrange("p (b c) -> p b c", c=4)
    units = [(h, a) for h in range(heads) for a in range(4)]
    names = ("scored", "peak", "raised", "normed", "t_done", "t_kept", "o_done", "o_kept")
    scored, peak, raised, normed, t_done, t_kept, o_done, o_kept = (k.sem(s) for s in names)
    with k.block() as block:
        @block.tensor
        def _(pe):
            def score(u):
                if u >= 2:
                    pe.wait_ge(raised, u - 1)
                terms = scores_of(*units[u])
                for t0, n in key_segs:
                    for m, (queries, keys) in enumerate(terms):
                        last = nc.tensor.matmul(k.pair(u % 2)[:, t0:t0 + n], queries, keys[:, t0:t0 + n], start=m == 0,
                                                stop=m == len(terms) - 1)
                last.then_inc(scored, 1)

            score(0)
            for u, (h, a) in enumerate(units):
                if u + 1 < len(units):
                    score(u + 1)
                pe.wait_ge(normed, u + 1)
                if u:
                    pe.wait_ge(t_kept, u)
                for b in range(tiles):
                    last = nc.tensor.transpose(k.pair(2)[:, lo + b * P:lo + (b + 1) * P], probs[u % 2][:, b * P:(b + 1) * P],
                                               k.const("ident"))
                last.then_inc(t_done, 1)
                if a == 3:
                    pe.wait_ge(t_kept, u + 1)
                    if h >= 2:
                        pe.wait_ge(o_kept, h - 1)
                    for b in range(tiles):
                        last = nc.tensor.matmul(k.bank(6 + h % 2)[out_rows(h), :], value_of(h, b), turned[h % 2][:, b, :],
                                                start=b == 0, stop=b == tiles - 1)
                    last.then_inc(o_done, 1)

        @block.vector
        def _(dve):
            chain = Chain(dve, k.sem("chain"))

            def find_peak(u):
                dve.wait_ge(scored, u + 1)
                b = u % 8
                chain.link(nc.vector.tensor_reduce(stats[:, b, 0:1], k.pair(u % 2)[:, lo:T], AX.X, ALU.max))
                nc.vector.tensor_scalar(stats[:, b, 1:2], stats[:, b, 0:1], -scale, None, ALU.mult).then_inc(peak, 1)

            find_peak(0)
            for u in range(len(units)):
                if u + 1 < len(units):
                    find_peak(u + 1)
                dve.wait_ge(raised, u + 1)
                b = u % 8
                chain.link(nc.vector.reciprocal(stats[:, b, 3:4], stats[:, b, 2:3]))
                nc.vector.tensor_scalar(probs[u % 2], probs[u % 2], stats[:, b, 3:4], None, ALU.mult).then_inc(normed, 1)

        @block.scalar
        def _(act):
            def raise_(u):
                act.wait_ge(peak, u + 1)
                if u >= 2:
                    act.wait_ge(t_done, u - 1)
                nc.scalar.activation(probs[u % 2], k.pair(u % 2)[:, lo:T], ACT.Exp, scale=scale,
                                     bias=stats[:, u % 8, 1:2], accum_out=stats[:, u % 8, 2:3]).then_inc(raised, 1)

            raise_(0)
            for u, (h, a) in enumerate(units):
                if u + 1 < len(units):
                    raise_(u + 1)
                act.wait_ge(t_done, u + 1)
                if h >= 2:
                    act.wait_ge(o_done, h - 1)
                nc.scalar.copy(turned[h % 2][:, :, a * P:(a + 1) * P],
                               k.pair(2)[:, lo:T].rearrange("p (b q) -> p b q", q=P)).then_inc(t_kept, 1)
                if a == 3:
                    act.wait_ge(o_done, h + 1)
                    nc.scalar.copy(dst_of(h), k.bank(6 + h % 2)[out_rows(h), :]).then_inc(o_kept, 1)


def load(k, pairs):
    nc = k.nc
    k.stage()
    landed = k.sem("landed")
    with k.block() as block:
        @block.sync
        def _(sp):
            for dst, name in pairs:
                sp.dma_start(dst, k.dram[name]).then_inc(landed, 16)
            sp.wait_ge(landed, 16 * len(pairs))


def mla(k):
    low = k.area(0, 6, T)
    qn, kn = k.area(6 * T, 8, LAT), k.area(6 * T + 4096, 8, T)
    v = k.area(6 * T + 4096 + 8 * T, 6, D)
    at = 6 * T + 4096 + 14 * T + 6 * (D - T)
    qr = k.area(at, 4, LAT)
    cos, sin, scratch = (k.arena[:, at + 2048 + j * LAT:at + 2048 + (j + 1) * LAT] for j in range(3))
    load(k, ((cos, "rope_cos"), (sin, "rope_sin")))
    project_act(k, "mla_w_down", low, ACT.Identity, None, SEGS)
    normalise(k, lambda n, c: k.col("mla_q_norm", n), None, SEG_LAT, low, low, kt=3, root_of=Q_RANK)
    normalise(k, lambda n, c: k.col("mla_kv_norm", n), None, SEGS, low[:, 3:5, :], low[:, 3:5, :], kt=2, root_of=KV_RANK)
    qa = Pair(k, H_HIGH_AT, WORK_AT, 3, T)
    kva = Pair(k, H_HIGH_AT + 3 * T, WORK_AT + 3 * T, 2, T)
    split(k, whole_tiles(qa, [low[:, n, CTX:T] for n in range(3)], CTX) + whole_tiles(kva, [low[:, 3 + n, :] for n in range(2)]))
    project_act(k, "mla_w_qn", qn, ACT.Identity, None, SEG_LAT, 3, qa)
    project_act(k, "mla_w_qr", qr, ACT.Identity, None, SEG_LAT, 3, qa)
    project_act(k, "mla_w_kn", kn, ACT.Identity, None, SEGS, 2, kva)
    for half in range(2):
        project_tokens(k, f"mla_w_v{half}", v[:, :, half * 512:(half + 1) * 512], 2, kva, range(6), 512)
    rotate(k, [qr[:, n, :] for n in range(4)] + [low[:, 5, CTX:T]], cos, sin, scratch)

    def scores_of(h, a):
        half = slice(64 * (h % 2), 64 * (h % 2) + 64)
        return ((qn[:, h, a * P:(a + 1) * P], kn[:, h, :]), (qr[half, h // 2, a * P:(a + 1) * P], low[half, 5, :]))

    attention(k, MLA_HEADS, SEGS, scores_of, lambda h, b: v[:, b, h * P:(h + 1) * P], lambda h: slice(0, P),
              lambda h: k.h[:, h, CTX:T], MLA_SCALE)
    split(k, whole_tiles(k.h_pair, [k.h[:, n, CTX:T] for n in range(DT)], CTX))
    project_residual(k, "mla_w_o", k.h_pair, 2, SEG_LAT, k.mod_next)


def normalise_heads(k, x, gain_col, squares, roots):
    nc = k.nc
    k.stage()
    n_tiles = x.shape[1]
    squared, summed, root, inverse, normed = (k.sem(s) for s in ("squared", "summed", "root", "inverse", "normed"))
    with k.block() as block:
        @block.tensor
        def _(pe):
            for n in range(n_tiles):
                pe.wait_ge(squared, n + 1)
                nc.tensor.matmul(k.bank(n), k.const("ones64"), squares[n % 2], start=True, stop=True).then_inc(summed, 1)

        @block.scalar
        def _(act):
            for n in range(n_tiles):
                if n >= 2:
                    act.wait_ge(summed, n - 1)
                nc.scalar.activation(squares[n % 2], x[:, n, :], ACT.Square).then_inc(squared, 1)
            for n in range(n_tiles):
                act.wait_ge(summed, n + 1)
                if n >= 2:
                    act.wait_ge(normed, n - 1)
                nc.scalar.activation(roots[n % 2], k.bank(n), ACT.Sqrt, scale=1.0 / 64, bias=k.const("eps")).then_inc(root, 1)

        @block.vector
        def _(dve):
            for n in range(n_tiles):
                dve.wait_ge(root, n + 1)
                nc.vector.reciprocal(roots[n % 2], roots[n % 2]).then_inc(inverse, 1)
                dve.wait_ge(inverse, n + 1)
                nc.vector.scalar_tensor_tensor(out=x[:, n, :], in0=x[:, n, :], scalar=gain_col(n), in1=roots[n % 2],
                                               op0=ALU.mult, op1=ALU.mult).then_inc(normed, 1)


def ssd_rows(k, sums, step, decay):
    nc = k.nc
    k.stage()
    raw, e, inv, sq, acc = (k.ring[:, 2048 + j * LAT:2048 + (j + 1) * LAT] for j in range(5))
    w = k.ring[:, 0:DT * 16]
    r16 = slice(0, 16)
    cols = k.vec[r16, COL["ssd_rows"]:COL["ssd_rows"] + 2]
    names = ("landed", "product", "raw_ready", "absolute", "exp_ready", "rates", "steps", "cleared", "moved", "negated")
    landed, product, raw_ready, absolute, exp_ready, rates, steps, cleared, moved, negated = (k.sem(s) for s in names)
    with k.block() as block:
        @block.sync
        def _(sp):
            sp.dma_start(w, k.dram["w_in_dt"]).then_inc(landed, 16)
            sp.wait_ge(cleared, 1)
            sp.wait_ge(steps, 2)
            for d, row in ((0, 0), (1, BWD)):
                sp.dma_start(step[row:row + SSD_HEADS, :], acc[8 * d:8 * d + 8, :]).then_inc(moved, 16)
                sp.dma_start(decay[row:row + SSD_HEADS, :], sq[8 * d:8 * d + 8, :]).then_inc(moved, 16)

        @block.tensor
        def _(pe):
            pe.wait_ge(landed, 16)
            project_few(k, w, lambda s: k.bank(0)[r16, :], SEG_LAT, 16).then_inc(product, 1)

        @block.scalar
        def _(act):
            act.wait_ge(raw_ready, 1)
            nc.scalar.activation(e[r16, :], raw[r16, :], ACT.Abs).then_inc(absolute, 1)
            act.wait_ge(absolute, 1)
            nc.scalar.activation(e[r16, :], e[r16, :], ACT.Exp, scale=-1.0).then_inc(exp_ready, 1)
            nc.scalar.activation(k.row[r16, 0:1], cols[:, 1:2], ACT.Exp).then_inc(rates, 1)

        @block.vector
        def _(dve):
            chain = Chain(dve, k.sem("chain"))
            for j in range(4):
                chain.link(nc.vector.memset(sums[j], 0.0))
            chain.link(nc.vector.memset(step, 0.0))
            nc.vector.memset(decay, 0.0).then_inc(cleared, 1)
            dve.wait_ge(product, 1)
            nc.vector.tensor_scalar(raw[r16, :], k.bank(0)[r16, :], cols[:, 0:1], None, ALU.add).then_inc(raw_ready, 1)
            dve.wait_ge(exp_ready, 1)
            log1p_series(k, chain, e[r16, :], inv[r16, :], sq[r16, :], acc[r16, :])
            chain.link(nc.vector.tensor_scalar(inv[r16, :], raw[r16, :], 0.0, None, ALU.max))
            nc.vector.scalar_tensor_tensor(out=acc[r16, :], in0=acc[r16, :], scalar=2.0, in1=inv[r16, :], op0=ALU.mult,
                                           op1=ALU.add).then_inc(steps, 1)
            dve.wait_ge(steps, 1)
            dve.wait_ge(rates, 1)
            nc.vector.tensor_scalar(sq[r16, :], acc[r16, :], k.row[r16, 0:1], -1.0, ALU.mult, ALU.mult).then_inc(steps, 1)
            dve.wait_ge(moved, 64)
            for j in range(4):
                for row, span, n in ((0, slice(j * P, LAT), LAT - j * P),
                                     (BWD, slice((j + 1) * P - 1, None, -1), (j + 1) * P)):
                    rows = slice(row, row + SSD_HEADS)
                    chain.link(nc.vector.tensor_tensor_scan(
                        sums[j][rows, span], k.cst[rows, ONE:ONE + 1].to_broadcast([SSD_HEADS, n]),
                        decay[rows, span], 0.0, ALU.mult, ALU.add))


def ssd_core(k, xbc, xs, sums, step, work, y):
    nc = k.nc
    k.stage()
    cb = k.ring[:, 0:8 * LAT].rearrange("p (u t) -> p u t", t=LAT)
    weights = [k.ring[:, (8 + b) * LAT:(9 + b) * LAT] for b in range(2)]
    probs = [k.ring[:, (10 + b) * LAT:(11 + b) * LAT] for b in range(2)]
    back = [k.ring[:, 12 * LAT + b * P:12 * LAT + (b + 1) * P] for b in range(2)]
    neg = k.ring[:, 12 * LAT + 256:12 * LAT + 512].rearrange("p (j r) -> p j r", r=ROWS)
    dt = k.ring[:, 12 * LAT + 512:12 * LAT + 768].rearrange("p (j r) -> p j r", r=ROWS)

    def select(row):
        return k.cst[0:ROWS, CAT["ident"] + row:CAT["ident"] + row + 1].to_broadcast([ROWS, P])

    units = [(h, j) for h in range(SSD_HEADS) for j in range(4)]
    names = ("prep", "prep_kept", "spread", "diag", "weighed", "prob", "pv", "y_kept")
    prep, prep_kept, spread, diag, weighed, prob, pv, y_kept = (k.sem(s) for s in names)
    n_prep = 4 + 2 + 8
    with k.block() as block:
        @block.tensor
        def _(pe):
            g = 0

            def begin():
                if g >= 4:
                    pe.wait_ge(prep_kept, g - 3)
                return k.bank(g % 4)
            for a in range(4):
                b = begin()
                for c in range(4):
                    last = nc.tensor.transpose(b[:, c * P:(c + 1) * P], xbc[:, c, a * P:(a + 1) * P], k.const("ident"))
                last.then_inc(prep, 1)
                g += 1
            ident64 = k.cst[0:ROWS, CAT["ident"]:CAT["ident"] + ROWS]
            for src in (lambda j: sums[j], lambda j: step):
                b = begin()
                for j in range(4):
                    last = nc.tensor.transpose(b[:, j * ROWS:(j + 1) * ROWS], src(j)[:, j * P:(j + 1) * P], ident64)
                last.then_inc(prep, 1)
                g += 1
            for grp in range(2):
                rows = slice(64 * grp, 64 * grp + 64)
                for j in range(4):
                    b = begin()
                    nc.tensor.matmul(b, xbc[rows, 4, j * P:(j + 1) * P], xbc[rows, 5, :], start=True,
                                     stop=True).then_inc(prep, 1)
                    g += 1
            pe.wait_ge(prep_kept, n_prep)

            def spread_rows(u):
                h, j = units[u]
                if u >= 2:
                    pe.wait_ge(weighed, u - 1)
                a, b = k.bank(2 * (u % 2)), k.bank(2 * (u % 2) + 1)
                if j:
                    nc.tensor.matmul(a[:, 0:j * P], select(BWD + h), sums[j][:, 0:j * P], start=True, stop=True)
                nc.tensor.matmul(a[:, j * P:LAT], select(h), sums[j][:, j * P:LAT], start=True, stop=True)
                nc.tensor.matmul(b[:, 0:P], select(BWD + h), sums[j][:, j * P:(j + 1) * P], start=True,
                                 stop=True).then_inc(spread, 1)

            spread_rows(0)
            for u, (h, j) in enumerate(units):
                if u + 1 < len(units):
                    spread_rows(u + 1)
                pe.wait_ge(prob, u + 1)
                if j == 0 and h >= 4:
                    pe.wait_ge(y_kept, h - 3)
                rows = slice(64 * (h % 2), 64 * (h % 2) + 64)
                nc.tensor.matmul(k.bank(4 + h % 4)[rows, :], xs[:, j, h * 64:(h + 1) * 64], probs[u % 2], start=j == 0,
                                 stop=j == 3).then_inc(pv, 1)

        @block.scalar
        def _(act):
            act.wait_ge(prep_kept, n_prep)
            for u, (h, j) in enumerate(units):
                act.wait_ge(diag, u + 1)
                w, a = weights[u % 2], k.bank(2 * (u % 2))
                nc.scalar.activation(back[u % 2], back[u % 2], ACT.Exp)
                last = nc.scalar.activation(w[:, j * P:(j + 1) * P], w[:, j * P:(j + 1) * P], ACT.Exp)
                if j:
                    last = nc.scalar.activation(w[:, 0:j * P], a[:, 0:j * P], ACT.Exp,
                                                bias=neg[:, j, BWD + h:BWD + h + 1])
                if j < 3:
                    last = nc.scalar.activation(w[:, (j + 1) * P:LAT], a[:, (j + 1) * P:LAT], ACT.Exp,
                                                bias=neg[:, j, h:h + 1])
                last.then_inc(weighed, 1)

        @block.vector
        def _(dve):
            chain = Chain(dve, k.sem("chain"))
            g = 0
            for a in range(4):
                dve.wait_ge(prep, g + 1)
                nc.vector.tensor_copy(xs[:, a, :], k.bank(g % 4)).then_inc(prep_kept, 1)
                g += 1
            dve.wait_ge(prep, g + 1)
            nc.vector.tensor_scalar(neg, k.bank(g % 4, 4 * ROWS).rearrange("p (j r) -> p j r", r=ROWS), -1.0, None,
                                    ALU.mult).then_inc(prep_kept, 1)
            g += 1
            dve.wait_ge(prep, g + 1)
            nc.vector.tensor_copy(dt, k.bank(g % 4, 4 * ROWS).rearrange("p (j r) -> p j r", r=ROWS)).then_inc(prep_kept, 1)
            g += 1
            for n in range(8):
                dve.wait_ge(prep, g + 1)
                nc.vector.tensor_copy(cb[:, n, :], k.bank(g % 4)).then_inc(prep_kept, 1)
                g += 1
            dve.wait_ge(prep_kept, n_prep)

            def diagonal(u):
                h, j = units[u]
                dve.wait_ge(spread, u + 1)
                span = slice(j * P, (j + 1) * P)
                nc.vector.tensor_scalar(weights[u % 2][:, span], k.bank(2 * (u % 2))[:, span], neg[:, j, h:h + 1], 0.0,
                                        ALU.add, ALU.min)
                nc.vector.tensor_scalar(back[u % 2], k.bank(2 * (u % 2) + 1)[:, 0:P], neg[:, j, BWD + h:BWD + h + 1], 0.0,
                                        ALU.add, ALU.min).then_inc(diag, 1)

            diagonal(0)
            for u, (h, j) in enumerate(units):
                if u + 1 < len(units):
                    diagonal(u + 1)
                dve.wait_ge(weighed, u + 1)
                if u >= 2:
                    dve.wait_ge(pv, u - 1)
                w, p, c = weights[u % 2], probs[u % 2], cb[:, 4 * (h // 4) + j, :]
                f, b = dt[:, j, h:h + 1], dt[:, j, BWD + h:BWD + h + 1]
                span = slice(j * P, (j + 1) * P)
                if j:
                    nc.vector.scalar_tensor_tensor(out=p[:, 0:j * P], in0=w[:, 0:j * P], scalar=b, in1=c[:, 0:j * P],
                                                   op0=ALU.mult, op1=ALU.mult)
                if j < 3:
                    nc.vector.scalar_tensor_tensor(out=p[:, (j + 1) * P:LAT], in0=w[:, (j + 1) * P:LAT], scalar=f,
                                                   in1=c[:, (j + 1) * P:LAT], op0=ALU.mult, op1=ALU.mult)
                chain.link(nc.vector.scalar_tensor_tensor(out=w[:, span], in0=w[:, span], scalar=f, in1=k.const("s_le_t"),
                                                          op0=ALU.mult, op1=ALU.mult))
                chain.link(nc.vector.scalar_tensor_tensor(out=back[u % 2], in0=back[u % 2], scalar=b,
                                                          in1=k.const("s_ge_t"), op0=ALU.mult, op1=ALU.mult))
                chain.link(nc.vector.tensor_tensor(w[:, span], w[:, span], back[u % 2], ALU.add))
                nc.vector.tensor_tensor(p[:, span], w[:, span], c[:, span], ALU.mult).then_inc(prob, 1)
                if j == 3:
                    dve.wait_ge(pv, u + 1)
                    rows = slice(64 * (h % 2), 64 * (h % 2) + 64)
                    nc.vector.scalar_tensor_tensor(out=y[rows, h // 2, :], in0=xbc[rows, h // 2, :],
                                                   scalar=k.vec[rows, COL["d_skip"] + h // 2:COL["d_skip"] + h // 2 + 1],
                                                   in1=k.bank(4 + h % 4)[rows, :], op0=ALU.mult,
                                                   op1=ALU.add).then_inc(y_kept, 1)


def multiply(k, pairs):
    nc = k.nc
    k.stage()
    with k.block() as block:
        @block.vector
        def _(dve):
            for x, y in pairs:
                nc.vector.tensor_tensor(x, x, y, ALU.mult)


def merge(k, attn, ssd, gates, dst):
    nc = k.nc
    k.stage()
    stream = Stream(k, "w_merge", D)
    scratch = [k.arena[:, stream.at - (b + 1) * LAT:stream.at - b * LAT] for b in range(2)]
    product, taken = [k.sem("product0"), k.sem("product1")], [k.sem("taken0"), k.sem("taken1")]
    with k.block() as block:
        @block.sync
        def _(sp):
            stream.load(sp)

        @block.tensor
        def _(pe):
            with pe.Fori(0, stream.tiles // 2) as i:
                for p in range(2):
                    pe.wait_ge(stream.ready[p], i + 1)
                    pe.wait_ge(taken[p], i + 1)
                    for half, x in enumerate((attn, ssd)):
                        last = project(k, [w[:, half * 512:(half + 1) * 512] for w in stream.parts[p]], 4, x,
                                       lambda s: k.bank(2 * p + half), ((0, LAT),))
                    last.then_inc(product[p], 1)

        @block.scalar
        def _(act):
            for p in range(2):
                stream.high(act, p, 1)
            with act.Fori(0, stream.tiles // 2 - 1) as i:
                for p in range(2):
                    act.wait_ge(product[p], i + 1)
                    stream.high(act, p, i + 2)

        @block.vector
        def _(dve):
            chain = Chain(dve, k.sem("chain"))
            free_all(dve, taken)
            for p in range(2):
                stream.low(dve, p, 1)

            def turn(i, last):
                chain.turn(i, 4)
                for p in range(2):
                    n = 2 * i + p
                    dve.wait_ge(product[p], i + 1)
                    if not last:
                        stream.low(dve, p, i + 2)
                    chain.link(nc.vector.tensor_tensor(scratch[0], k.bank(2 * p), gates[:, n, :], ALU.mult))
                    chain.link(nc.vector.tensor_tensor(scratch[1], k.bank(2 * p + 1), gates[:, n + DT, :], ALU.mult))
                    nc.vector.tensor_tensor(dst[:, n, CTX:T], scratch[0], scratch[1], ALU.add).then_inc(taken[p], 1)
                    dve.wait_ge(taken[p], i + 2)

            in_turns(dve, stream.tiles // 2, turn)


def second_mixer(k):
    qk, z, xbc = k.area(0, 6, LAT), k.area(3072, 4, LAT), k.area(5120, 6, LAT)
    gates, v, xs = k.area(8192, 16, LAT), k.area(16384, 4, P), k.area(16896, 4, 512)
    attn, y = k.area(18944, 4, LAT), k.area(20992, 4, LAT)
    cos, sin, scratch = (k.arena[:, 23040 + j * LAT:23040 + (j + 1) * LAT] for j in range(3))
    sums = [k.arena[0:ROWS, j * LAT:(j + 1) * LAT] for j in range(4)]
    step, decay = k.arena[0:ROWS, 2048:2560], k.arena[0:ROWS, 2560:3072]
    load(k, ((cos, "rope_cos"), (sin, "rope_sin")))
    project_act(k, "w_qk_2", qk, ACT.Identity, None, SEG_LAT)
    project_act(k, "w_z_2", z, ACT.Silu, None, SEG_LAT)
    project_act(k, "w_gates_2", gates, ACT.Sigmoid, "b_gate_2", SEG_LAT)
    project_conv(k, "w_xbc_2", xbc, "conv_w_2", "conv_b_2", True, 7, SEG_LAT)
    project_tokens(k, "w_v_2", v, DT, k.h_pair, range(2, 6), P)
    ring = [k.ring[:, j * LAT:(j + 1) * LAT] for j in range(4)]
    normalise_heads(k, qk, lambda n: k.col("qk_norm_2", 0 if n < 4 else 1), ring[0:2], ring[2:4])
    rotate(k, [qk[:, n, :] for n in range(6)], cos, sin, scratch)

    def half(h):
        return slice(64 * (h % 2), 64 * (h % 2) + 64)

    def shifted(n, rows):
        at = n * LAT - CTX
        return _Tokens(k.arena, rows, at)

    attention(k, SSD_HEADS, SEG_LAT,
              lambda h, a: ((qk[half(h), h // 2, a * P:(a + 1) * P], shifted(4 + h // 4, half(h))),),
              lambda h, b: v[:, b, (h // 4) * 64:(h // 4) * 64 + 64], half, lambda h: attn[half(h), h // 2, :], 0.125)
    ssd_rows(k, sums, step, decay)
    ssd_core(k, xbc, xs, sums, step, None, y)
    multiply(k, [(y[:, n, :], z[:, n, :]) for n in range(4)])
    y_all = _Tiles(y)
    normalise(k, lambda n, c: k.col("ssd_norm_w_2", n), None, SEG_LAT, y_all, y_all, kt=4, root_of=512)
    attn_pair, y_pair = Pair(k, WORK_AT, WORK_AT + 18944, 4, LAT), Pair(k, WORK_AT + 3072, WORK_AT + 20992, 4, LAT)
    split(k, whole_tiles(attn_pair, [attn[:, n, :] for n in range(4)]) + whole_tiles(y_pair, [y[:, n, :] for n in range(4)]))
    merge(k, attn_pair, y_pair, gates, k.h)
    split(k, whole_tiles(k.h_pair, [k.h[:, n, CTX:T] for n in range(DT)], CTX))
    project_residual(k, "w_out_2", k.h_pair, None, SEG_LAT)


class _Tokens:

    def __init__(self, mem, rows, at):
        self.mem, self.rows, self.at = mem, rows, at

    def __getitem__(self, key):
        _, t = key
        return self.mem[self.rows, self.at + t.start:self.at + t.stop]


class _Tiles:

    def __init__(self, x):
        self.x = x

    def __getitem__(self, key):
        rows, n, t = key
        return self.x[rows, n, t.start - CTX:t.stop - CTX]


def route(k, spread_to):
    nc = k.nc
    k.stage()
    w = k.ring[:, 0:DT * 20]
    at = [20 * DT]

    def room(*shape):
        n = int(np.prod(shape))
        a = k.ring[:, at[0]:at[0] + n]
        at[0] += n
        if len(shape) == 2:
            return a.rearrange("p (a b) -> p a b", b=shape[1])
        return a.rearrange("p (a g e) -> p a g e", g=shape[1], e=shape[2]) if len(shape) == 3 else a

    logits, g_top, g_exp, g_sum, g_hot = room(4, 20), room(4), room(4, 4), room(4), room(4, 4)
    mixed, fine, top1, hot1, rest, top2, hot2 = room(4, 4, 4), room(4, 4), room(4), room(4, 4), room(4, 4), room(4), room(4, 4)
    gap, p1, p2, rank, best, comb = room(4), room(4), room(4), room(4, 4), room(4), room(4, 4, 4)
    rows = k.row[0:N_EXPERTS, 0:LAT]
    names = ("landed", "logit", "spaced", "raised", "turned", "rows_kept", "spread", "spread_kept")
    landed, logit, spaced, raised, turned, rows_kept, spread, spread_kept = (k.sem(s) for s in names)

    def over(a, shape=(P, 4, 4)):
        return a.unsqueeze(2).to_broadcast(list(shape))

    with k.block() as block:
        @block.sync
        def _(sp):
            sp.dma_start(w, k.dram["w_router"]).then_inc(landed, 16)

        @block.tensor
        def _(pe):
            pe.wait_ge(landed, 16)
            for a in range(4):
                for kk in range(DT):
                    for part, x in enumerate((k.h_pair.high_plain, k.h_pair.low_plain)):
                        last = nc.tensor.matmul(k.bank(0, 20, 20 * a), x[:, kk, CTX + a * P:CTX + (a + 1) * P],
                                                w[:, kk * 20:(kk + 1) * 20], start=kk == 0 and part == 0,
                                                stop=kk == DT - 1 and part == 1)
            last.then_inc(logit, 1)
            pe.wait_ge(turned, 1)
            flat = comb.rearrange("p a g e -> p a (g e)")
            for a in range(4):
                last = nc.tensor.transpose(k.bank(1, P, a * P)[0:N_EXPERTS, :], flat[:, a, :], k.const("ident"))
            last.then_inc(spread, 1)
            pe.wait_ge(rows_kept, 1)
            for e in range(N_EXPERTS):
                if e >= 4:
                    pe.wait_ge(spread_kept, e - 3)
                nc.tensor.matmul(k.bank(4 + e % 4), k.cst[0:N_EXPERTS, CAT["ident"] + e:CAT["ident"] + e + 1].to_broadcast(
                    [N_EXPERTS, P]), rows, start=True, stop=True).then_inc(spread, 1)

        @block.scalar
        def _(act):
            act.wait_ge(spaced, 1)
            nc.scalar.activation(g_exp, g_exp, ACT.Exp).then_inc(raised, 1)
            act.wait_ge(spaced, 2)
            nc.scalar.activation(gap, gap, ACT.Exp).then_inc(raised, 1)
            for e in range(N_EXPERTS):
                act.wait_ge(spread, e + 2)
                nc.scalar.copy(spread_to[:, e, :], k.bank(4 + e % 4)).then_inc(spread_kept, 1)

        @block.vector
        def _(dve):
            chain = Chain(dve, k.sem("chain"))
            V, link = nc.vector, chain.link
            first = k.const("first").unsqueeze(1).to_broadcast([P, 4, 4])

            def one_hot(out, values, top):
                link(V.tensor_reduce(top, values, AX.X, ALU.max))
                link(V.tensor_tensor(rank, values, over(top), ALU.is_equal))
                link(V.tensor_tensor(rank, rank, first, ALU.mult))
                link(V.tensor_reduce(best, rank, AX.X, ALU.max))
                link(V.tensor_tensor(out, rank, over(best), ALU.is_equal))

            dve.wait_ge(logit, 1)
            bias = k.vec[:, COL["b_router"]:COL["b_router"] + 20].unsqueeze(1).to_broadcast([P, 4, 20])
            link(V.tensor_tensor(logits, k.bank(0, 80).rearrange("p (a n) -> p a n", n=20), bias, ALU.add))
            groups = logits[:, :, 0:4]
            one_hot(g_hot, groups, g_top)
            V.tensor_tensor(g_exp, groups, over(g_top), ALU.subtract).then_inc(spaced, 1)
            link(V.tensor_tensor(mixed, logits[:, :, 4:20].rearrange("p a (g e) -> p a g e", e=4),
                                 g_hot.unsqueeze(3).to_broadcast([P, 4, 4, 4]), ALU.mult))
            link(V.tensor_reduce(fine, mixed.rearrange("p a g e -> p a e g"), AX.X, ALU.add))
            one_hot(hot1, fine, top1)
            link(V.scalar_tensor_tensor(out=rest, in0=hot1, scalar=-3.0e38, in1=fine, op0=ALU.mult, op1=ALU.add))
            one_hot(hot2, rest, top2)
            V.tensor_tensor(gap, top2, top1, ALU.subtract).then_inc(spaced, 1)
            dve.wait_ge(raised, 1)
            link(V.tensor_reduce(g_sum, g_exp, AX.X, ALU.add))
            dve.wait_ge(raised, 2)
            link(V.tensor_scalar(p1, gap, 1.0, None, ALU.add))
            link(V.tensor_tensor(p1, p1, g_sum, ALU.mult))
            link(V.reciprocal(p1, p1))
            link(V.tensor_tensor(p2, p1, gap, ALU.mult))
            link(V.tensor_tensor(hot1, hot1, over(p1), ALU.mult))
            link(V.tensor_tensor(hot2, hot2, over(p2), ALU.mult))
            link(V.tensor_tensor(hot1, hot1, hot2, ALU.add))
            V.tensor_tensor(comb, g_hot.unsqueeze(3).to_broadcast([P, 4, 4, 4]),
                            hot1.unsqueeze(2).to_broadcast([P, 4, 4, 4]), ALU.mult).then_inc(turned, 1)
            dve.wait_ge(spread, 1)
            V.tensor_copy(rows, k.bank(1)[0:N_EXPERTS, :]).then_inc(rows_kept, 1)


def experts(k):
    share = k.area(0, N_EXPERTS, LAT)
    route(k, share)
    nc = k.nc
    k.stage()
    stream = Stream(k, "moe", 2 * D)
    at = WORK_AT + N_EXPERTS * LAT
    inner = [Pair(k, at + b * 4 * LAT, at + (2 + b) * 4 * LAT, 4, LAT) for b in range(2)]
    up, silu, rounded, gated = ([k.sem(f"{s}{q}") for q in range(2)] for s in ("up", "silu", "rounded", "gated"))
    down, added = ([k.sem(f"{s}{q}") for q in range(4)] for s in ("down", "added"))
    weighted = k.sem("weighted")
    UP, DOWN = 0, 1

    def walk(engine, step):
        for f in range(4):
            step(UP, 0, f, 0, f % 2, f // 2 + 1)

        def expert(e, b, loads):
            for c, (kind, idx) in enumerate(((UP, 0), (DOWN, 0), (UP, 1), (DOWN, 1), (UP, 2), (UP, 3))):
                step(kind, e if kind == UP else e - 1, idx, b if kind == UP else 1 - b, c % 2, loads + c // 2 + 1)

        with engine.Fori(0, N_EXPERTS // 2 - 1) as i:
            expert(2 * i + 1, 1, 6 * i + 2)
            expert(2 * i + 2, 0, 6 * i + 5)
        expert(N_EXPERTS - 1, 1, 3 * N_EXPERTS - 4)
        for c in range(2):
            step(DOWN, N_EXPERTS - 1, c, 1, c, 3 * N_EXPERTS)

    with k.block() as block:
        @block.sync
        def _(sp):
            stream.load(sp)

        @block.tensor
        def _(pe):
            def step(kind, e, idx, b, slot, loads):
                pe.wait_ge(stream.ready[slot], loads)
                if kind == UP:
                    q = idx % 2
                    pe.wait_ge(gated[q], 2 * e + idx // 2 + 1)
                    for half in range(2):
                        last = project(k, stream.parts[slot], DT, k.h_pair, lambda s: k.bank(2 * q + half), SEG_LAT,
                                       col=half * P, width=2 * P)
                    last.then_inc(up[q], 1)
                else:
                    if idx == 0:
                        for q in range(2):
                            pe.wait_ge(gated[q], 2 * e + 3)
                    for j in range(4):
                        pe.wait_ge(added[j], 2 * e + idx + 1)
                        last = project(k, [w[:, j * 512:(j + 1) * 512] for w in stream.parts[slot]], 4, inner[b],
                                       lambda s: k.bank(4 + j), ((0, LAT),))
                        last.then_inc(down[j], 1)

            walk(pe, step)

        @block.scalar
        def _(act):
            for s in range(2):
                stream.high(act, s, 1)
            total = 3 * N_EXPERTS

            def step(kind, e, idx, b, slot, loads):
                if kind == UP:
                    q = idx % 2
                    act.wait_ge(up[q], 2 * e + idx // 2 + 1)
                else:
                    act.wait_ge(down[3], 2 * e + idx + 1)
                if not isinstance(loads, int) or loads < total:
                    stream.high(act, slot, loads + 1)
                if kind == UP:
                    nc.scalar.activation(inner[b].whole[:, idx, :], k.bank(2 * q), ACT.Silu).then_inc(silu[q], 1)
                    act.wait_ge(weighted, 4 * e + idx + 1)
                    nc.scalar.copy(inner[b].high[:, idx, :], inner[b].whole[:, idx, :]).then_inc(rounded[q], 1)

            walk(act, step)

        @block.vector
        def _(dve):
            chain = Chain(dve, k.sem("chain"))
            free_all(dve, gated + added)
            for s in range(2):
                stream.low(dve, s, 1)
            total = 3 * N_EXPERTS

            def step(kind, e, idx, b, slot, loads):
                if not isinstance(loads, int) or loads < total:
                    stream.low(dve, slot, loads + 1)
                if kind == UP:
                    q = idx % 2
                    part = inner[b].whole[:, idx, :]
                    dve.wait_ge(silu[q], 2 * e + idx // 2 + 1)
                    chain.n, chain.base = 0, 4 * e + idx
                    chain.link(nc.vector.tensor_tensor(part, part, k.bank(2 * q + 1), ALU.mult))
                    nc.vector.tensor_tensor(part, part, share[:, e, :], ALU.mult).then_inc(weighted, 1)
                    dve.wait_ge(rounded[q], 2 * e + idx // 2 + 1)
                    nc.vector.tensor_tensor(inner[b].low[:, idx, :], part, inner[b].high_plain[:, idx, :],
                                            ALU.subtract).then_inc(gated[q], 1)
                else:
                    for j in range(4):
                        dve.wait_ge(down[j], 2 * e + idx + 1)
                        x = k.x[:, 4 * idx + j, CTX:T]
                        nc.vector.tensor_tensor(x, x, k.bank(4 + j), ALU.add).then_inc(added[j], 1)

            walk(dve, step)


def finish(k, out):
    nc = k.nc
    k.stage()
    tok = k.area(0, 4, D)
    turned, kept, stored = k.sem("turned"), [k.sem("kept0"), k.sem("kept1")], k.sem("stored")
    with k.block() as block:
        @block.tensor
        def _(pe):
            for a in range(4):
                for half in range(2):
                    for d in range(4):
                        last = nc.tensor.transpose(k.bank(2 * a + half, P, d * P),
                                                   k.x[:, 4 * half + d, CTX + a * P:CTX + (a + 1) * P], k.const("ident"))
                    last.then_inc(turned, 1)

        @block.vector
        def _(dve):
            for a in range(4):
                dve.wait_ge(turned, 2 * a + 1)
                nc.vector.tensor_copy(tok[:, a, 0:512], k.bank(2 * a)).then_inc(kept[0], 1)

        @block.scalar
        def _(act):
            for a in range(4):
                act.wait_ge(turned, 2 * a + 2)
                nc.scalar.copy(tok[:, a, 512:1024], k.bank(2 * a + 1)).then_inc(kept[1], 1)

        @block.sync
        def _(sp):
            for a in range(4):
                sp.wait_ge(kept[0], a + 1)
                sp.wait_ge(kept[1], a + 1)
                sp.dma_start(out[a * P:(a + 1) * P, :], tok[:, a, :]).then_inc(stored, 16)
            sp.wait_ge(stored, 64)


def build(nc, dram, out, upto=None):
    with ExitStack() as ctx:
        k = Kernel(nc, ctx, dram)

        def gain(a):
            return lambda kk, c: k.gain[:, a, kk, c:c + 1]

        def shift(a, layer=0):
            mod = k.mod_next if layer else k.mod
            return lambda kk, c: mod[:, 3 * a * DT + kk, c:c + 1]

        hidden, scratch = k.area(0, FFT, T), k.area(FFT * T, 2, T)
        pair = k.h_pair
        steps = [
            ("load", lambda: load_inputs(k)),
            ("mod0", lambda: modulations(k, 0, k.mod)),
            ("norm0", lambda: normalise(k, gain(0), shift(0), SEGS, pair=pair)),
            ("hyproj", lambda: project_conv(k, "w_in_hy", k.area(0, 12, T), "hy_conv_w", "hy_conv_b", False)),
            ("hyena", lambda: hyena(k, k.area(0, 12, T))),
            ("mlstm", lambda: mlstm(k)),
            ("splitmix", lambda: split(k, whole_tiles(pair, [k.area(0, 8, T)[:, n, :] for n in range(DT)]))),
            ("out0", lambda: project_residual(k, "w_out_0", pair, 2, SEGS)),
            ("norm0f", lambda: normalise(k, gain(1), shift(1), SEGS, pair=pair)),
            ("up0", lambda: ffn_up(k, 0, hidden, scratch, SEGS)),
            ("down0", lambda: [ffn_down(k, "ffn_down_0", hidden, k.mod, seg) for seg in SEGS]),
            ("mod1", lambda: modulations(k, 1, k.mod_next)),
            ("norm1", lambda: normalise(k, gain(0), shift(0, 1), SEGS, pair=pair)),
            ("mla", lambda: mla(k)),
            ("norm1f", lambda: normalise(k, gain(1), shift(1, 1), SEG_LAT, pair=pair)),
            ("up1", lambda: ffn_up(k, 1, hidden, scratch, SEG_LAT)),
            ("down1", lambda: ffn_down(k, "ffn_down_1", hidden, k.mod_next, SEG_LAT[0])),
            ("final", lambda: normalise(k, lambda kk, c: k.col("final_norm", kk), None, SEG_LAT, k.x)),
            ("norm2", lambda: normalise(k, lambda kk, c: k.col("norm_mix_w_2", kk), None, SEG_LAT, pair=pair)),
            ("block2", lambda: second_mixer(k)),
            ("norm2f", lambda: normalise(k, lambda kk, c: k.col("norm_ffn_w_2", kk), None, SEG_LAT, pair=pair)),
            ("moe", lambda: experts(k)),
            ("finish", lambda: finish(k, out)),
        ]
        for name, step in steps:
            step()
            if name == upto:
                break


def tiles(w, width=P):
    kt, n = w.shape[0] // P, w.shape[1] // width
    return np.ascontiguousarray(w.reshape(kt, P, n, width).transpose(2, 1, 0, 3).reshape(n, P, kt * width))


def columns(v):
    return np.asarray(v).reshape(-1, P).T


def padded(v):
    out = np.zeros((P, 1), np.float32)
    out[:v.shape[0], 0] = v
    return out


def rope_tables():
    t = np.arange(LAT)
    axis = np.stack([t // GRID_W, t % GRID_W]).astype(np.float64)
    inv = 10000.0 ** (-np.arange(0, 32, 2) / 32.0)
    ang = axis[:, None, :] * inv[None, :, None]
    ang = np.concatenate([ang, ang], axis=1).reshape(64, LAT)
    sign = np.where((np.arange(64) % 32) < 16, -1.0, 1.0)[:, None]
    return np.cos(ang).astype(np.float32), (sign * np.sin(ang)).astype(np.float32)


def rotation(n):
    r = np.zeros((n, n), np.float32)
    for i in range(n):
        r[i + 16 if i % 32 < 16 else i - 16, i] = 1.0
    return r


def constants():
    out = np.zeros((P, N_CONST), np.float32)
    i = np.arange(P)
    parts = {
        "ident": np.eye(P), "ones64": np.kron(np.eye(2), np.ones((64, 64))),
        "onecol": np.tile((np.arange(127) == 63) * 1.0, (P, 1)), "s_le_t": i[:, None] <= i[None, :],
        "s_ge_t": i[:, None] >= i[None, :], "rot_gqa": rotation(P), "eps": np.full((P, 1), EPS),
        "first": np.tile(np.arange(4.0, 0.0, -1.0), (P, 1)),
    }
    for name, a in parts.items():
        out[:, CAT[name]:CAT[name] + a.shape[1]] = a
    return out


def hyena_tables(L):
    n = L // P
    ang = np.pi * np.outer(np.arange(L), 2 * np.arange(L) + 1) / (2 * L)
    fwd = [np.cos(ang), -np.sin(ang)]
    inv = [a.T / L for a in fwd]
    dft = np.stack([a.reshape(n, P, L).transpose(1, 0, 2) for a in fwd + inv]).astype(np.float32)
    pos = np.arange(L, dtype=np.float32)
    t = pos / np.float32(L - 1)
    f = np.linspace(1e-4, 15, 16).astype(np.float32)
    ang = (np.float32(2 * math.pi / L) * pos[:, None] * f[None, :]).astype(np.float32)
    z = np.concatenate([t[:, None], np.cos(ang), -np.sin(ang)], axis=1).T
    deltas = np.abs(np.linspace(math.log(1e-2) / 0.3, math.log(1e-2) / 1.5, HY))
    decay = (np.exp(-t[:, None] * deltas[None, :]) + 0.05).reshape(n, P, HY).transpose(1, 0, 2)
    return dft, np.ascontiguousarray(z.astype(np.float32)), np.ascontiguousarray(decay.astype(np.float32))


def lay_out(inp):
    a = {n: np.asarray(v) for n, v in inp.items()}
    d = {"x": a["x"][0], "ctx": a["ctx"][0], "consts": constants()}
    for layer in range(2):
        d[f"ada_w_{layer}"] = tiles(a[f"ada_w_{layer}"], 512)
        up = a[f"ffn_up_{layer}"].reshape(D, 2, FFT, P).transpose(0, 2, 1, 3).reshape(D, 2 * D_FF)
        d[f"ffn_up_{layer}"] = tiles(up, 2 * P)
        d[f"ffn_down_{layer}"] = a[f"ffn_down_{layer}"].reshape(FFT, P, D)
    d["w_in_hy"] = tiles(a["w_in_0"][:, 0:3 * HY])
    for n in ("hy_fw1", "hy_fw2", "hy_fw3"):
        d[n] = a[n]
    for name, L in (("lat", LAT), ("ctx", CTX)):
        d[f"hy_dft_{name}"], d[f"hy_pos_{name}"], d[f"hy_decay_{name}"] = hyena_tables(L)
    d["w_out_0"] = tiles(a["w_out_0"])
    v = {n: a[n] for n, _ in VECTORS if n in a}
    one = {
        "hy_small": np.concatenate([padded(a["hy_fb1"]), padded(a["hy_fb2"]), padded(a["hy_freq"])], axis=1),
        "ml_gate_b": padded(a["ml_gate_b"]),
        "ssd_rows": np.concatenate([padded(a["dt_bias_2"].reshape(-1)), padded(a["a_log_2"].reshape(-1))], axis=1),
        "qk_norm_2": np.stack([np.tile(a["q_norm_w_2"][0], 2), np.tile(a["k_norm_w_2"][0], 2)], axis=1),
        "d_skip": columns(np.repeat(a["d_skip_2"][0], 64)),
        "b_router": np.tile(np.concatenate([a["b_router_group_2"][0], a["b_router_expert_2"][0]]), (P, 1)),
    }
    vec = np.zeros((P, N_COLS), np.float32)
    for n, width in VECTORS:
        if n in one:
            part = one[n]
        elif n in v:
            part = columns(v[n].reshape(-1))
        else:
            continue
        vec[:, COL[n]:COL[n] + width] = part
    d["vectors"] = vec
    extra_layout(a, d, vec)
    return d


def extra_layout(a, d, vec):
    w = a["w_in_0"]
    d["w_in_qk"] = tiles(w[:, 1536:2560])
    d["w_in_v"] = tiles(w[:, 2560:3072], ML_W)[0]
    d["w_in_og"] = tiles(w[:, 3072:3584])
    cos, sin = rope_tables()
    d["rope_cos"], d["rope_sin"] = np.tile(cos, (2, 1)), np.tile(sin, (2, 1))
    down = a["mla_w_down"]
    kr = down[:, Q_RANK + KV_RANK:]
    d["mla_w_down"] = tiles(np.concatenate([down[:, 0:Q_RANK + KV_RANK], kr, kr], axis=1))
    uq = a["mla_w_uq"].reshape(Q_RANK, MLA_HEADS, 192)
    d["mla_w_qn"], d["mla_w_qr"] = tiles(uq[:, :, 0:128].reshape(Q_RANK, -1)), tiles(uq[:, :, 128:].reshape(Q_RANK, -1))
    ukv = a["mla_w_ukv"].reshape(KV_RANK, MLA_HEADS, 2, P)
    d["mla_w_kn"] = tiles(ukv[:, :, 0].reshape(KV_RANK, -1))
    d["mla_w_v0"], d["mla_w_v1"] = tiles(ukv[:, :, 1].reshape(KV_RANK, -1), 512)
    d["mla_w_o"] = tiles(a["mla_w_o"])
    w2 = a["w_in_2"][0]
    kd = w2[:, 512:640].reshape(D, 2, 1, 64)
    kd = np.concatenate([kd, kd], axis=2).reshape(D, 256)
    d["w_qk_2"] = tiles(np.concatenate([w2[:, 0:512], kd], axis=1))
    d["w_v_2"] = tiles(w2[:, 640:768])[0]
    d["w_z_2"], d["w_xbc_2"] = tiles(w2[:, 768:1280]), tiles(w2[:, 1280:2048])
    d["w_in_dt"] = tiles(w2[:, 2048:2064], 16)[0]
    d["w_gates_2"] = tiles(w2[:, 2064:4112])
    d["w_merge"] = np.concatenate([tiles(a["w_attn_o_2"][0]), tiles(a["w_ssd_o_2"][0])], axis=2)
    d["w_out_2"] = tiles(a["w_out_2"][0])
    d["w_router"] = tiles(np.concatenate([a["w_router_group_2"][0], a["w_router_expert_2"][0]], axis=1), 20)[0]
    up = np.stack([a["w1_2"][0], a["w3_2"][0]], axis=2).reshape(N_EXPERTS, DT, P, 2, 4, P)
    up = up.transpose(0, 4, 2, 1, 3, 5).reshape(N_EXPERTS, 4, P, 2 * D)
    dn = a["w2_2"][0].reshape(N_EXPERTS, 4, P, 2, 4, P).transpose(0, 3, 2, 4, 1, 5).reshape(N_EXPERTS, 2, P, 2 * D)
    chunks = list(up[0])
    for e in range(1, N_EXPERTS):
        chunks += [up[e, 0], dn[e - 1, 0], up[e, 1], dn[e - 1, 1], up[e, 2], up[e, 3]]
    d["moe"] = np.stack(chunks + list(dn[N_EXPERTS - 1]))
    d["w_in_gates"] = tiles(w[:, 3584:3600], 16)[0]


def kernel(**inputs):
    import concourse.bacc as _bacc
    from concourse.bass_utils import run_bass_kernel_spmd as _run

    nc = _bacc.Bacc("TRN2", target_bir_lowering=False, num_devices=1)
    arrays, dram = {}, {}
    for name, a in lay_out(inputs).items():
        arrays[f"in_{name}"] = np.ascontiguousarray(a)
        dram[name] = nc.dram_tensor(f"in_{name}", a.shape, mybir.dt.from_np(a.dtype), kind="ExternalInput").ap()
    out = nc.dram_tensor("out_x", (LAT, D), F32, kind="ExternalOutput").ap()
    build(nc, dram, out)
    r = _run(nc, [arrays], core_ids=[0])
    return np.asarray(r.results[0]["out_x"]).reshape(1, LAT, D)
```
